# Optimizing a Trainium2 kernel written in Bass

```python
import jax, jax.numpy as jnp
from jax import lax
import numpy as np

D_MODEL = 1024
BATCH = 1
SEQ = 512
DEPTH = 2
DEC_BATCH = 8
DEC_SEQ = 8
PAST_LEN = 4096
PAGE_SIZE = 128

N_EVEN = (DEPTH + 1) // 2
N_ODD = DEPTH // 2
CONV_A_DIM = D_MODEL // 2
CONV_A_W = 3
DN_HEADS = 4
DN_HEAD_DIM = (D_MODEL // 2) // DN_HEADS
DN_DIM = DN_HEADS * DN_HEAD_DIM
DN_CONV_W = 4
DN_CHUNK = 64
EVEN_IN = 3 * CONV_A_DIM + 4 * DN_DIM + 2 * DN_HEADS
RET_HEADS = 8
RET_QK_DIM = D_MODEL // RET_HEADS
RET_V_DIM = 2 * D_MODEL // RET_HEADS
RET_CHUNK = 64
ODD_IN = 2 * D_MODEL + 4 * D_MODEL
ROPE_BASE = 10000.0
D_FF = ((-(-8 * D_MODEL // 3) + 255) // 256) * 256
EPS = 1e-6
GN_EPS = 1e-5

kernel_name = "hybrid_conv_deltanet_retention_step"

F32 = jnp.float32

def rmsnorm(x, g):
    xf = x.astype(F32)
    y = xf * lax.rsqrt(jnp.mean(xf * xf, axis=-1, keepdims=True) + EPS)
    return (y * g.astype(F32)).astype(x.dtype)

def l2norm(x):
    return x * lax.rsqrt(jnp.sum(x * x, axis=-1, keepdims=True) + EPS)

def split_heads(t, h):
    return t.reshape(t.shape[:-1] + (h, t.shape[-1] // h))

def chunk_len(length, chunk):
    return chunk if length % chunk == 0 else length

def causal_dwconv(x, prefix, w):
    width = w.shape[0]
    length = x.shape[1]
    xp = jnp.concatenate([prefix.astype(x.dtype), x], axis=1)
    y = xp[:, 0:length] * w[0]
    for i in range(1, width):
        y = y + xp[:, i:i + length] * w[i]
    return y, xp[:, length:]

def to_blocks(t, n, c):
    b = t.shape[0]
    return jnp.moveaxis(t.reshape((b, n, c) + t.shape[2:]), 3, 2)

def from_blocks(o):
    o = jnp.moveaxis(o, 0, 1)
    o = jnp.moveaxis(o, 2, 3)
    b, n, c, h, d = o.shape
    return o.reshape(b, n * c, h, d)

def gated_delta_chunked(q, k, v, g, beta, s0, chunk):
    bsz, length, h, dk = q.shape
    c = chunk_len(length, chunk)
    n = length // c
    qc, kc, vc, gc, bc = [to_blocks(t, n, c) for t in (q, k, v, g, beta)]
    G = jnp.cumsum(gc, axis=-1)
    causal = jnp.tril(jnp.ones((c, c), dtype=bool))
    decay = jnp.exp(jnp.where(causal, G[..., :, None] - G[..., None, :], -jnp.inf))
    strict = jnp.tril(jnp.ones((c, c), F32), -1)
    kb = kc * bc[..., None]
    vb = vc * bc[..., None]
    a_mat = jnp.eye(c, dtype=F32) + jnp.einsum('bnhid,bnhjd->bnhij', kb, kc) * decay * strict
    u_base = lax.linalg.triangular_solve(a_mat, vb, left_side=True, lower=True, unit_diagonal=True)
    w_mat = lax.linalg.triangular_solve(a_mat, kb * jnp.exp(G)[..., None], left_side=True,
                                        lower=True, unit_diagonal=True)
    aqk = jnp.einsum('bnhid,bnhjd->bnhij', qc, kc) * decay
    xs = tuple(jnp.moveaxis(t, 1, 0) for t in (qc, kc, G, u_base, w_mat, aqk))

    def step(s, inp):
        q_, k_, g_, ub, w_, a_ = inp
        u = ub - jnp.einsum('bhck,bhkv->bhcv', w_, s)
        o = (jnp.einsum('bhck,bhkv->bhcv', q_ * jnp.exp(g_)[..., None], s)
             + jnp.einsum('bhij,bhjv->bhiv', a_, u))
        g_last = g_[..., -1:]
        s = s * jnp.exp(g_last)[..., None] + jnp.einsum(
            'bhck,bhcv->bhkv', k_ * jnp.exp(g_last - g_)[..., None], u)
        return s, o

    s, o = lax.scan(step, s0, xs)
    return from_blocks(o), s

def retention_chunked(q, k, v, log_gamma, r0, chunk):
    bsz, length, h, dk = q.shape
    c = chunk_len(length, chunk)
    n = length // c
    qc, kc, vc = [to_blocks(t, n, c) for t in (q, k, v)]
    idx = jnp.arange(c, dtype=F32)
    diff = idx[:, None] - idx[None, :]
    lg = log_gamma[:, None, None]
    decay = jnp.where(diff >= 0, jnp.exp(jnp.maximum(diff, 0.0) * lg), 0.0)
    inner = jnp.exp((idx + 1.0) * log_gamma[:, None])[..., None]
    kdec = jnp.exp((c - 1.0 - idx) * log_gamma[:, None])[..., None]
    cdec = jnp.exp(c * log_gamma)[:, None, None]
    xs = tuple(jnp.moveaxis(t, 1, 0) for t in (qc, kc, vc))

    def step(r, inp):
        q_, k_, v_ = inp
        att = jnp.einsum('bhid,bhjd->bhij', q_, k_) * decay
        o = jnp.einsum('bhij,bhjv->bhiv', att, v_) + jnp.einsum('bhck,bhkv->bhcv', q_, r) * inner
        r = r * cdec + jnp.einsum('bhck,bhcv->bhkv', k_ * kdec, v_)
        return r, o

    r, o = lax.scan(step, r0, xs)
    return from_blocks(o), r

def rotary(x, pos):
    half = x.shape[-1] // 2
    inv = ROPE_BASE ** (-jnp.arange(half, dtype=F32) / half)
    ang = pos.astype(F32)[:, None] * inv[None, :]
    cos = jnp.cos(ang)[:, None, :]
    sin = jnp.sin(ang)[:, None, :]
    x1, x2 = x[..., :half], x[..., half:]
    return jnp.concatenate([x1 * cos - x2 * sin, x1 * sin + x2 * cos], axis=-1)

def even_mixer(h, w_in, conv_a_w, conv_qkv_w, a_log, dt_bias, dn_norm_g, w_out,
               conv_a_prev, conv_qkv_prev, delta_prev):
    bsz, length, _ = h.shape
    p = h @ w_in
    cuts = [int(c) for c in np.cumsum([CONV_A_DIM] * 3 + [DN_DIM] * 4 + [DN_HEADS])]
    gate_b, gate_c, h_a, q, k, v, z, a, b = jnp.split(p, cuts, axis=-1)
    conv_out, conv_a_new = causal_dwconv(gate_c * h_a, conv_a_prev, conv_a_w)
    y_a = gate_b * conv_out
    qkv, conv_qkv_new = causal_dwconv(jnp.concatenate([q, k, v], axis=-1), conv_qkv_prev, conv_qkv_w)
    qkv = jax.nn.silu(qkv.astype(F32))
    q, k, v = jnp.split(qkv, 3, axis=-1)
    q = l2norm(split_heads(q, DN_HEADS)) * (DN_HEAD_DIM ** -0.5)
    k = l2norm(split_heads(k, DN_HEADS))
    v = split_heads(v, DN_HEADS)
    beta = jax.nn.sigmoid(b.astype(F32))
    g = -jnp.exp(a_log.astype(F32)) * jax.nn.softplus(a.astype(F32) + dt_bias.astype(F32))
    o, s_new = gated_delta_chunked(q, k, v, g, beta, delta_prev.astype(F32), DN_CHUNK)
    o = (o * lax.rsqrt(jnp.mean(o * o, axis=-1, keepdims=True) + EPS) * dn_norm_g.astype(F32)
         * jax.nn.silu(split_heads(z, DN_HEADS).astype(F32)))
    y_b = o.reshape(bsz, length, DN_DIM)
    y = jnp.concatenate([y_a.astype(h.dtype), y_b.astype(h.dtype)], axis=-1) @ w_out
    return y, conv_a_new, conv_qkv_new, s_new

def odd_mixer(h, w_in, gn_g, gn_b, w_out, ret_prev, pos):
    bsz, length, _ = h.shape
    p = h @ w_in
    q, k, v, gate = jnp.split(p, [D_MODEL, 2 * D_MODEL, 4 * D_MODEL], axis=-1)
    q = rotary(split_heads(q, RET_HEADS).astype(F32), pos)
    k = rotary(split_heads(k, RET_HEADS).astype(F32), pos) * (RET_QK_DIM ** -0.5)
    v = split_heads(v, RET_HEADS).astype(F32)
    log_gamma = jnp.log(1.0 - 2.0 ** (-5.0 - jnp.arange(RET_HEADS, dtype=F32)))
    o, r_new = retention_chunked(q, k, v, log_gamma, ret_prev.astype(F32), RET_CHUNK)
    mu = jnp.mean(o, axis=-1, keepdims=True)
    var = jnp.mean(jnp.square(o - mu), axis=-1, keepdims=True)
    o = ((o - mu) * lax.rsqrt(var + GN_EPS)).reshape(bsz, length, 2 * D_MODEL)
    o = o * gn_g.astype(F32) + gn_b.astype(F32)
    y = (jax.nn.silu(gate.astype(F32)) * o).astype(h.dtype) @ w_out
    return y, r_new

def run_trunk(x, conv_a_prev, conv_qkv_prev, delta_prev, ret_prev, pos, w):
    conv_a_out, conv_qkv_out, delta_out, ret_out = [], [], [], []
    for i in range(DEPTH):
        h = rmsnorm(x, w['norm_mix'][i])
        if i % 2 == 0:
            e = i // 2
            y, ca, cq, s = even_mixer(h, w['even_w_in'][e], w['even_conv_a'][e], w['even_conv_qkv'][e],
                                      w['even_a_log'][e], w['even_dt_bias'][e], w['even_dn_norm'][e],
                                      w['even_w_out'][e], conv_a_prev[e], conv_qkv_prev[e], delta_prev[e])
            conv_a_out.append(ca)
            conv_qkv_out.append(cq)
            delta_out.append(s)
        else:
            o = i // 2
            y, r = odd_mixer(h, w['odd_w_in'][o], w['odd_gn_g'][o], w['odd_gn_b'][o], w['odd_w_out'][o],
                             ret_prev[o], pos)
            ret_out.append(r)
        x = x + y.astype(x.dtype)
        h = rmsnorm(x, w['norm_ffn'][i])
        f = (jax.nn.silu(h @ w['ffn_w_gate'][i]) * (h @ w['ffn_w_up'][i])) @ w['ffn_w_down'][i]
        x = x + f.astype(x.dtype)
    y = rmsnorm(x, w['final_norm'])
    return y, jnp.stack(conv_a_out), jnp.stack(conv_qkv_out), jnp.stack(delta_out), jnp.stack(ret_out)

def setup_inputs(seed: int = 0) -> dict:
    key = jax.random.key(seed)
    ks = jax.random.split(key, 32)
    nrm = lambda k, shape, s: jax.random.normal(k, shape, F32) * s
    dt = jnp.exp(jax.random.uniform(ks[10], (N_EVEN, DN_HEADS), F32, np.log(1e-3), np.log(1e-1)))
    return {
        "x_prompt": nrm(ks[0], (BATCH, SEQ, D_MODEL), 1.0),
        "x_sample": nrm(ks[1], (DEC_BATCH, DEC_SEQ, D_MODEL), 1.0),
        "state_conv_a": nrm(ks[2], (N_EVEN, DEC_BATCH, CONV_A_W - 1, CONV_A_DIM), 1.0),
        "state_conv_qkv": nrm(ks[3], (N_EVEN, DEC_BATCH, DN_CONV_W - 1, 3 * DN_DIM), 1.0),
        "state_delta": nrm(ks[4], (N_EVEN, DEC_BATCH, DN_HEADS, DN_HEAD_DIM, DN_HEAD_DIM), 0.1),
        "state_ret": nrm(ks[5], (N_ODD, DEC_BATCH, RET_HEADS, RET_QK_DIM, RET_V_DIM), 1.0),
        "norm_mix": 1.0 + nrm(ks[6], (DEPTH, D_MODEL), 0.02),
        "norm_ffn": 1.0 + nrm(ks[7], (DEPTH, D_MODEL), 0.02),
        "final_norm": 1.0 + nrm(ks[8], (D_MODEL,), 0.02),
        "even_w_in": nrm(ks[9], (N_EVEN, D_MODEL, EVEN_IN), D_MODEL ** -0.5),
        "even_conv_a": nrm(ks[11], (N_EVEN, CONV_A_W, CONV_A_DIM), CONV_A_W ** -0.5),
        "even_conv_qkv": nrm(ks[12], (N_EVEN, DN_CONV_W, 3 * DN_DIM), DN_CONV_W ** -0.5),
        "even_a_log": jnp.log(jax.random.uniform(ks[13], (N_EVEN, DN_HEADS), F32, 1.0, 16.0)),
        "even_dt_bias": dt + jnp.log(-jnp.expm1(-dt)),
        "even_dn_norm": 1.0 + nrm(ks[14], (N_EVEN, DN_HEAD_DIM), 0.02),
        "even_w_out": nrm(ks[15], (N_EVEN, D_MODEL, D_MODEL), D_MODEL ** -0.5),
        "odd_w_in": nrm(ks[16], (N_ODD, D_MODEL, ODD_IN), D_MODEL ** -0.5),
        "odd_gn_g": 1.0 + nrm(ks[17], (N_ODD, 2 * D_MODEL), 0.02),
        "odd_gn_b": nrm(ks[18], (N_ODD, 2 * D_MODEL), 0.02),
        "odd_w_out": nrm(ks[19], (N_ODD, 2 * D_MODEL, D_MODEL), (2 * D_MODEL) ** -0.5),
        "ffn_w_gate": nrm(ks[20], (DEPTH, D_MODEL, D_FF), D_MODEL ** -0.5),
        "ffn_w_up": nrm(ks[21], (DEPTH, D_MODEL, D_FF), D_MODEL ** -0.5),
        "ffn_w_down": nrm(ks[22], (DEPTH, D_FF, D_MODEL), D_FF ** -0.5),
    }

def reference(x_prompt, x_sample, state_conv_a, state_conv_qkv, state_delta, state_ret,
              norm_mix, norm_ffn, final_norm, even_w_in, even_conv_a, even_conv_qkv, even_a_log,
              even_dt_bias, even_dn_norm, even_w_out, odd_w_in, odd_gn_g, odd_gn_b, odd_w_out,
              ffn_w_gate, ffn_w_up, ffn_w_down):
    w = dict(norm_mix=norm_mix, norm_ffn=norm_ffn, final_norm=final_norm, even_w_in=even_w_in,
             even_conv_a=even_conv_a, even_conv_qkv=even_conv_qkv, even_a_log=even_a_log,
             even_dt_bias=even_dt_bias, even_dn_norm=even_dn_norm, even_w_out=even_w_out,
             odd_w_in=odd_w_in, odd_gn_g=odd_gn_g, odd_gn_b=odd_gn_b, odd_w_out=odd_w_out,
             ffn_w_gate=ffn_w_gate, ffn_w_up=ffn_w_up, ffn_w_down=ffn_w_down)
    bp, lp, _ = x_prompt.shape
    ls = x_sample.shape[1]
    zc_a = jnp.zeros((N_EVEN, bp, CONV_A_W - 1, CONV_A_DIM), x_prompt.dtype)
    zc_qkv = jnp.zeros((N_EVEN, bp, DN_CONV_W - 1, 3 * DN_DIM), x_prompt.dtype)
    z_delta = jnp.zeros((N_EVEN, bp, DN_HEADS, DN_HEAD_DIM, DN_HEAD_DIM), F32)
    z_ret = jnp.zeros((N_ODD, bp, RET_HEADS, RET_QK_DIM, RET_V_DIM), F32)
    pos_p = jnp.arange(lp, dtype=jnp.int32)
    y_prompt, ca_p, cq_p, d_p, r_p = run_trunk(x_prompt, zc_a, zc_qkv, z_delta, z_ret, pos_p, w)
    pos_s = PAST_LEN + jnp.arange(ls, dtype=jnp.int32)
    y_sample, ca_s, cq_s, d_s, r_s = run_trunk(x_sample, state_conv_a, state_conv_qkv, state_delta,
                                               state_ret, pos_s, w)
    return (y_prompt, y_sample, ca_p, cq_p, d_p, r_p, ca_s, cq_s, d_s, r_s)


_drawn_inputs = setup_inputs


def setup_inputs(seed=0):
    import zlib

    import numpy as np

    out = dict(_drawn_inputs(seed))
    spreads = {}
    factors = {'norm_ffn': 3.006,
     'final_norm': 2.991,
     'even_dn_norm': 6.645,
     'odd_gn_g': 6.752,
     'odd_gn_b': 6.799}
    for name, (base, spread) in spreads.items():
        noise = np.random.default_rng([zlib.crc32(name.encode()), seed]).standard_normal(out[name].shape)
        drawn = base * np.exp(spread * noise) if base else spread * noise
        out[name] = __import__('jax').numpy.asarray(drawn.astype(out[name].dtype))
    for name, factor in factors.items():
        out[name] = (out[name] * factor).astype(out[name].dtype)
    return out
```

```python
import math
from contextlib import ExitStack

import numpy as np

import concourse.bass as bass
from concourse import mybir

F32 = mybir.dt.float32
F32R = mybir.dt.float32r
ALU = mybir.AluOpType
ACT = mybir.ActivationFunctionType
ds = bass.ds

P = 128
D = 1024
KT = D // P
TP = 512
NB, LS = 8, 8
TS = NB * LS
T = TP + TS
HALF = T // 2
NC = TP // P
CA = D // 2
DN_H, DN_D = 4, 128
RET_H, RET_V = 8, 256
EVEN_IN = 3 * CA + 4 * DN_H * DN_D + 2 * DN_H
ODD_IN = 6 * D
FF = 2816
FT = FF // P
PAST = 4096
WA, WQ = 3, 4
EPS, GN_EPS = 1e-6, 1e-5
ROPE_BASE = 10000.0
PADA = WA - 1 + TP + NB * (LS + WA - 1)
PADQ = WQ - 1 + TP + NB * (LS + WQ - 1)
NA, NQ = PADA - (WA - 1), PADQ - (WQ - 1)
SA, SQ = WA - 1 + TP, WQ - 1 + TP

PHASES = {
    "x": (1, (), (), (0, 1) * 4),
    "ab": (1, (3,), (2,), (1,)),
    "even": (DN_H, (0, 1, 2) * 3, (0, 1, 2) * 3, tuple(n % 2 for n in range(15))),
    "up0": (FT // 2, (0, 1, 2, 3), (0, 1, 0, 1), (0, 1, 0, 1)),
    "down0": (KT // 2, (0, 1, 2) * 2, (0, 1, 2) * 2, (0, 1)),
    "odd": (RET_H, (0, 1, 2, 3) * 2, (0, 1, 2, 0, 1, 2, 0, 1), (0, 1) * 7),
    "up1": (FT // 2, (0, 1, 2, 3), (0, 1, 0, 1), (0, 1, 0, 1)),
    "down1": (KT // 2, (0, 1, 2) * 2, (0, 1, 2) * 2, (0, 1)),
    "y": (1, (), (), (0, 1, 0, 1, 0)),
}
DOWN = (8, 8, FT - 16)
RAW_LAG, SPLIT_LAG = 3, 2


class Plan:

    def __init__(self):
        self.unit0, self.mark0, self.raw0, self.pair0 = {}, {}, {}, {}
        units, marks, raws, pairs = 0, 0, [0] * 4, [0] * 2
        seen_raw, seen_split, self.ends = [], [], []
        for name, (count, raw, split, pair) in PHASES.items():
            self.unit0[name], self.mark0[name] = units, marks
            self.raw0[name], self.pair0[name] = list(raws), list(pairs)
            for i in range(count):
                self.ends += [marks + i * self.marks(name) + self.unit_mark(name, j) + 1 for j in range(len(raw))]
            units += count * len(raw)
            marks += count * self.marks(name)
            raws = [n + count * raw.count(s) for s, n in enumerate(raws)]
            pairs = [n + count * pair.count(s) for s, n in enumerate(pairs)]
            seen_raw += list(raw) * count
            seen_split += list(split) * count
        for seen, lag in ((seen_raw, RAW_LAG), (seen_split, SPLIT_LAG)):
            assert all(len(set(seen[n:n + lag])) == len(seen[n:n + lag]) for n in range(len(seen)))

    def marks(self, phase):
        _, raw, _, pair = PHASES[phase]
        return len(raw) if phase[:4] == "down" else len(pair)

    def unit_mark(self, phase, j):
        plain = {"even": 7, "odd": 6}.get(phase, 99)
        return j if j < plain else plain + 4 * (j - plain) + 3

    def sum_mark(self, phase, n):
        return 3 * n + 2 if phase[:4] == "down" else n

    def split_free(self, phase, i, j, again=False):
        k = j - SPLIT_LAG
        if k >= 0:
            return self.mark0[phase] + i * self.marks(phase) + self.unit_mark(phase, k) + 1
        if self.unit0[phase] + k < 0:
            return 1
        back = self.mark0[phase] - self.ends[self.unit0[phase] + k]
        if PHASES[phase][0] > 1:
            inside = self.marks(phase) - 1 - self.unit_mark(phase, k + len(PHASES[phase][1]))
            back = inside if again else min(back, inside)
        return self.mark0[phase] + i * self.marks(phase) - back

    def unit(self, phase, i, j):
        return self.unit0[phase] + i * len(PHASES[phase][1]) + j

    def landed(self, phase, i, j):
        raw = PHASES[phase][1]
        s = raw[j]
        return s, (i * raw.count(s) + self.raw0[phase][s] + raw[:j + 1].count(s)) * 16

    def split_slot(self, phase, j):
        return PHASES[phase][2][j]

    def summed(self, phase, i, n):
        return self.mark0[phase] + i * self.marks(phase) + self.sum_mark(phase, n) + 1

    def pair(self, phase, n):
        return PHASES[phase][3][n]

    def drained(self, phase, i, n):
        pair = PHASES[phase][3]
        return i * pair.count(pair[n]) + self.pair0[phase][pair[n]] + pair[:n].count(pair[n])


class Steps:

    def __init__(self, sem, names):
        self.sem, self.names, self.at = sem, names, 0

    def done(self, ins, name):
        assert self.names[self.at % len(self.names)] == name, (name, self.names[self.at % len(self.names)])
        self.at += 1
        ins.then_inc(self.sem, 1)

    def wait(self, eng, i, name):
        eng.wait_ge(self.sem, i * len(self.names) + self.names.index(name) + 1)


MASKS = (1, 2, 4, 8, 16, 32, 64)


def constants():
    j, i = np.arange(P)[:, None], np.arange(P)[None, :]
    same = (j // LS == i // LS)[:TS, :TS]

    def padded(a):
        return np.pad(a, ((0, P - a.shape[0]), (0, 0)))

    ident, ones = (i == j), np.ones((P, P))
    block = padded(np.arange(TS)[:, None] // LS == np.arange(NB)[None, :])
    every = np.concatenate([ident, ones, block], axis=1)
    tri, low = j <= i, j > i
    levels = [(j // (2 * s) == i // (2 * s)) & (j // s % 2 == 1) & (i // s % 2 == 0) for s in MASKS]
    even = np.concatenate([tri, low, padded(tri[:TS, :TS] & same), padded(low[:TS, :TS] & same), *levels], axis=1)
    pos = np.concatenate([np.arange(TP), np.tile(PAST + np.arange(LS), NB)]).astype(np.float32)
    inv = (ROPE_BASE ** (-np.arange(P // 2) / (P // 2))).astype(np.float32)
    ang = (inv[:, None] * pos[None, :]).astype(np.float32).astype(np.float64)
    odd = np.concatenate([np.tile(np.cos(ang), (2, 1)), np.concatenate([-np.sin(ang), np.sin(ang)])], axis=1)
    heads = []
    for h in range(RET_H):
        gamma = 1.0 - 2.0 ** (-5.0 - h)
        att = np.where(j <= i, gamma ** np.maximum(i - j, 0), 0.0)
        att_s = padded(att[:TS, :TS] * same)
        inner = np.tile(gamma ** (np.arange(P) + 1.0), (P, 1))
        inner_s = np.tile(gamma ** (np.arange(TS) % LS + 1.0), (P, 1))
        kdec = gamma ** (P - 1.0 - np.arange(P))[:, None]
        kdec_s = gamma ** (LS - 1.0 - np.arange(P) % LS)[:, None]
        cdec = np.tile([[gamma ** float(P), gamma ** float(LS)]], (P, 1))
        heads.append(np.concatenate([att, att_s, inner, inner_s, kdec, kdec_s, cdec], axis=1))
    return {"every": every.astype(np.float32), "even": even.astype(np.float32), "odd": odd.astype(np.float32),
            "heads": np.stack(heads).astype(np.float32)}


COL_NORM = (0, 16, 8, 24, 32)
COL_GN_G, COL_GN_B = 40, 56
ROWS_1 = 72
COL_CONV_A, COL_CONV_Q, COL_DN = ROWS_1, ROWS_1 + WA * 4, ROWS_1 + WA * 4 + WQ * 12
ROWS_2 = WA * 4 + WQ * 12 + 1

_LATER = tuple(s for s in MASKS if s > 1)
A_PE = ("ab_t", "gcum")
A_ACT = ("abs", "exp", "nega", "ln", "beta", "kdec")
A_DVE = ("zero", "gate", "sum", "ad", "relu", "softplus", "neg", "g", "gc0", "gc")
E_PE = ("rows", "l2k", "l2q", "kk", "kq", "tk", "tv", "P1", *(f"{a}{s}" for s in _LATER for a in "PQ"),
        "u0", "Rs", "S0", "o0", "R1", "u1", "S1", "o1", "R2", "u2", "us", "S2", "o2", "R3", "u3", "S3", "o3",
        "os", "onorm", "Ss")
E_ACT = ("gr", "eg", "ks", "k_sq", "dm", "dt", "k_ln", "k_inv", "qs", "q_sq", "q_ln", "q_inv", "vs", *(f"p{s}" for s in _LATER),
         "yah", "uu0", "uu1", "uu2", "us_", "uu3", "o_sq", "o_ln", "o_inv", "ybh")
E_DVE = ("pw", "gbc", "pre_k", "ck0", "ck1", "ck2", "ck", "bg", "df", "dt_lo", "dt_in", "pre_q",
         "cq0", "cq1", "cq2", "cq", "kT", "kbg", "km", "dmb", "qT", "qg", "A", "pre_v",
         "cv0", "cv1", "cv2", "cv", "aqk", "kd", "vb", *(f"{a}{s}" for s in (1, 2, 4, 8, 16) for a in "zx"),
         "ca0", "ca1", "ca2", "z32", "x32", "z64", "s0", "rr1", "rs", "s1", "rr2", "s2", "rr3", "s3", "yal",
         "oT_s", "oT_p", "s_dec", "s_new", "on", "yb", "ybl")
E_POOL = ("dtm", *(f"b{s}" for s in MASKS), "um")
O_PE = ("att", "tk", "tv0", "tv1", "kv", "op", "os", "mean", "var", "kvs")
O_ACT = ("kdt", "v0", "v1", "osq", "oln", "oinv", "yh0", "yh1")
O_DVE = ("tk", "rk", "tq", "rq", "qg", "att", "r0", "r1", "r2", "r3", "of_p", "of_s", "cen",
         "on0", "y0", "on1", "y1", "yl0", "yl1", "rs")
O_POOL = ("kdm",)


def build(nc, x_prompt, x_sample, state_conv_a, state_conv_qkv, state_delta, state_ret, norm_mix, norm_ffn,
          final_norm, even_w_in, even_conv_a, even_conv_qkv, even_a_log, even_dt_bias, even_dn_norm, even_w_out,
          odd_w_in, odd_gn_g, odd_gn_b, odd_w_out, ffn_w_gate, ffn_w_up, ffn_w_down,
          c_every, c_even, c_odd, c_heads,
          y_prompt, y_sample, conv_a_p, conv_qkv_p, delta_p, ret_p, conv_a_s, conv_qkv_s, delta_s, ret_s):
    plan = Plan()
    ctx = ExitStack()
    with ctx:
        def sb(stack, name, shape, dt=F32):
            return stack.enter_context(nc.sbuf_tensor(name, [P] + shape, dt))

        def sem(name):
            return ctx.enter_context(nc.semaphore(name))

        x = sb(ctx, "x", [KT, T])
        xn_hi = sb(ctx, "xn_hi", [KT, T], F32R)
        with ExitStack() as m:
            n_sq = sb(m, "n_sq", [2, T])
            n_ss = sb(m, "n_ss", [T])
        xn_lo = sb(ctx, "xn_lo", [KT, T], F32R)
        raw = sb(ctx, "raw", [4, KT * P])
        w_hi = sb(ctx, "w_hi", [3, KT * P], F32R)
        w_lo = sb(ctx, "w_lo", [3, KT * P], F32R)
        every = sb(ctx, "every", [2 * P + NB])
        cols = sb(ctx, "cols", [ROWS_1 + ROWS_2])
        eps = sb(ctx, "eps", [2])
        dtb, nega = sb(ctx, "dtb", [DN_H]), sb(ctx, "nega", [DN_H])
        spare = sb(ctx, "spare", [RAW_LAG + 2])
        ident, ones, block = every[:, 0:P], every[:, P:2 * P], every[:, 2 * P:2 * P + NB]
        acc = ctx.enter_context(nc.psum_tensor("acc", [P, 2, 2, 512], F32))
        mx = ctx.enter_context(nc.psum_tensor("mx", [P, 4, 512], F32))

        with ExitStack() as m:
            n_rs = sb(m, "n_rs", [T])
            n_xf = sb(m, "n_xf", [4, T])
            x_in = sb(m, "x_in", [NC + 1, D])
            rows_1 = sb(m, "rows_1", [P])
            rows_2 = sb(m, "rows_2", [P])
            rows_a = sb(m, "rows_a", [CA])
            rows_q = sb(m, "rows_q", [3 * CA])
        with ExitStack() as m:
            gate = sb(m, "gate", [NC + 1, 8])

            g_ab, g_sp, g_rl, g_g, g_beta = (sb(m, n, [NC + 1, DN_H]) for n in
                                             ("g_ab", "g_sp", "g_rl", "g_g", "g_beta"))
            gcum, kdec = sb(m, "gcum", [NC + 1, DN_H]), sb(m, "kdec", [NC + 1, DN_H])
            yf = sb(m, "yf", [T])
            gbc, bbc = sb(m, "gbc", [NC + 1, P]), sb(m, "bbc", [NC + 1, P])
            cbuf, ca1, ca2, cs = sb(m, "cbuf", [PADQ]), sb(m, "ca1", [PADQ]), sb(m, "ca2", [PADQ]), sb(m, "cs", [T])
            ks, qs, vs = sb(m, "ks", [T]), sb(m, "qs", [T]), sb(m, "vs", [T])
            sq, std = sb(m, "sq", [T]), sb(m, "std", [T])
            kT, qT, kbg, qg = sb(m, "kT", [T]), sb(m, "qT", [T]), sb(m, "kbg", [T]), sb(m, "qg", [T])
            gr, eg, bg = sb(m, "gr", [T]), sb(m, "eg", [T]), sb(m, "bg", [T])
            dm, dt_ = sb(m, "dm", [T]), sb(m, "dt", [T])
            zi, xi, pp = sb(m, "zi", [T]), sb(m, "xi", [T]), sb(m, "pp", [T])
            bm = sb(m, "bm", [2, T])
            kd, vb = sb(m, "kd", [NC + 1, P]), sb(m, "vb", [NC + 1, P])
            rr, uu, rs_, us_, s_p = (sb(m, n, [P]) for n in ("rr", "uu", "rs_", "us_", "s_p"))
            oT = sb(m, "oT", [T])
            km = sb(m, "km", [NB * (TS + LS)])
            um = sb(m, "um", [NB, P])
            s_s = sb(m, "s_s", [NB, P])
            zs, gcs, bufa = sb(m, "zs", [T]), sb(m, "gcs", [T]), sb(m, "bufa", [PADA])
            yh = sb(m, "yh", [2, T], F32R)
            yl = sb(m, "yl", [2, T], F32R)
            pw = sb(m, "pw", [16])
            pre_a, pre_q = sb(m, "pre_a", [4, 2 * NB]), sb(m, "pre_q", [3, 4, 3 * NB])
            out_a, out_q = sb(m, "out_a", [4, 2 + 2 * NB]), sb(m, "out_q", [3, 4, 3 + 3 * NB])
            out_rows = sb(m, "out_rows", [4, CA])
            ce = sb(m, "ce", [2 * P + 2 * TS + len(MASKS) * P])
        tri, low = ce[:, 0:P], ce[:, P:2 * P]
        tri_s, low_s = ce[0:TS, 2 * P:2 * P + TS], ce[0:TS, 2 * P + TS:2 * P + 2 * TS]
        level = [ce[:, 2 * P + 2 * TS + n * P:2 * P + 2 * TS + (n + 1) * P] for n in range(len(MASKS))]
        with ExitStack() as m:
            h_hi = sb(m, "h_hi", [FT, T], F32R)
            h_lo = sb(m, "h_lo", [FT, T], F32R)
            f_g = sb(m, "f_g", [T])
            f_h = sb(m, "f_h", [T])
        with ExitStack() as m:
            o_pad = sb(m, "o_pad", [5 * T])
            co = sb(m, "co", [2, T])
            ch = sb(m, "ch", [3 * P + 4])
            qa, qb, ka, kb = (sb(m, n, [T]) for n in ("qa", "qb", "ka", "kb"))
            t1, t2, rq, rk, rqg = (sb(m, n, [T]) for n in ("t1", "t2", "rq", "rk", "rqg"))
            va = sb(m, "va", [2, T])
            gs = sb(m, "gs", [2, T])
            vtok = sb(m, "vtok", [NC + 1, RET_V])
            kdt = sb(m, "kdt", [NC + 1, P])
            kdm = sb(m, "kdm", [NB, P])
            att = sb(m, "att", [T])
            gnw = sb(m, "gnw", [2, 2])
            rst = sb(m, "rst", [NC, RET_V])
            r_s = sb(m, "r_s", [NB, RET_V])
            of = sb(m, "of", [2, T])
            osq = sb(m, "osq", [2, T])
            orv = sb(m, "orv", [T])
            oyh = sb(m, "oyh", [2, T], F32R)
            oyl = sb(m, "oyl", [2, T], F32R)
        with ExitStack() as m:
            y_pad = sb(m, "y_pad", [5 * T])
            yT = sb(m, "yT", [KT, T])
            y_out = sb(m, "y_out", [2, D])

        s_every, s_in, s_par, s_a, s_q, s_gp, s_ce = (sem(n) for n in (
            "every_in", "x_in_landed", "rows_in", "rows_a_in", "rows_q_in", "gate_params_in", "even_consts_in"))
        s_co, s_ch = sem("odd_consts_in"), sem("head_decays_in")
        raw_in = [sem(f"raw_in_{s}") for s in range(4)]
        hi_ready = sem("w_hi_ready")
        w_ready = sem("w_ready")
        multiplied = sem("multiplied")
        drained = [sem("drained_0"), sem("drained_1")]
        s_setup_t, s_setup_c = sem("setup_transposed"), sem("setup_copied")
        s_eps = sem("constants_set")
        q_sq, q_ss, q_sum, q_std, q_rs, q_xf, q_hi = (sem("norm_" + n) for n in (
            "squared", "added", "summed", "log", "inverse", "scaled", "hi"))
        q_lo = [sem("norm_lo_even"), sem("norm_lo_odd")]
        f_hi, f_lo = sem("ffn_hi"), sem("ffn_lo")
        state_in, state_free = sem("state_in"), sem("state_sent")
        ret_in, ret_free, o_start = sem("ret_in"), sem("ret_sent"), sem("odd_head_begun")
        rows_turned, rows_copied, rows_sent = sem("rows_turned"), sem("rows_copied"), sem("rows_sent")
        y_norm, y_row, y_sent = sem("y_normed"), sem("y_row_ready"), [sem("y_sent_0"), sem("y_sent_1")]

        e_pe, e_act, e_dve, e_pool = (Steps(sem("even_" + n), N) for n, N in (
            ("tensor", E_PE), ("scalar", E_ACT), ("vector", E_DVE), ("gpsimd", E_POOL)))
        a_pe, a_act, a_dve = (Steps(sem("gates_" + n), N) for n, N in (
            ("tensor", A_PE), ("scalar", A_ACT), ("vector", A_DVE)))
        o_pe, o_act, o_dve, o_pool = (Steps(sem("odd_" + n), N) for n, N in (
            ("tensor", O_PE), ("scalar", O_ACT), ("vector", O_DVE), ("gpsimd", O_POOL)))
        block_ = ctx.enter_context(nc.Block())

        def pair_view(p):
            return acc[:, p, :, 0:HALF]

        def halves(a):
            return a.rearrange("p (a n) -> p a n", a=2)

        def chunks(a):
            return a.rearrange("p (c n) -> p c n", n=P)

        def prompt_pad(buf, pre):
            return buf[:, pre:pre + TP]

        def sample_pad(buf, pre, pad):
            return buf[:, pre + TP:pad].rearrange("p (b n) -> p b n", b=NB)

        def seqs(a):
            return a.rearrange("p (b n) -> p b n", b=NB)

        def emptied(eng, phase, i, n):
            eng.wait_ge(drained[plan.pair(phase, n)], plan.drained(phase, i, n) + 1)

        def outputs_at(buf, at, stride):
            return buf[:, at:at + NB * stride].rearrange("p (b n) -> p b n", b=NB)[:, :, 0:LS]

        def diagonal(buf):
            return buf[:, :].rearrange("p (b n) -> p b n", b=NB)[:, :, 0:LS]

        def each_chunk(a):
            return a.unsqueeze(1).to_broadcast([P, NC, P])

        def state_in_wait(eng, i):
            eng.wait_ge(state_in, 16 * (i + 1))

        def wcol(w, col, n=P):
            return w.rearrange("(k p) c -> p k c", p=P)[:, :, ds(col, n)]

        w_e, w_o, w_eo, w_oo = even_w_in[0], odd_w_in[0], even_w_out[0], odd_w_out[0]
        E_COL = [2048, 1536, 2560, 3072, 512, 1024, 0]
        O_COL = [(1024, P, 0), (0, P, 0), (2048, 2 * P, 0), (2048, 2 * P, P), (4096, 2 * P, 0), (4096, 2 * P, P)]

        def load(sp, phase, i, j, dst, src, slots=1):
            s, _ = plan.landed(phase, i, j)
            if slots:
                sp.wait_ge(w_ready, plan.unit(phase, i, j) + slots)
            sp.dma_start(dst(raw[:, s, :]), src).then_inc(raw_in[s], 16)

        def by_kt(n=KT):
            return lambda r: r[:, 0:n * P].rearrange("p (k c) -> p k c", k=n)

        def two_rows(r):
            return r.rearrange("p (k c) -> p k c", k=2)

        def split_hi(act, phase, i, j, n=KT, again=False):
            s, there = plan.landed(phase, i, j)
            d = plan.split_slot(phase, j)
            act.wait_ge(raw_in[s], there)
            act.wait_ge(multiplied, plan.split_free(phase, i, j, again))
            nc.scalar.activation(w_hi[:, d, 0:n * P], raw[:, s, 0:n * P], ACT.Copy).then_inc(hi_ready, 1)

        def split_lo(pool, phase, i, j, n=KT):
            s, there = plan.landed(phase, i, j)
            d = plan.split_slot(phase, j)
            pool.wait_ge(hi_ready, plan.unit(phase, i, j) + 1)
            nc.gpsimd.tensor_tensor(w_lo[:, d, 0:n * P], raw[:, s, 0:n * P], w_hi[:, d, 0:n * P].bitcast(F32),
                                    ALU.subtract).then_inc(w_ready, 1)

        def product(pe, out, whi, wlo, mhi, mlo, first, last):
            for n, (w, mv) in enumerate(((whi, mhi), (whi, mlo), (wlo, mhi))):
                for h in range(2):
                    ins = nc.tensor.matmul(out[:, h, :], w, mv[:, h * HALF:(h + 1) * HALF],
                                           start=first and n == 0, stop=last and n == 2)
            return ins

        def unit(pe, phase, i, j, n, a=0, b=KT, wait_norm=None):
            d, p = plan.split_slot(phase, j), plan.pair(phase, n)
            if a == 0:
                pe.wait_ge(w_ready, plan.unit(phase, i, j) + 1 + RAW_LAG)
                pe.wait_ge(drained[p], plan.drained(phase, i, n))
            for k in range(a, b):
                if wait_norm is not None:
                    pe.wait_ge(q_lo[k % 2], (wait_norm * KT + k) // 2 + 1)
                ins = product(pe, pair_view(p), w_hi[:, d, k * P:(k + 1) * P], w_lo[:, d, k * P:(k + 1) * P],
                              xn_hi[:, k, :], xn_lo[:, k, :], k == 0, k == KT - 1)
            if b == KT:
                ins.then_inc(multiplied, 1)

        def rows_unit(pe, phase, i, j, base, src_hi, src_lo, ready=None):
            d = plan.split_slot(phase, j)
            pe.wait_ge(w_ready, plan.unit(phase, i, j) + 1 + RAW_LAG)
            for mb in range(4):
                p = plan.pair(phase, base + mb)
                pe.wait_ge(drained[p], plan.drained(phase, i, base + mb))
                for k in range(2):
                    c = (4 * k + mb) * P
                    ins = product(pe, pair_view(p), w_hi[:, d, c:c + P], w_lo[:, d, c:c + P],
                                  src_hi[:, k, :], src_lo[:, k, :], k == 0, k == 1)
                ins.then_inc(multiplied, 1)

        NORM_AFTER = (lambda m: ("x", 0, m), lambda m: ("even", DN_H - 1, 7 + m),
                      lambda m: ("down0", m // 2, m % 2), lambda m: ("odd", RET_H - 1, 6 + m),
                      lambda m: ("down1", m // 2, m % 2))

        def norm_sum(pe, k):
            first = 0 if k == 0 else KT - 1
            if first:
                pe.wait_ge(q_ss, (k + 1) * (KT - 1))
                for h in range(2):
                    nc.tensor.matmul(mx[:, h, 0:HALF], ones, n_ss[:, h * HALF:(h + 1) * HALF], start=True, stop=False)
            for t in range(first, KT):
                pe.wait_ge(q_sq, k * KT + t + 1)
                for h in range(2):
                    ins = nc.tensor.matmul(mx[:, h, 0:HALF], ones, n_sq[:, t % 2, h * HALF:(h + 1) * HALF],
                                           start=t == 0, stop=t == KT - 1)
                ins.then_inc(q_sum if t == KT - 1 else q_ss, 1)

        def norm_scalar(act, k, last=False, meanwhile=None):
            for t in range(KT):
                emptied(act, *NORM_AFTER[k](t))
                if t >= 2:
                    act.wait_ge(q_ss, k * (KT - 1) + t - 1)
                nc.scalar.activation(n_sq[:, t % 2, :], x[:, t, :], ACT.Square).then_inc(q_sq, 1)
            if meanwhile:
                meanwhile()
            act.wait_ge(q_sum, k + 1)
            nc.scalar.activation(halves(n_rs[:, :]), mx[:, 0:2, 0:HALF], ACT.Ln, bias=eps[:, 0:1],
                                 scale=1.0 / D).then_inc(q_std, 1)
            act.wait_ge(q_std, k + 1)
            nc.scalar.activation(n_rs[:, :], n_rs[:, :], ACT.Exp, scale=-0.5).then_inc(q_rs, 1)
            if not last:
                for t in range(KT):
                    act.wait_ge(q_xf, k * KT + t + 1)
                    nc.scalar.activation(xn_hi[:, t, :], n_xf[:, t % 4, :], ACT.Copy).then_inc(q_hi, 1)

        def low_part(eng, k, t):
            eng.wait_ge(q_hi, k * KT + t + 1)
            nc_eng = nc.vector if t % 2 == 0 else nc.gpsimd
            nc_eng.tensor_tensor(xn_lo[:, t, :], n_xf[:, t % 4, :], xn_hi[:, t, :].bitcast(F32),
                                 ALU.subtract).then_inc(q_lo[t % 2], 1)

        def norm_gpsimd(pool, k, last=False, meanwhile=None):
            for t in range(KT - 1) if k else ():
                pool.wait_ge(q_sq, k * KT + t + 1)
                if t == 0:
                    nc.gpsimd.tensor_copy(n_ss[:, :], n_sq[:, 0, :]).then_inc(q_ss, 1)
                else:
                    pool.wait_ge(q_ss, k * (KT - 1) + t)
                    nc.gpsimd.tensor_tensor(n_ss[:, :], n_ss[:, :], n_sq[:, t % 2, :], ALU.add).then_inc(q_ss, 1)
            if meanwhile:
                meanwhile()
            if not last:
                for t in range(1, KT, 2):
                    low_part(pool, k, t)

        def norm_vector(dve, k, last=False):
            dve.wait_ge(q_rs, k + 1)
            for t in range(KT):
                if not last and t >= 4:
                    dve.wait_ge(q_lo[t % 2], (k * KT + t - 4) // 2 + 1)
                g = cols[:, COL_NORM[k] + t:COL_NORM[k] + t + 1]
                dst = yT[:, t, :] if last else n_xf[:, t % 4, :]
                nc.vector.scalar_tensor_tensor(out=dst, in0=x[:, t, :], scalar=g, in1=n_rs[:, :], op0=ALU.mult,
                                               op1=ALU.mult).then_inc(y_norm if last else q_xf, 1)
                if not last and t % 2 == 1:
                    low_part(dve, k, t - 1)
            if not last:
                dve.wait_ge(q_xf, (k + 1) * KT)
                for n in range(2):
                    dve.wait_ge(q_lo[n], (k + 1) * KT // 2)

        def add_to_x(dve, phase, i, n, m):
            p = plan.pair(phase, n)
            dve.wait_ge(multiplied, plan.summed(phase, i, n))
            dst = x[:, m, :].rearrange("p a n -> p (a n)") if len(x[:, m, :].shape) == 3 else x[:, m, :]
            nc.vector.tensor_tensor(halves(dst), pair_view(p), halves(dst), ALU.add).then_inc(drained[p], 1)

        def ffn_tensor(pe, layer):
            up, down, k = f"up{layer}", f"down{layer}", 2 * layer + 1
            with pe.Fori(0, FT // 2) as i:
                for t in range(2):
                    unit(pe, up, i, 2 * t, 2 * t, wait_norm=k if t == 0 else None)
                    unit(pe, up, i, 2 * t + 1, 2 * t + 1)
            pe.wait_ge(f_lo, (layer + 1) * FT)
            with pe.Fori(0, KT // 2) as i:
                for t in range(2):
                    p = plan.pair(down, t)
                    pe.wait_ge(drained[p], plan.drained(down, i, t))
                    for j in range(3):
                        d = plan.split_slot(down, 3 * t + j)
                        pe.wait_ge(w_ready, plan.unit(down, i, 3 * t + j) + 1 + RAW_LAG)
                        for q in range(DOWN[j]):
                            k2 = 8 * j + q
                            ins = product(pe, pair_view(p), w_hi[:, d, q * P:(q + 1) * P],
                                          w_lo[:, d, q * P:(q + 1) * P], h_hi[:, k2, :], h_lo[:, k2, :],
                                          k2 == 0, k2 == FT - 1)
                        ins.then_inc(multiplied, 1)

        def split_next(act, phase, i, j, sizes=(KT,)):
            n = len(PHASES[phase][1])
            if j + 1 < n:
                split_hi(act, phase, i, j + 1, sizes[(j + 1) % len(sizes)])
            else:
                split_hi(act, phase, i + 1, 0, again=True)

        def ffn_scalar(act, layer, last=False):
            up, down = f"up{layer}", f"down{layer}"
            split_hi(act, up, 0, 1)
            with act.Fori(0, FT // 2) as i:
                for t in range(2):
                    act.wait_ge(multiplied, plan.summed(up, i, 2 * t))
                    act.wait_ge(drained[1], plan.drained(up, i, 2 * t + 1))
                    nc.scalar.activation(halves(f_g[:, :]), pair_view(0), ACT.Silu).then_inc(drained[0], 1)
                    split_hi(act, up, i + t, 2 * (1 - t), again=t == 1)
                    split_hi(act, up, i + t, 2 * (1 - t) + 1, again=t == 1)
                    act.wait_ge(drained[1], plan.drained(up, i, 2 * t + 1) + 1)
                    nc.scalar.activation(h_hi[:, ds(i * 2 + t, 1), :].rearrange("p a n -> p (a n)"), f_h[:, :],
                                         ACT.Copy).then_inc(f_hi, 1)
            for j in range(1, 6):
                split_next(act, down, 0, j, DOWN)
            with act.Fori(1, KT // 2 - last) as i:
                for j in range(6):
                    split_next(act, down, i, j, DOWN)
            if last:
                for j in range(5):
                    split_next(act, down, KT // 2 - 1, j, DOWN)

        def ffn_gpsimd(pool, layer):
            up, down = f"up{layer}", f"down{layer}"
            with pool.Fori(0, FT // 2) as i:
                for j in range(4):
                    split_lo(pool, up, i, j)
            with pool.Fori(0, KT // 2) as i:
                for j in range(6):
                    split_lo(pool, down, i, j, DOWN[j % 3])

        def ffn_vector(dve, layer):
            up, down = f"up{layer}", f"down{layer}"
            with dve.Fori(0, FT // 2) as i:
                for t in range(2):
                    n = layer * FT + i * 2 + t + 1
                    dve.wait_ge(multiplied, plan.summed(up, i, 2 * t + 1))
                    dve.wait_ge(drained[0], plan.drained(up, i, 2 * t) + 1)
                    nc.vector.tensor_tensor(halves(f_h[:, :]), pair_view(1), halves(f_g[:, :]),
                                            ALU.mult).then_inc(drained[1], 1)
                    dve.wait_ge(f_hi, n)
                    nc.vector.tensor_tensor(h_lo[:, ds(i * 2 + t, 1), :].rearrange("p a n -> p (a n)"), f_h[:, :],
                                            h_hi[:, ds(i * 2 + t, 1), :].rearrange("p a n -> p (a n)").bitcast(F32),
                                            ALU.subtract).then_inc(f_lo, 1)
                    dve.wait_ge(f_lo, n)
            with dve.Fori(0, KT // 2) as i:
                for t in range(2):
                    add_to_x(dve, down, i, t, ds(i * 2 + t, 1))

        C_ATT, C_ATT_S, C_IN, C_IN_S, C_KD = 0, P, P + TS, 2 * P + TS, 2 * P + 2 * TS
        kdec_p, kdec_s = ch[:, C_KD:C_KD + 1], ch[0:TS, C_KD + 1:C_KD + 2]
        cdec_p, cdec_s = ch[:, C_KD + 2:C_KD + 3], ch[:, C_KD + 3:C_KD + 4]

        def odd_scalar(act, i):
            def evac_rotary(j, a, b, scale):
                p = plan.pair("odd", j)
                act.wait_ge(multiplied, plan.summed("odd", i, j))
                nc.scalar.activation(halves(a[:, :]), pair_view(p), ACT.Copy, scale=scale)
                nc.scalar.activation(halves(b[0:64, :]), acc[64:128, p, :, 0:HALF], ACT.Copy, scale=scale)
                nc.scalar.activation(halves(b[64:128, :]), acc[0:64, p, :, 0:HALF], ACT.Copy, scale=scale)\
                    .then_inc(drained[p], 1)

            def evac(j, out, func):
                act.wait_ge(multiplied, plan.summed("odd", i, j))
                nc.scalar.activation(halves(out), pair_view(plan.pair("odd", j)), func)\
                    .then_inc(drained[plan.pair("odd", j)], 1)

            split_next(act, "odd", i, 0)
            evac_rotary(0, ka, kb, P ** -0.5)
            split_next(act, "odd", i, 1)
            evac_rotary(1, qa, qb, 1.0)
            split_next(act, "odd", i, 2)
            evac(2, va[:, 0, :], ACT.Copy)
            split_next(act, "odd", i, 3)
            e = o_pe
            e.wait(act, i, "tk")
            act.wait_ge(s_ch, 16 * (i + 1))
            nc.scalar.activation(kdt[:, 0:NC, :], chunks(mx[:, 2, :]), ACT.Copy, scale=kdec_p)
            o_act.done(nc.scalar.activation(kdt[0:TS, NC, :], mx[0:TS, 3, 0:P], ACT.Copy, scale=kdec_s), "kdt")
            e.wait(act, i, "tv0")
            nc.scalar.activation(vtok[:, 0:NC, 0:P], chunks(mx[:, 0, :]), ACT.Copy)
            o_act.done(nc.scalar.activation(vtok[0:TS, NC, 0:P], mx[0:TS, 1, 0:P], ACT.Copy), "v0")
            evac(3, va[:, 1, :], ACT.Copy)
            e.wait(act, i, "tv1")
            nc.scalar.activation(vtok[:, 0:NC, P:2 * P], chunks(mx[:, 2, :]), ACT.Copy)
            o_act.done(nc.scalar.activation(vtok[0:TS, NC, P:2 * P], mx[0:TS, 3, 0:P], ACT.Copy), "v1")
            split_next(act, "odd", i, 4)
            evac(4, gs[:, 0, :], ACT.Silu)
            split_next(act, "odd", i, 5)
            evac(5, gs[:, 1, :], ACT.Silu)
            o_dve.wait(act, i, "cen")
            o_act.done(nc.scalar.activation(osq[:, :, :], of[:, :, :], ACT.Square), "osq")
            e.wait(act, i, "var")
            o_act.done(nc.scalar.activation(halves(orv[:, :]), mx[:, 2:4, 0:HALF], ACT.Ln, bias=eps[:, 1:2],
                                            scale=1.0 / RET_V), "oln")
            o_act.wait(act, i, "oln")
            o_act.done(nc.scalar.activation(orv[:, :], orv[:, :], ACT.Exp, scale=-0.5), "oinv")
            split_next(act, "odd", i, 6)
            for d in range(2):
                o_dve.wait(act, i, f"y{d}")
                o_act.done(nc.scalar.activation(oyh[:, d, :], of[:, d, :], ACT.Copy), f"yh{d}")
            o_dve.wait(act, i, "rs")
            act.dma_start(ret_s[0].rearrange("b h k v -> h k b v")[ds(i, 1)].rearrange("a k b v -> k (a b) v"),
                          r_s[:, :, :]).then_inc(ret_free, 16)
            act.dma_start(ret_p[0, 0][ds(i, 1)].rearrange("a k v -> k (a v)"), rst[:, NC - 1, :]).then_inc(ret_free, 16)
            split_next(act, "odd", i, 7)

        def odd_vector(dve, i):
            def step(ins, name):
                o_dve.done(ins, name)
                o_dve.wait(dve, i, name)

            nc.vector.tensor_copy(gnw[:, 0, :], cols[:, COL_GN_G:COL_GN_G + 16].rearrange("p (h g) -> p h g", g=2)
                                  [:, ds(i, 1), :].rearrange("p a g -> p (a g)"))
            nc.vector.tensor_copy(gnw[:, 1, :], cols[:, COL_GN_B:COL_GN_B + 16].rearrange("p (h g) -> p h g", g=2)
                                  [:, ds(i, 1), :].rearrange("p a g -> p (a g)")).then_inc(o_start, 1)
            dve.wait_ge(s_co, 16)
            for j, (a, b, out, n) in enumerate(((ka, kb, rk, "k"), (qa, qb, rq, "q"))):
                emptied(dve, "odd", i, j)
                nc.vector.tensor_tensor(t1[:, :], a[:, :], co[:, 0, :], ALU.mult)
                step(nc.vector.tensor_tensor(t2[:, :], b[:, :], co[:, 1, :], ALU.mult), "t" + n)
                step(nc.vector.tensor_tensor(out[:, :], t1[:, :], t2[:, :], ALU.add), "r" + n)
            dve.wait_ge(s_ch, 16 * (i + 1))
            nc.vector.tensor_tensor(chunks(rqg[:, 0:TP]), chunks(rq[:, 0:TP]), each_chunk(ch[:, C_IN:C_IN + P]),
                                    ALU.mult)
            step(nc.vector.tensor_tensor(rqg[:, TP:T], rq[:, TP:T], ch[:, C_IN_S:C_IN_S + TS], ALU.mult), "qg")
            o_pe.wait(dve, i, "att")
            nc.vector.tensor_tensor(chunks(att[:, 0:TP]), chunks(mx[:, 0, :]), each_chunk(ch[:, C_ATT:C_ATT + P]),
                                    ALU.mult)
            step(nc.vector.tensor_tensor(att[0:TS, TP:T], mx[0:TS, 1, 0:TS], ch[0:TS, C_ATT_S:C_ATT_S + TS],
                                         ALU.mult), "att")
            o_pe.wait(dve, i, "kv")
            step(nc.vector.tensor_copy(rst[:, 0, :], mx[:, 0, 0:RET_V]), "r0")
            for c in range(1, NC):
                src = mx[:, c // 2, (c % 2) * RET_V:(c % 2 + 1) * RET_V]
                step(nc.vector.scalar_tensor_tensor(out=rst[:, c, :], in0=rst[:, c - 1, :], scalar=cdec_p, in1=src,
                                                    op0=ALU.mult, op1=ALU.add), f"r{c}")
            o_pe.wait(dve, i, "op")
            step(nc.vector.tensor_copy(of[:, :, 0:TP], mx[:, 2:4, :]), "of_p")
            o_pe.wait(dve, i, "os")
            step(nc.vector.tensor_copy(of[:, :, TP:T], mx[:, 0, 0:2 * TS].rearrange("p (d n) -> p d n", d=2)), "of_s")
            o_pe.wait(dve, i, "mean")
            for d in range(2):
                ins = nc.vector.scalar_tensor_tensor(out=halves(of[:, d, :]), in0=mx[:, 0:2, 0:HALF],
                                                     scalar=-1.0 / RET_V, in1=halves(of[:, d, :]), op0=ALU.mult,
                                                     op1=ALU.add)
            step(ins, "cen")
            o_act.wait(dve, i, "oinv")
            for d in range(2):
                step(nc.vector.scalar_tensor_tensor(out=of[:, d, :], in0=of[:, d, :], scalar=gnw[:, 0, d:d + 1],
                                                    in1=orv[:, :], op0=ALU.mult, op1=ALU.mult), f"on{d}")
                emptied(dve, "odd", i, 4 + d)
                step(nc.vector.scalar_tensor_tensor(out=of[:, d, :], in0=of[:, d, :], scalar=gnw[:, 1, d:d + 1],
                                                    in1=gs[:, d, :], op0=ALU.add, op1=ALU.mult), f"y{d}")
            for d in range(2):
                o_act.wait(dve, i, f"yh{d}")
                step(nc.vector.tensor_tensor(oyl[:, d, :], of[:, d, :], oyh[:, d, :].bitcast(F32), ALU.subtract),
                     f"yl{d}")
            o_pe.wait(dve, i, "kvs")
            step(nc.vector.scalar_tensor_tensor(out=r_s[:, :, :].rearrange("p b n -> p (b n)"),
                                                in0=r_s[:, :, :].rearrange("p b n -> p (b n)"), scalar=cdec_s,
                                                in1=mx[:, :, :].rearrange("p a n -> p (a n)"), op0=ALU.mult,
                                                op1=ALU.add), "rs")
            for m in range(KT):
                add_to_x(dve, "odd", i, 6 + m, m)

        def odd_tensor(pe, i):
            def mm(out, lhs, rhs, start=True, stop=True):
                return nc.tensor.matmul(out, lhs, rhs, start=start, stop=stop)

            def at(a, c):
                return a[:, c * P:(c + 1) * P]

            def turn(src, bank, name):
                for c in range(NC):
                    nc.tensor.transpose(mx[:, bank, c * P:(c + 1) * P], at(src, c), ident)
                o_pe.done(nc.tensor.transpose(mx[0:TS, bank + 1, 0:P], src[:, TP:T], ident), name)

            def U(j, a=0, b=KT, wait_norm=None):
                unit(pe, "odd", i, j, j, a, b, wait_norm)

            U(0, wait_norm=2)
            U(1)
            U(2, 0, 4)
            o_dve.wait(pe, i, "rq")
            for c in range(NC):
                mm(mx[:, 0, c * P:(c + 1) * P], at(rk, c), at(rq, c))
            o_pe.done(mm(mx[0:TS, 1, 0:TS], rk[:, TP:T], rq[:, TP:T]), "att")
            U(2, 4, 8)
            turn(rk, 2, "tk")
            U(3, 0, 4)
            emptied(pe, "odd", i, 2)
            o_dve.wait(pe, i, "att")
            turn(va[:, 0, :], 0, "tv0")
            U(3, 4, 8)
            U(4, 0, 2)
            emptied(pe, "odd", i, 3)
            o_act.wait(pe, i, "kdt")
            turn(va[:, 1, :], 2, "tv1")
            U(4, 2, 5)
            o_act.wait(pe, i, "v1")
            for c in range(NC):
                ins = mm(mx[:, c // 2, (c % 2) * RET_V:(c % 2 + 1) * RET_V], kdt[:, c, :], vtok[:, c, :])
            o_pe.done(ins, "kv")
            U(4, 5, 8)
            U(5, 0, 2)
            o_dve.wait(pe, i, f"r{NC - 1}")
            for d in range(2):
                for c in range(NC):
                    ins = mm(mx[:, 2 + d, c * P:(c + 1) * P], vtok[:, c, d * P:(d + 1) * P], at(att, c), True, c == 0)
                    if c:
                        ins = mm(mx[:, 2 + d, c * P:(c + 1) * P], rst[:, c - 1, d * P:(d + 1) * P], at(rqg, c),
                                 False, True)
            o_pe.done(ins, "op")
            U(5, 2, 4)
            pe.wait_ge(ret_in, 16 * (i + 1))
            for d in range(2):
                mm(mx[:, 0, d * TS:(d + 1) * TS], vtok[0:TS, NC, d * P:(d + 1) * P], att[0:TS, TP:T], True, False)
                for b in range(NB):
                    c = d * TS + b * LS
                    ins = mm(mx[:, 0, c:c + LS], r_s[:, b, d * P:(d + 1) * P], rqg[:, TP + b * LS:TP + (b + 1) * LS],
                             False, b == NB - 1)
            o_pe.done(ins, "os")
            U(5, 4, 6)
            o_dve.wait(pe, i, "of_s")
            for h in range(2):
                for d in range(2):
                    ins = mm(mx[:, h, 0:HALF], ones, of[:, d, h * HALF:(h + 1) * HALF], d == 0, d == 1)
            o_pe.done(ins, "mean")
            U(5, 6, 8)
            o_act.wait(pe, i, "osq")
            for h in range(2):
                for d in range(2):
                    ins = mm(mx[:, 2 + h, 0:HALF], ones, osq[:, d, h * HALF:(h + 1) * HALF], d == 0, d == 1)
            o_pe.done(ins, "var")
            o_pool.wait(pe, i, "kdm")
            o_act.wait(pe, i, "oln")
            for b in range(NB):
                ins = mm(mx[:, b // 2, (b % 2) * RET_V:(b % 2 + 1) * RET_V], kdm[0:TS, b, :], vtok[0:TS, NC, :])
            o_pe.done(ins, "kvs")
            o_dve.wait(pe, i, "yl1")
            for j in range(2):
                rows_unit(pe, "odd", i, 6 + j, 6 + 4 * j, oyh, oyl)

        def odd_gpsimd(pool, i):
            for j in range(5):
                split_lo(pool, "odd", i, j)
            o_act.wait(pool, i, "kdt")
            o_pool.done(nc.gpsimd.tensor_tensor(kdm[0:TS, :, :], kdt[0:TS, NC, :].unsqueeze(1).to_broadcast([TS, NB, P]),
                                                block[0:TS, :].unsqueeze(2).to_broadcast([TS, NB, P]), ALU.mult), "kdm")
            for j in range(5, 8):
                split_lo(pool, "odd", i, j)

        @block_.sync
        def _(sp):
            sp.dma_start(every[:, :], c_every).then_inc(s_every, 16)
            sp.dma_start(x_in[:, 0:NC, :], x_prompt[0].rearrange("(c p) d -> p c d", p=P)).then_inc(s_in, 16)
            sp.dma_start(x_in[0:TS, NC, :], x_sample.rearrange("b t d -> (b t) d")).then_inc(s_in, 16)
            at = 0
            for src in (norm_mix, norm_ffn, final_norm, odd_gn_g, odd_gn_b):
                a = (src.rearrange("l (k p) -> (l k) p", p=P) if len(src.shape) == 2
                     else src.rearrange("(k p) -> k p", p=P))
                sp.dma_start(rows_1[at:at + a.shape[0], :], a).then_inc(s_par, 16)
                at += a.shape[0]
            at = 0
            for src in (even_conv_a, even_conv_qkv, even_dn_norm):
                a = (src[0].rearrange("w (k p) -> (w k) p", p=P) if len(src.shape) == 3 else src)
                sp.dma_start(rows_2[at:at + a.shape[0], :], a).then_inc(s_par, 16)
                at += a.shape[0]
            load(sp, "ab", 0, 0, by_kt(), wcol(w_e, EVEN_IN - P))
            sp.dma_start(rows_a[0:2 * NB, :], state_conv_a[0].rearrange("b w c -> (b w) c")).then_inc(s_a, 16)
            sp.dma_start(rows_q[0:3 * NB, :], state_conv_qkv[0].rearrange("b w c -> (b w) c")).then_inc(s_q, 16)
            sp.dma_start(ce[:, :], c_even).then_inc(s_ce, 16)
            sp.dma_start(dtb[:, :], even_dt_bias.partition_broadcast(P)[:, 0, :]
                         if len(even_dt_bias.partition_broadcast(P).shape) == 3
                         else even_dt_bias.partition_broadcast(P)).then_inc(s_gp, 16)
            sp.dma_start(nega[:, :], even_a_log.partition_broadcast(P)[:, 0, :]
                         if len(even_a_log.partition_broadcast(P).shape) == 3
                         else even_a_log.partition_broadcast(P)).then_inc(s_gp, 16)
            with sp.Fori(0, DN_H) as i:
                for j in range(7):
                    load(sp, "even", i, j, by_kt(), wcol(w_e, E_COL[j] + i * P), slots={5: 2, 6: 0}.get(j, 1))
                    if j == 4:
                        sp.wait_ge(state_free, 32 * i + 1)
                        sp.dma_start(s_s[:, :, :], state_delta[0].rearrange("b h k v -> h k b v")[ds(i, 1)]
                                     .rearrange("a k b v -> k (a b) v")).then_inc(state_in, 16)
                for j in range(2):
                    load(sp, "even", i, 7 + j, two_rows, w_eo.rearrange("(g r p) n -> r p g n", g=2, p=P)
                         [ds(i, 1), :, :, j * 512:(j + 1) * 512].rearrange("a p g n -> p (a g) n"))
            for layer in range(2):
                wg, wu, wd = ffn_w_gate[layer], ffn_w_up[layer], ffn_w_down[layer]
                up, down = f"up{layer}", f"down{layer}"
                with sp.Fori(0, FT // 2) as i:
                    for t in range(2):
                        load(sp, up, i, 2 * t, by_kt(), wcol(wg, i * 2 * P + t * P))
                        load(sp, up, i, 2 * t + 1, by_kt(), wcol(wu, i * 2 * P + t * P))
                with sp.Fori(0, KT // 2) as i:
                    for t in range(2):
                        for j in range(3):
                            load(sp, down, i, 3 * t + j, by_kt(DOWN[j]),
                                 wd.rearrange("(k p) c -> p k c", p=P)[:, 8 * j:8 * j + DOWN[j], ds(i * 2 * P + t * P, P)])
                if layer == 0:
                    with sp.Fori(0, RET_H) as i:
                        for j, (c0, per, off) in enumerate(O_COL):
                            load(sp, "odd", i, j, by_kt(), wcol(w_o, c0 + off + i * per),
                                 slots={0: 2, 1: 0}.get(j, 1))
                            if j == 3:
                                sp.wait_ge(o_start, i + 1)
                                sp.dma_start(ch[:, :], c_heads[ds(i, 1)].rearrange("a p n -> p (a n)")).then_inc(s_ch, 16)
                                sp.wait_ge(ret_free, 32 * i + 1)
                                sp.dma_start(r_s[:, :, :], state_ret[0].rearrange("b h k v -> h k b v")[ds(i, 1)]
                                             .rearrange("a k b v -> k (a b) v")).then_inc(ret_in, 16)
                        for j in range(2):
                            load(sp, "odd", i, 6 + j, two_rows, w_oo.rearrange("(r g p) n -> r p g n", g=2, p=P)
                                 [ds(i, 1), :, :, j * 512:(j + 1) * 512].rearrange("a p g n -> p (a g) n"))
            for c in range(NC + 1):
                sp.wait_ge(y_row, c + 1)
                dst = y_prompt[0, c * P:(c + 1) * P, :] if c < NC else y_sample.rearrange("b t d -> (b t) d")
                n = P if c < NC else TS
                sp.dma_start(dst, y_out[0:n, c % 2, :]).then_inc(y_sent[c % 2], 16)
            sp.wait_ge(y_sent[0], 16 * 3)
            sp.wait_ge(y_sent[1], 16 * 2)
            sp.wait_ge(state_free, 32 * DN_H + 1)
            sp.wait_ge(ret_free, 32 * RET_H + 1)
            sp.wait_ge(rows_sent, 16 * 8)

        def even_scalar(act, i, inner=True):
            def evac_conv(j):
                p = plan.pair("even", j)
                act.wait_ge(multiplied, plan.summed("even", i, j))
                nc.scalar.activation(cbuf[:, WQ - 1:WQ - 1 + HALF], acc[:, p, 0, 0:HALF], ACT.Copy)
                nc.scalar.activation(cbuf[:, WQ - 1 + HALF:SQ], acc[:, p, 1, 0:TP - HALF], ACT.Copy)
                nc.scalar.activation(sample_pad(cbuf, WQ - 1, PADQ)[:, :, WQ - 1:], seqs(acc[:, p, 1, TP - HALF:HALF]),
                                     ACT.Copy).then_inc(drained[p], 1)

            def inverse_root(name, bank, scale):
                e_act.done(nc.scalar.activation(halves(std[:, :]), mx[:, bank:bank + 2, 0:HALF], ACT.Ln,
                                                bias=eps[:, 0:1], scale=scale), name + "_ln")
                e_act.wait(act, i, name + "_ln")
                e_act.done(nc.scalar.activation(std[:, :], std[:, :], ACT.Exp, scale=-0.5), name + "_inv")

            split_next(act, "even", i, 0)
            evac_conv(0)
            e_pe.wait(act, i, "rows")
            nc.scalar.activation(gr[:, 0:TP], mx[:, 0, :], ACT.Copy)
            e_act.done(nc.scalar.activation(gr[:, TP:T], mx[:, 1, 0:TS], ACT.Copy), "gr")
            nc.scalar.activation(eg[:, 0:TP], mx[:, 0, :], ACT.Exp)
            e_act.done(nc.scalar.activation(eg[:, TP:T], mx[:, 1, 0:TS], ACT.Exp), "eg")
            e_dve.wait(act, i, "ck")
            e_act.done(nc.scalar.activation(ks[:, :], cs[:, :], ACT.Silu), "ks")
            e_act.wait(act, i, "ks")
            e_act.done(nc.scalar.activation(sq[:, :], ks[:, :], ACT.Square), "k_sq")
            split_next(act, "even", i, 1)
            evac_conv(1)
            e_dve.wait(act, i, "dt_in")
            e_act.done(nc.scalar.activation(dm[:, :], dm[:, :], ACT.Exp, scale=-1.0), "dm")
            e_act.done(nc.scalar.activation(dt_[:, :], dt_[:, :], ACT.Exp), "dt")
            e_pe.wait(act, i, "l2k")
            inverse_root("k", 0, 1.0)
            e_dve.wait(act, i, "cq")
            e_act.done(nc.scalar.activation(qs[:, :], cs[:, :], ACT.Silu), "qs")
            e_act.wait(act, i, "qs")
            e_act.done(nc.scalar.activation(sq[:, :], qs[:, :], ACT.Square), "q_sq")
            split_next(act, "even", i, 2)
            e_pe.wait(act, i, "l2q")
            e_dve.wait(act, i, "kT")
            inverse_root("q", 2, 1.0)
            evac_conv(2)
            split_next(act, "even", i, 3)
            e_dve.wait(act, i, "cv")
            e_act.done(nc.scalar.activation(vs[:, :], cs[:, :], ACT.Silu), "vs")
            act.wait_ge(multiplied, plan.summed("even", i, 3))
            nc.scalar.activation(halves(zs[:, :]), pair_view(plan.pair("even", 3)), ACT.Silu)\
                .then_inc(drained[plan.pair("even", 3)], 1)
            split_next(act, "even", i, 4)

            def copy_p(s):
                e_pe.wait(act, i, f"P{s}")
                if s <= 4:
                    nc.scalar.activation(pp[0:TS, TP:T], mx[0:TS, 1, 0:TS], ACT.Copy)
                e_act.done(nc.scalar.activation(pp[:, 0:TP], mx[:, 0, :], ACT.Copy), f"p{s}")

            copy_p(2)
            copy_p(4)
            act.wait_ge(multiplied, plan.summed("even", i, 4))
            nc.scalar.activation(halves(gcs[:, :]), pair_view(plan.pair("even", 4)), ACT.Copy)\
                .then_inc(drained[plan.pair("even", 4)], 1)
            split_next(act, "even", i, 5)
            copy_p(8)
            copy_p(16)
            split_next(act, "even", i, 6)
            copy_p(32)
            copy_p(64)
            split_next(act, "even", i, 7)
            emptied(act, "even", i, 6)
            e_act.done(nc.scalar.activation(yh[:, 0, :], ca1[:, 0:T], ACT.Copy), "yah")
            for c in range(NC):
                e_pe.wait(act, i, f"u{c}")
                e_act.done(nc.scalar.activation(uu[:, :], mx[:, 1, 256:384], ACT.Copy), f"uu{c}")
                if c == 2:
                    e_pe.wait(act, i, "us")
                    e_act.done(nc.scalar.activation(us_[0:TS, :], mx[0:TS, 2, P:2 * P], ACT.Copy), "us_")
            e_dve.wait(act, i, "oT_p")
            e_act.done(nc.scalar.activation(sq[:, :], oT[:, :], ACT.Square), "o_sq")
            e_pe.wait(act, i, "onorm")
            inverse_root("o", 0, 1.0 / DN_D)
            e_dve.wait(act, i, "yb")
            e_act.done(nc.scalar.activation(yh[:, 1, :], yf[:, :], ACT.Copy), "ybh")
            e_dve.wait(act, i, "s_new")
            act.dma_start(delta_s[0].rearrange("b h k v -> h k b v")[ds(i, 1)].rearrange("a k b v -> k (a b) v"),
                          s_s[:, :, :]).then_inc(state_free, 16)
            act.dma_start(delta_p[0, 0][ds(i, 1)].rearrange("a k v -> k (a v)"), s_p[:, :]).then_inc(state_free, 16)
            split_next(act, "even", i, 8)

        @block_.scalar
        def _(act):
            for t in range(1, KT, 2):
                act.wait_ge(multiplied, plan.summed("x", 0, t))
                nc.scalar.activation(x[:, t, 0:TP], acc[:, 1, 0, :], ACT.Copy)
                nc.scalar.activation(x[:, t, TP:T], acc[:, 1, 1, 0:TS], ACT.Copy).then_inc(drained[1], 1)
            act.wait_ge(s_eps, 1)
            split_hi(act, "ab", 0, 0)
            norm_scalar(act, 0)
            split_hi(act, "even", 0, 0)
            act.wait_ge(multiplied, plan.summed("ab", 0, 0))
            nc.scalar.activation(halves(yf[:, :]), pair_view(1), ACT.Copy).then_inc(drained[1], 1)
            a_dve.wait(act, 0, "ad")
            a_act.done(nc.scalar.activation(g_ab[:, :, :], g_ab[:, :, :], ACT.Abs), "abs")
            a_act.wait(act, 0, "abs")
            a_act.done(nc.scalar.activation(g_ab[:, :, :], g_ab[:, :, :], ACT.Exp, scale=-1.0), "exp")
            act.wait_ge(s_gp, 32)
            a_act.done(nc.scalar.activation(nega[:, :], nega[:, :], ACT.Exp), "nega")
            a_act.wait(act, 0, "exp")
            a_act.done(nc.scalar.activation(g_ab[:, :, :], g_ab[:, :, :], ACT.Ln, bias=1.0), "ln")
            a_act.done(nc.scalar.activation(g_beta[:, :, :], gate[:, :, DN_H:2 * DN_H], ACT.Sigmoid), "beta")
            a_pe.wait(act, 0, "gcum")
            nc.scalar.activation(kdec[:, 0:NC, :], mx[:, 3, 0:NC * DN_H].rearrange("p (c h) -> p c h", h=DN_H),
                                 ACT.Exp)
            a_act.done(nc.scalar.activation(kdec[0:TS, NC, :], mx[0:TS, 3, 16:16 + DN_H], ACT.Exp), "kdec")
            with act.Fori(0, DN_H) as i:
                even_scalar(act, i)
            norm_scalar(act, 1)
            for n in range(4):
                act.wait_ge(rows_copied, n + 1)
                k = 2 if n == 0 else 3
                dst_p = conv_a_p[0, 0] if n == 0 else conv_qkv_p[0, 0][:, (n - 1) * CA:n * CA]
                dst_s = (conv_a_s[0] if n == 0 else conv_qkv_s[0][:, :, (n - 1) * CA:n * CA])
                act.dma_start(dst_p, out_rows[0:k, n, :]).then_inc(rows_sent, 16)
                act.dma_start(dst_s.rearrange("b w c -> (b w) c"), out_rows[k:k + k * NB, n, :]).then_inc(rows_sent, 16)
            act.wait_ge(rows_sent, 16 * 8)
            act.wait_ge(state_free, 32 * DN_H + 1)
            ffn_scalar(act, 0)
            norm_scalar(act, 2, meanwhile=lambda: act.dma_start(
                co[:, :, :], c_odd.rearrange("p (a n) -> p a n", a=2)).then_inc(s_co, 16))
            with act.Fori(0, RET_H) as i:
                odd_scalar(act, i)
            norm_scalar(act, 3)
            act.wait_ge(ret_free, 32 * RET_H + 1)
            ffn_scalar(act, 1, last=True)
            norm_scalar(act, 4, last=True)
            for c in range(1, NC + 1, 2):
                act.wait_ge(multiplied, plan.summed("y", 0, c))
                if c > 1:
                    act.wait_ge(y_sent[1], 16)
                act.wait_ge(y_row, c)
                nc.scalar.activation(y_out[:, 1, :].rearrange("p (a n) -> p a n", a=2), acc[:, 1, :, :],
                                     ACT.Copy).then_inc(y_row, 1)

        def even_vector(dve, i):
            def w(n):
                return pw[:, n:n + 1]

            def step(ins, name):
                e_dve.done(ins, name)
                e_dve.wait(dve, i, name)

            def conv_qkv(j, kind, name):
                emptied(dve, "even", i, j)
                nc.vector.tensor_copy(out_q[:, kind, ds(i, 1), 0:3].rearrange("p a n -> p (a n)"), cbuf[:, SQ - 3:SQ])
                nc.vector.tensor_copy(out_q[:, kind, ds(i, 1), 3:].rearrange("p a (b n) -> p (a b) n", n=3),
                                      sample_pad(cbuf, WQ - 1, PADQ)[:, :, LS:])
                step(nc.vector.tensor_scalar(ca1[:, 0:NQ], cbuf[:, 0:NQ], w(kind), None, ALU.mult), name + "0")
                for t, (a, b) in ((1, (ca1, ca2)), (2, (ca2, ca1))):
                    step(nc.vector.scalar_tensor_tensor(out=b[:, 0:NQ], in0=cbuf[:, t:t + NQ], scalar=w(3 * t + kind),
                                                        in1=a[:, 0:NQ], op0=ALU.mult, op1=ALU.add),
                         f"{name}{t}")
                nc.vector.scalar_tensor_tensor(out=cs[:, 0:TP], in0=cbuf[:, 3:3 + TP], scalar=w(9 + kind),
                                               in1=ca1[:, 0:TP], op0=ALU.mult, op1=ALU.add)
                step(nc.vector.scalar_tensor_tensor(out=seqs(cs[:, TP:T]), in0=sample_pad(cbuf, WQ - 1, PADQ)[:, :, 3:],
                                                    scalar=w(9 + kind), in1=outputs_at(ca1, SQ, LS + WQ - 1),
                                                    op0=ALU.mult, op1=ALU.add), name)

            def prefix(kind, name):
                step(nc.vector.tensor_copy(sample_pad(cbuf, WQ - 1, PADQ)[:, :, 0:3],
                                           pre_q[:, kind, ds(i, 1), :].rearrange("p a (b n) -> p (a b) n", n=3)), name)

            nc.vector.tensor_copy(pw[:, 0:12].rearrange("p (t a) -> p t a", a=1),
                                  cols[:, COL_CONV_Q:COL_CONV_Q + 48].rearrange("p (t h) -> p t h", h=4)[:, :, ds(i, 1)])
            step(nc.vector.tensor_copy(pw[:, 12:15].rearrange("p (t a) -> p t a", a=1),
                                       cols[:, COL_CONV_A:COL_CONV_A + 12].rearrange("p (t h) -> p t h", h=4)
                                       [:, :, ds(i, 1)]), "pw")
            nc.vector.tensor_copy(gbc[:, :, :], g_g[:, :, ds(i, 1)].to_broadcast([P, NC + 1, P]))
            step(nc.vector.tensor_copy(bbc[:, :, :], g_beta[:, :, ds(i, 1)].to_broadcast([P, NC + 1, P])), "gbc")
            prefix(1, "pre_k")
            conv_qkv(0, 1, "ck")
            e_act.wait(dve, i, "eg")
            nc.vector.tensor_tensor(bg[:, 0:TP], mx[:, 2, :], eg[:, 0:TP], ALU.mult)
            step(nc.vector.tensor_tensor(bg[:, TP:T], mx[:, 1, TS:2 * TS], eg[:, TP:T], ALU.mult), "bg")
            nc.vector.tensor_tensor(chunks(dm[:, 0:TP]), chunks(gr[:, 0:TP]),
                                    gcum[:, 0:NC, ds(i, 1)].to_broadcast([P, NC, P]), ALU.subtract)
            step(nc.vector.tensor_tensor(dm[:, TP:T], gr[:, TP:T],
                                         gcum[:, NC, ds(i, 1)].to_broadcast([P, TS]), ALU.subtract), "df")
            step(nc.vector.tensor_scalar(dt_[:, :], dm[:, :], 0.0, None, ALU.min), "dt_lo")
            step(nc.vector.tensor_scalar(dm[:, :], dm[:, :], 0.0, None, ALU.max), "dt_in")
            prefix(0, "pre_q")
            e_act.wait(dve, i, "ks")
            conv_qkv(1, 0, "cq")
            e_act.wait(dve, i, "k_inv")
            step(nc.vector.tensor_tensor(kT[:, :], ks[:, :], std[:, :], ALU.mult), "kT")
            step(nc.vector.tensor_tensor(kbg[:, :], kT[:, :], bg[:, :], ALU.mult), "kbg")
            step(nc.vector.tensor_copy(diagonal(km), seqs(kbg[:, TP:T])), "km")
            e_act.wait(dve, i, "dt")
            nc.vector.tensor_tensor(chunks(dm[:, 0:TP]), chunks(dm[:, 0:TP]), bbc[:, 0:NC, :], ALU.mult)
            step(nc.vector.tensor_tensor(dm[0:TS, TP:T], dm[0:TS, TP:T], bbc[0:TS, NC, 0:TS], ALU.mult), "dmb")
            e_act.wait(dve, i, "q_inv")
            step(nc.vector.scalar_tensor_tensor(out=qT[:, :], in0=qs[:, :], scalar=DN_D ** -0.5, in1=std[:, :],
                                                op0=ALU.mult, op1=ALU.mult), "qT")
            step(nc.vector.tensor_tensor(qg[:, :], qT[:, :], eg[:, :], ALU.mult), "qg")
            e_pe.wait(dve, i, "kk")
            nc.vector.tensor_tensor(dm[:, 0:TP], mx[:, 0, :], dm[:, 0:TP], ALU.mult)
            step(nc.vector.tensor_tensor(dm[0:TS, TP:T], mx[0:TS, 1, 0:TS], dm[0:TS, TP:T], ALU.mult), "A")
            prefix(2, "pre_v")
            e_act.wait(dve, i, "qs")
            conv_qkv(2, 2, "cv")
            e_pe.wait(dve, i, "kq")
            e_pool.wait(dve, i, "dtm")
            nc.vector.tensor_tensor(dt_[:, 0:TP], mx[:, 2, :], dt_[:, 0:TP], ALU.mult)
            step(nc.vector.tensor_tensor(dt_[0:TS, TP:T], mx[0:TS, 3, 0:TS], dt_[0:TS, TP:T], ALU.mult), "aqk")
            e_pe.wait(dve, i, "tk")
            nc.vector.tensor_tensor(kd[:, 0:NC, :], chunks(mx[:, 0, :]),
                                    kdec[:, 0:NC, ds(i, 1)].to_broadcast([P, NC, P]), ALU.mult)
            step(nc.vector.tensor_tensor(kd[0:TS, NC, :], mx[0:TS, 1, 0:P],
                                         kdec[0:TS, NC, ds(i, 1)].to_broadcast([TS, P]), ALU.mult), "kd")
            e_pe.wait(dve, i, "tv")
            nc.vector.tensor_tensor(vb[:, 0:NC, :], chunks(mx[:, 2, :]), bbc[:, 0:NC, :], ALU.mult)
            step(nc.vector.tensor_tensor(vb[0:TS, NC, :], mx[0:TS, 3, 0:P], bbc[0:TS, NC, :], ALU.mult), "vb")

            e_pe.wait(dve, i, "P1")
            e_pool.wait(dve, i, "b1")
            nc.vector.tensor_tensor(zi[0:TS, TP:T], ident[0:TS, 0:TS], mx[0:TS, 1, 0:TS], ALU.subtract)
            nc.vector.tensor_tensor(xi[0:TS, TP:T], ident[0:TS, 0:TS], bm[0:TS, 0, TP:T], ALU.subtract)
            e_dve.done(nc.vector.tensor_tensor(chunks(zi[:, 0:TP]), each_chunk(ident), chunks(mx[:, 0, :]),
                                               ALU.subtract), "z1")
            step(nc.vector.tensor_tensor(chunks(xi[:, 0:TP]), each_chunk(ident), chunks(bm[:, 0, 0:TP]),
                                         ALU.subtract), "x1")

            def inverse_step(s):
                e_pe.wait(dve, i, f"Q{s}")
                if s <= 4:
                    nc.vector.tensor_tensor(zi[0:TS, TP:T], zi[0:TS, TP:T], mx[0:TS, 1, TS:2 * TS], ALU.subtract)
                    nc.vector.tensor_tensor(xi[0:TS, TP:T], xi[0:TS, TP:T], mx[0:TS, 1, 2 * TS:3 * TS], ALU.subtract)
                e_dve.done(nc.vector.tensor_tensor(zi[:, 0:TP], zi[:, 0:TP], mx[:, 2, :], ALU.subtract), f"z{s}")
                if s < MASKS[-1]:
                    e_dve.done(nc.vector.tensor_tensor(xi[:, 0:TP], xi[:, 0:TP], mx[:, 3, :], ALU.subtract), f"x{s}")
                e_dve.wait(dve, i, f"x{s}" if s < MASKS[-1] else f"z{s}")

            for s in (2, 4, 8, 16):
                inverse_step(s)
            p = plan.pair("even", 5)
            dve.wait_ge(multiplied, plan.summed("even", i, 5))
            emptied(dve, "even", i, 4)
            nc.vector.tensor_copy(sample_pad(bufa, WA - 1, PADA)[:, :, 0:2],
                                  pre_a[:, ds(i, 1), :].rearrange("p a (b n) -> p (a b) n", n=2))
            nc.vector.tensor_tensor(bufa[:, WA - 1:WA - 1 + HALF], acc[:, p, 0, 0:HALF], gcs[:, 0:HALF], ALU.mult)
            nc.vector.tensor_tensor(bufa[:, WA - 1 + HALF:SA], acc[:, p, 1, 0:TP - HALF], gcs[:, HALF:TP], ALU.mult)
            nc.vector.tensor_tensor(sample_pad(bufa, WA - 1, PADA)[:, :, 2:], seqs(acc[:, p, 1, TP - HALF:HALF]),
                                    seqs(gcs[:, TP:T]), ALU.mult).then_inc(drained[p], 1)
            emptied(dve, "even", i, 5)
            nc.vector.tensor_copy(out_a[:, ds(i, 1), 0:2].rearrange("p a n -> p (a n)"), bufa[:, SA - 2:SA])
            nc.vector.tensor_copy(out_a[:, ds(i, 1), 2:].rearrange("p a (b n) -> p (a b) n", n=2),
                                  sample_pad(bufa, WA - 1, PADA)[:, :, LS:])
            step(nc.vector.tensor_scalar(ca1[:, 0:NA], bufa[:, 0:NA], w(12), None, ALU.mult), "ca0")
            step(nc.vector.scalar_tensor_tensor(out=ca2[:, 0:NA], in0=bufa[:, 1:1 + NA], scalar=w(13), in1=ca1[:, 0:NA],
                                                op0=ALU.mult, op1=ALU.add), "ca1")
            nc.vector.scalar_tensor_tensor(out=cs[:, 0:TP], in0=bufa[:, 2:2 + TP], scalar=w(14), in1=ca2[:, 0:TP],
                                           op0=ALU.mult, op1=ALU.add)
            step(nc.vector.scalar_tensor_tensor(out=seqs(cs[:, TP:T]), in0=sample_pad(bufa, WA - 1, PADA)[:, :, 2:],
                                                scalar=w(14), in1=outputs_at(ca2, SA, LS + WA - 1), op0=ALU.mult,
                                                op1=ALU.add), "ca2")
            inverse_step(32)
            inverse_step(64)
            p = plan.pair("even", 6)
            dve.wait_ge(multiplied, plan.summed("even", i, 6))
            nc.vector.tensor_tensor(halves(ca1[:, 0:T]), pair_view(p), halves(cs[:, :]), ALU.mult)\
                .then_inc(drained[p], 1)

            state_in_wait(dve, i)
            e_pe.wait(dve, i, "S0")
            step(nc.vector.tensor_copy(s_p[:, :], mx[:, 0, 0:P]), "s0")
            for c in range(1, NC):
                e_pe.wait(dve, i, f"R{c}")
                step(nc.vector.tensor_tensor(rr[:, :], vb[:, c, :], mx[:, 1, 0:P], ALU.subtract), f"rr{c}")
                if c == 1:
                    e_pe.wait(dve, i, "Rs")
                    step(nc.vector.tensor_tensor(rs_[0:TS, :], vb[0:TS, NC, :], mx[0:TS, 2, 0:P],
                                                 ALU.subtract), "rs")
                e_pe.wait(dve, i, f"S{c}")
                step(nc.vector.scalar_tensor_tensor(out=s_p[:, :], in0=s_p[:, :],
                                                    scalar=eg[:, (c + 1) * P - 1:(c + 1) * P], in1=mx[:, 0, 0:P],
                                                    op0=ALU.mult, op1=ALU.add), f"s{c}")
            e_act.wait(dve, i, "yah")
            step(nc.vector.tensor_tensor(yl[:, 0, :], ca1[:, 0:T], yh[:, 0, :].bitcast(F32), ALU.subtract), "yal")
            e_pe.wait(dve, i, "os")
            step(nc.vector.tensor_copy(oT[:, TP:T], mx[:, 2, 256:256 + TS]), "oT_s")
            e_pe.wait(dve, i, f"o{NC - 1}")
            step(nc.vector.tensor_copy(oT[:, 0:TP], mx[:, 3, :]), "oT_p")
            step(nc.vector.tensor_tensor(s_s[:, :, :], s_s[:, :, :],
                                         seqs(eg[:, TP:T])[:, :, LS - 1:LS].to_broadcast([P, NB, P]), ALU.mult), "s_dec")
            e_pe.wait(dve, i, "Ss")
            step(nc.vector.tensor_tensor(s_s[:, :, :].rearrange("p (a b) n -> p a (b n)", a=2),
                                         s_s[:, :, :].rearrange("p (a b) n -> p a (b n)", a=2), mx[:, 2:4, :],
                                         ALU.add), "s_new")
            e_act.wait(dve, i, "o_inv")
            step(nc.vector.scalar_tensor_tensor(out=yf[:, :], in0=oT[:, :], scalar=cols[:, COL_DN:COL_DN + 1],
                                                in1=std[:, :], op0=ALU.mult, op1=ALU.mult), "on")
            emptied(dve, "even", i, 3)
            step(nc.vector.tensor_tensor(yf[:, :], yf[:, :], zs[:, :], ALU.mult), "yb")
            e_act.wait(dve, i, "ybh")
            step(nc.vector.tensor_tensor(yl[:, 1, :], yf[:, :], yh[:, 1, :].bitcast(F32), ALU.subtract), "ybl")
            for m in range(KT):
                add_to_x(dve, "even", i, 7 + m, m)

        @block_.vector
        def _(dve):
            nc.vector.memset(eps[:, 0:1], EPS)
            nc.vector.memset(eps[:, 1:2], GN_EPS).then_inc(s_eps, 1)
            dve.wait_ge(s_setup_t, 1)
            nc.vector.tensor_copy(cols[:, :], mx[:, 0, 0:ROWS_1 + ROWS_2])
            nc.vector.tensor_copy(pre_a[:, :, :].rearrange("p t n -> p (t n)"), mx[:, 1, 0:4 * 2 * NB])
            nc.vector.tensor_copy(pre_q[:, :, :, :].rearrange("p k t n -> p (k t n)"), mx[:, 2, 0:12 * 3 * NB])\
                .then_inc(s_setup_c, 1)
            for t in range(0, KT, 2):
                dve.wait_ge(multiplied, plan.summed("x", 0, t))
                nc.vector.tensor_copy(x[:, t, 0:TP], acc[:, 0, 0, :])
                nc.vector.tensor_copy(x[:, t, TP:T], acc[:, 0, 1, 0:TS]).then_inc(drained[0], 1)
            dve.wait_ge(s_setup_c, 1)
            norm_vector(dve, 0)

            def step(ins, name):
                a_dve.done(ins, name)
                a_dve.wait(dve, 0, name)

            step(nc.vector.memset(gate[:, :, :], 0.0), "zero")
            a_pe.wait(dve, 0, "ab_t")
            nc.vector.tensor_copy(gate[:, 0:NC, :], chunks(mx[:, 0, :])[:, :, P - 8:P])
            step(nc.vector.tensor_copy(gate[0:TS, NC, :], mx[0:TS, 1, P - 8:P]), "gate")
            dve.wait_ge(s_gp, 32)
            step(nc.vector.tensor_tensor(g_sp[:, :, :], gate[:, :, 0:DN_H],
                                         dtb[:, :].unsqueeze(1).to_broadcast([P, NC + 1, DN_H]), ALU.add), "sum")
            step(nc.vector.tensor_copy(g_ab[:, :, :], g_sp[:, :, :]), "ad")
            step(nc.vector.tensor_scalar(g_rl[:, :, :], g_sp[:, :, :], 0.0, None, ALU.max), "relu")
            a_act.wait(dve, 0, "ln")
            step(nc.vector.tensor_tensor(g_rl[:, :, :], g_rl[:, :, :], g_ab[:, :, :], ALU.add), "softplus")
            step(nc.vector.tensor_scalar(nega[:, :], nega[:, :], -1.0, None, ALU.mult), "neg")
            step(nc.vector.tensor_tensor(g_g[:, :, :], g_rl[:, :, :],
                                         nega[:, :].unsqueeze(1).to_broadcast([P, NC + 1, DN_H]), ALU.mult), "g")
            a_pe.wait(dve, 0, "gcum")
            nc.vector.memset(gcum[:, NC, :], 0.0)
            nc.vector.tensor_copy(gcum[:, 0:NC, :], mx[:, 2, 0:NC * DN_H].rearrange("p (c h) -> p c h", h=DN_H))
            a_dve.done(nc.vector.memset(bufa[:, 0:2], 0.0), "gc0")
            a_dve.wait(dve, 0, "gc0")
            nc.vector.tensor_copy(gcum[0:TS, NC, :], mx[0:TS, 2, 16:16 + DN_H])
            nc.vector.memset(km[:, :], 0.0)
            a_dve.done(nc.vector.memset(cbuf[:, 0:3], 0.0), "gc")
            a_dve.wait(dve, 0, "gc")
            a_act.wait(dve, 0, "kdec")
            with dve.Fori(0, DN_H) as i:
                even_vector(dve, i)
            for n in range(4):
                dve.wait_ge(rows_turned, n + 1)
                r = 2 + 2 * NB if n == 0 else 3 + 3 * NB
                nc.vector.tensor_copy(out_rows[0:r, n, :], mx[0:r, n, :]).then_inc(rows_copied, 1)
            norm_vector(dve, 1)
            ffn_vector(dve, 0)
            norm_vector(dve, 2)
            with dve.Fori(0, RET_H) as i:
                odd_vector(dve, i)
            norm_vector(dve, 3)
            ffn_vector(dve, 1)
            norm_vector(dve, 4, last=True)
            for c in range(0, NC + 1, 2):
                dve.wait_ge(multiplied, plan.summed("y", 0, c))
                if c:
                    dve.wait_ge(y_sent[0], 16 * (c // 2))
                    dve.wait_ge(y_row, c)
                n = P if c < NC else TS
                nc.vector.tensor_copy(y_out[0:n, 0, :].rearrange("p (a n) -> p a n", a=2), acc[0:n, 0, :, :])\
                    .then_inc(y_row, 1)

        def even_tensor(pe, i):
            def mm(out, lhs, rhs, start=True, stop=True):
                return nc.tensor.matmul(out, lhs, rhs, start=start, stop=stop)

            def by_chunk(bank, lhs, rhs):
                for c in range(NC):
                    ins = mm(mx[:, bank, c * P:(c + 1) * P], lhs(c), rhs(c))
                return ins

            def at(a, c):
                return a[:, c * P:(c + 1) * P]

            def squares(b, name):
                for h in range(2):
                    ins = mm(mx[:, b + h, 0:HALF], ones, sq[:, h * HALF:(h + 1) * HALF])
                e_pe.done(ins, name)

            def U(j, a=0, b=KT, wait_norm=None):
                unit(pe, "even", i, j, j, a, b, wait_norm)

            def level_p(s):
                b = MASKS.index(s) % 2
                e_pool.wait(pe, i, f"b{s}")
                if s == 1:
                    e_dve.wait(pe, i, "kd")
                    by_chunk(0, lambda c: bm[:, b, c * P:(c + 1) * P], lambda c: ident)
                    e_pe.done(mm(mx[0:TS, 1, 0:TS], bm[0:TS, b, TP:T], ident[0:TS, 0:TS]), "P1")
                    return
                e_dve.wait(pe, i, f"x{s // 2}")
                ins = by_chunk(0, lambda c: bm[:, b, c * P:(c + 1) * P], lambda c: at(zi, c))
                if s <= 4:
                    ins = mm(mx[0:TS, 1, 0:TS], bm[0:TS, b, TP:T], zi[0:TS, TP:T])
                e_pe.done(ins, f"P{s}")

            def level_q(s):
                e_act.wait(pe, i, f"p{s}")
                if s == 2:
                    e_dve.wait(pe, i, "vb")
                ins = by_chunk(2, lambda c: at(xi, c), lambda c: at(pp, c))
                if s < MASKS[-1]:
                    ins = by_chunk(3, lambda c: at(pp, c), lambda c: at(xi, c))
                if s <= 4:
                    mm(mx[0:TS, 1, TS:2 * TS], xi[0:TS, TP:T], pp[0:TS, TP:T])
                    ins = mm(mx[0:TS, 1, 2 * TS:3 * TS], pp[0:TS, TP:T], xi[0:TS, TP:T])
                e_pe.done(ins, f"Q{s}")

            U(0, wait_norm=0)
            e_dve.wait(pe, i, "gbc")
            by_chunk(0, lambda c: gbc[:, c, :], lambda c: tri)
            mm(mx[:, 1, 0:TS], gbc[0:TS, NC, :], tri_s)
            by_chunk(2, lambda c: bbc[:, c, :], lambda c: ident)
            e_pe.done(mm(mx[:, 1, TS:2 * TS], bbc[0:TS, NC, :], ident[0:TS, 0:TS]), "rows")
            U(1)
            e_act.wait(pe, i, "k_sq")
            e_dve.wait(pe, i, "bg")
            squares(0, "l2k")
            U(2, 0, 4)
            e_act.wait(pe, i, "q_sq")
            squares(2, "l2q")
            U(2, 4, 8)
            e_dve.wait(pe, i, "kT")
            by_chunk(0, lambda c: at(kT, c), lambda c: at(kT, c))
            e_pe.done(mm(mx[0:TS, 1, 0:TS], kT[:, TP:T], kT[:, TP:T]), "kk")
            U(3, 0, 2)
            e_dve.wait(pe, i, "qT")
            mm(mx[0:TS, 3, 0:TS], kT[:, TP:T], qT[:, TP:T])
            e_pe.done(by_chunk(2, lambda c: at(kT, c), lambda c: at(qT, c)), "kq")
            U(3, 2, 4)
            e_dve.wait(pe, i, "A")
            for c in range(NC):
                nc.tensor.transpose(mx[:, 0, c * P:(c + 1) * P], at(kT, c), ident)
            e_pe.done(nc.tensor.transpose(mx[0:TS, 1, 0:P], kT[:, TP:T], ident), "tk")
            U(3, 4, 6)
            e_act.wait(pe, i, "vs")
            e_dve.wait(pe, i, "aqk")
            for c in range(NC):
                nc.tensor.transpose(mx[:, 2, c * P:(c + 1) * P], at(vs, c), ident)
            e_pe.done(nc.tensor.transpose(mx[0:TS, 3, 0:P], vs[:, TP:T], ident), "tv")
            U(3, 6, 8)
            level_p(1)
            for j, pair in ((4, (2, 4)), (5, (8, 16)), (6, (32, 64))):
                for t, s in enumerate(pair):
                    U(j, 4 * t, 4 * t + 2)
                    level_p(s)
                    U(j, 4 * t + 2, 4 * t + 4)
                    level_q(s)
            e_dve.wait(pe, i, "z64")
            e_pe.done(mm(mx[:, 1, 256:384], at(zi, 0), vb[:, 0, :]), "u0")
            state_in_wait(pe, i)
            e_dve.wait(pe, i, "km")
            for b in range(NB):
                ins = mm(mx[0:TS, 2, 0:P], km[:, b * TS:(b + 1) * TS], s_s[:, b, :], b == 0, b == NB - 1)
            e_pe.done(ins, "Rs")
            e_act.wait(pe, i, "uu0")
            e_pe.done(mm(mx[:, 0, 0:P], kd[:, 0, :], uu[:, :]), "S0")
            e_pe.done(mm(mx[:, 3, 0:P], uu[:, :], at(dt_, 0)), "o0")
            for c in range(1, NC):
                e_dve.wait(pe, i, f"s{c - 1}")
                e_pe.done(mm(mx[:, 1, 0:P], at(kbg, c), s_p[:, :]), f"R{c}")
                mm(mx[:, 3, c * P:(c + 1) * P], s_p[:, :], at(qg, c), True, False)
                e_dve.wait(pe, i, f"rr{c}")
                e_pe.done(mm(mx[:, 1, 256:384], at(zi, c), rr[:, :]), f"u{c}")
                if c == 2:
                            e_pe.done(mm(mx[0:TS, 2, P:2 * P], zi[0:TS, TP:T], rs_[0:TS, :]), "us")
                e_act.wait(pe, i, f"uu{c}")
                e_pe.done(mm(mx[:, 0, 0:P], kd[:, c, :], uu[:, :]), f"S{c}")
                e_pe.done(mm(mx[:, 3, c * P:(c + 1) * P], uu[:, :], at(dt_, c), False, True), f"o{c}")
            e_act.wait(pe, i, "us_")
            mm(mx[:, 2, 256:256 + TS], us_[0:TS, :], dt_[0:TS, TP:T], True, False)
            for b in range(NB):
                c = TP + b * LS
                ins = mm(mx[:, 2, 256 + b * LS:256 + (b + 1) * LS], s_s[:, b, :], qg[:, c:c + LS], False, b == NB - 1)
            e_pe.done(ins, "os")
            e_act.wait(pe, i, "o_sq")
            e_dve.wait(pe, i, f"s{NC - 1}")
            squares(0, "onorm")
            e_pool.wait(pe, i, "um")
            for h in range(2):
                ins = mm(mx[:, 2 + h, :], kd[0:TS, NC, :], um[0:TS, 4 * h:4 * h + 4, :])
            e_pe.done(ins, "Ss")
            e_dve.wait(pe, i, "ybl")
            for j in range(2):
                rows_unit(pe, "even", i, 7 + j, 7 + 4 * j, yh, yl)

        @block_.tensor
        def _(pe):
            pe.wait_ge(s_every, 16)
            pe.wait_ge(s_par, 16 * 8)
            nc.tensor.transpose(mx[:, 0, 0:ROWS_1], rows_1[0:ROWS_1, :], ident[0:ROWS_1, 0:ROWS_1])
            nc.tensor.transpose(mx[:, 0, ROWS_1:ROWS_1 + ROWS_2], rows_2[0:ROWS_2, :], ident[0:ROWS_2, 0:ROWS_2])
            pe.wait_ge(s_a, 16)
            pe.wait_ge(s_q, 16)
            for t in range(4):
                n = 2 * NB
                nc.tensor.transpose(mx[:, 1, t * n:(t + 1) * n], rows_a[0:n, t * P:(t + 1) * P], ident[0:n, 0:n])
            for t in range(12):
                n = 3 * NB
                ins = nc.tensor.transpose(mx[:, 2, t * n:(t + 1) * n], rows_q[0:n, t * P:(t + 1) * P], ident[0:n, 0:n])
            ins.then_inc(s_setup_t, 1)
            pe.wait_ge(s_in, 32)
            for t in range(KT):
                p = t % 2
                if t >= 2:
                    pe.wait_ge(drained[p], plan.drained("x", 0, t))
                for c in range(NC):
                    nc.tensor.transpose(acc[:, p, 0, c * P:(c + 1) * P], x_in[:, c, t * P:(t + 1) * P], ident)
                nc.tensor.transpose(acc[:, p, 1, 0:TS], x_in[0:TS, NC, t * P:(t + 1) * P], ident[0:TS, 0:TS])\
                    .then_inc(multiplied, 1)
            pe.wait_ge(s_setup_c, 1)
            norm_sum(pe, 0)
            unit(pe, "ab", 0, 0, 0, wait_norm=0)
            emptied(pe, "ab", 0, 0)
            for c in range(NC):
                nc.tensor.transpose(mx[:, 0, c * P:(c + 1) * P], yf[:, c * P:(c + 1) * P], ident)
            a_pe.done(nc.tensor.transpose(mx[0:TS, 1, 0:P], yf[:, TP:T], ident), "ab_t")
            a_dve.wait(pe, 0, "g")
            pe.wait_ge(s_ce, 16)
            for bank, m, m_s in ((2, tri, tri_s), (3, low, low_s)):
                nc.tensor.matmul(mx[:, bank, 0:16], m, g_g[:, 0:NC, :].rearrange("p c h -> p (c h)"), start=True,
                                 stop=True)
                ins = nc.tensor.matmul(mx[0:TS, bank, 16:20], m_s, g_g[0:TS, NC, :], start=True, stop=True)
            a_pe.done(ins, "gcum")
            with pe.Fori(0, DN_H) as i:
                even_tensor(pe, i)
            for t in range(4):
                ins = nc.tensor.transpose(mx[0:18, 0, t * P:(t + 1) * P], out_a[:, t, :], ident)
            ins.then_inc(rows_turned, 1)
            for kind in range(3):
                for t in range(4):
                    ins = nc.tensor.transpose(mx[0:27, 1 + kind, t * P:(t + 1) * P], out_q[:, kind, t, :], ident)
                ins.then_inc(rows_turned, 1)
            pe.wait_ge(rows_copied, 4)
            norm_sum(pe, 1)
            ffn_tensor(pe, 0)
            norm_sum(pe, 2)
            with pe.Fori(0, RET_H) as i:
                odd_tensor(pe, i)
            norm_sum(pe, 3)
            ffn_tensor(pe, 1)
            norm_sum(pe, 4)
            for c in range(NC + 1):
                p = c % 2
                n = P if c < NC else TS
                pe.wait_ge(drained[p], plan.drained("y", 0, c)) if c < 2 else pe.wait_ge(y_row, c - 1)
                for t in range(KT):
                    pe.wait_ge(y_norm, t + 1)
                    ins = nc.tensor.transpose(acc[0:n, p, t // 4, (t % 4) * P:(t % 4 + 1) * P],
                                              yT[:, t, c * P:c * P + n], ident)
                ins.then_inc(multiplied, 1)

        def even_gpsimd(pool, i):
            def mask(s):
                n = MASKS.index(s)
                if n >= 2:
                    e_pe.wait(pool, i, f"P{MASKS[n - 2]}")
                else:
                    e_dve.wait(pool, i, "A")
                if n >= 2:
                    e_dve.wait(pool, i, "x1")
                if s <= 4:
                    nc.gpsimd.tensor_tensor(bm[0:TS, n % 2, TP:T], dm[0:TS, TP:T], level[n][0:TS, 0:TS], ALU.mult)
                e_pool.done(nc.gpsimd.tensor_tensor(chunks(bm[:, n % 2, 0:TP]), chunks(dm[:, 0:TP]),
                                                    each_chunk(level[n]), ALU.mult), f"b{s}")

            for j in range(4):
                split_lo(pool, "even", i, j)
            e_act.wait(pool, i, "dt")
            nc.gpsimd.tensor_tensor(dt_[0:TS, TP:T], dt_[0:TS, TP:T], tri_s, ALU.mult)
            e_pool.done(nc.gpsimd.tensor_tensor(chunks(dt_[:, 0:TP]), chunks(dt_[:, 0:TP]), each_chunk(tri), ALU.mult),
                        "dtm")
            split_lo(pool, "even", i, 4)
            mask(1)
            mask(2)
            split_lo(pool, "even", i, 5)
            mask(4)
            mask(8)
            split_lo(pool, "even", i, 6)
            mask(16)
            mask(32)
            split_lo(pool, "even", i, 7)
            mask(64)
            e_act.wait(pool, i, "us_")
            e_pool.done(nc.gpsimd.tensor_tensor(um[0:TS, :, :], us_[0:TS, :].unsqueeze(1).to_broadcast([TS, NB, P]),
                                                block[0:TS, :].unsqueeze(2).to_broadcast([TS, NB, P]), ALU.mult), "um")
            split_lo(pool, "even", i, 8)

        @block_.gpsimd
        def _(pool):
            for n, free in enumerate((w_ready,) * RAW_LAG + (state_free, ret_free)):
                nc.gpsimd.memset(spare[:, n:n + 1], 0.0).then_inc(free, 1)
            split_lo(pool, "ab", 0, 0)
            norm_gpsimd(pool, 0)
            pool.wait_ge(s_ce, 16)
            with pool.Fori(0, DN_H) as i:
                even_gpsimd(pool, i)
            norm_gpsimd(pool, 1)
            ffn_gpsimd(pool, 0)
            norm_gpsimd(pool, 2)
            with pool.Fori(0, RET_H) as i:
                odd_gpsimd(pool, i)
            norm_gpsimd(pool, 3)
            ffn_gpsimd(pool, 1)
            norm_gpsimd(pool, 4, last=True)


_INS = ["x_prompt", "x_sample", "state_conv_a", "state_conv_qkv", "state_delta", "state_ret", "norm_mix", "norm_ffn",
        "final_norm", "even_w_in", "even_conv_a", "even_conv_qkv", "even_a_log", "even_dt_bias", "even_dn_norm",
        "even_w_out", "odd_w_in", "odd_gn_g", "odd_gn_b", "odd_w_out", "ffn_w_gate", "ffn_w_up", "ffn_w_down"]
_OUTS = [(1, TP, D), (NB, LS, D), (1, 1, WA - 1, CA), (1, 1, WQ - 1, 3 * CA), (1, 1, DN_H, DN_D, DN_D),
         (1, 1, RET_H, P, RET_V), (1, NB, WA - 1, CA), (1, NB, WQ - 1, 3 * CA), (1, NB, DN_H, DN_D, DN_D),
         (1, NB, RET_H, P, RET_V)]


def kernel(**inputs):
    import concourse.bacc as _bacc
    from concourse.bass_utils import run_bass_kernel_spmd as _run

    nc = _bacc.Bacc("TRN2", target_bir_lowering=False, num_devices=1)
    arrays, args = {}, []
    for name in _INS:
        arrays[f"in_{name}"] = np.ascontiguousarray(inputs[name])
    for name, a in constants().items():
        arrays[f"const_{name}"] = a
    for name, a in arrays.items():
        args.append(nc.dram_tensor(name, a.shape, mybir.dt.from_np(a.dtype), kind="ExternalInput").ap())
    for n, shape in enumerate(_OUTS):
        args.append(nc.dram_tensor(f"out_{n}", shape, F32, kind="ExternalOutput").ap())
    build(nc, *args)
    r = _run(nc, [arrays], core_ids=[0])
    return tuple(r.results[0][f"out_{n}"] for n in range(len(_OUTS)))
```

```python
from contextlib import ExitStack

import numpy as np

import concourse.bass as bass
from concourse import mybir

F32 = mybir.dt.float32
F32R = mybir.dt.float32r
ALU = mybir.AluOpType
ACT = mybir.ActivationFunctionType
ds = bass.ds

P = 128
D = 1024
KT = D // P
TP = 512
NB, LS = 8, 8
TS = NB * LS
T = TP + TS
HALF = T // 2
NC = TP // P
CA = D // 2
DN_H, DN_D = 4, 128
RET_H, RET_V = 8, 256
EVEN_IN = 3 * CA + 4 * DN_H * DN_D + 2 * DN_H
ODD_IN = 6 * D
FF = 2816
FT = FF // P
PAST = 4096
WA, WQ = 3, 4
EPS, GN_EPS = 1e-6, 1e-5
ROPE_BASE = 10000.0
PADA = WA - 1 + TP + NB * (LS + WA - 1)
PADQ = WQ - 1 + TP + NB * (LS + WQ - 1)
NA, NQ = PADA - (WA - 1), PADQ - (WQ - 1)
SA, SQ = WA - 1 + TP, WQ - 1 + TP

PHASES = {
    "x": (1, (), (), (0, 1) * 4),
    "ab": (1, (3,), (2,), (1,)),
    "even_kq": (1, (0, 1), (0, 1), (0, 1)),
    "even": (DN_H - 1, (2, 0, 1) * 3, (2, 0, 1) * 3, (0, 1, 0, 1, 0, 0, 1) + (0, 1) * 4),
    "even_end": (1, (2, 0, 1, 2, 0, 1, 2), (2, 0, 1, 2, 0, 1, 2), (0, 1, 0, 1, 0) + (1, 0) * 4),
    "up0": (FT // 2, (0, 1, 2, 3), (0, 1, 0, 1), (0, 1, 0, 1)),
    "down0": (KT // 2, (0, 1, 2) * 2, (0, 1, 2) * 2, (0, 1)),
    "odd_kq": (1, (0, 1), (0, 1), (0, 1)),
    "odd": (RET_H - 1, (2, 3, 0, 1) * 2, (2, 0, 1, 2, 0, 1, 2, 0), (0, 1) * 7),
    "odd_end": (1, (2, 3, 0, 1, 2, 3), (2, 0, 1, 2, 0, 1), (0, 1) * 6),
    "up1": (FT // 2, (0, 1, 2, 3), (0, 1, 0, 1), (0, 1, 0, 1)),
    "down1": (KT // 2, (0, 1, 2) * 2, (0, 1, 2) * 2, (0, 1)),
    "y": (1, (), (), (0, 1, 0, 1, 0)),
}
PLAIN = {"even": 7, "even_end": 5, "odd": 6, "odd_end": 4}
DOWN = (8, 8, FT - 16)
FIRST = (2, 0, 1)
RAW_LAG, SPLIT_LAG = 3, 2


class Plan:

    def __init__(self):
        self.unit0, self.mark0, self.raw0, self.pair0 = {}, {}, {}, {}
        units, marks, raws, pairs = 0, 0, [0] * 4, [0] * 2
        seen_raw, seen_split, self.ends = [], [], []
        for name, (count, raw, split, pair) in PHASES.items():
            self.unit0[name], self.mark0[name] = units, marks
            self.raw0[name], self.pair0[name] = list(raws), list(pairs)
            for i in range(count):
                self.ends += [marks + i * self.marks(name) + self.unit_mark(name, j) + 1 for j in range(len(raw))]
            units += count * len(raw)
            marks += count * self.marks(name)
            raws = [n + count * raw.count(s) for s, n in enumerate(raws)]
            pairs = [n + count * pair.count(s) for s, n in enumerate(pairs)]
            seen_raw += list(raw) * count
            seen_split += list(split) * count
        self.slots = seen_split
        assert tuple(seen_split[:len(FIRST)]) == FIRST
        for seen, lag in ((seen_raw, RAW_LAG), (seen_split, SPLIT_LAG)):
            assert all(len(set(seen[n:n + lag])) == len(seen[n:n + lag]) for n in range(len(seen)))

    def marks(self, phase):
        _, raw, _, pair = PHASES[phase]
        return len(raw) if phase[:4] == "down" else len(pair)

    def unit_mark(self, phase, j):
        plain = PLAIN.get(phase, 99)
        return j if j < plain else plain + 4 * (j - plain) + 3

    def sum_mark(self, phase, n):
        return 3 * n + 2 if phase[:4] == "down" else n

    def split_free(self, phase, i, j, again=False):
        k = j - SPLIT_LAG
        if k >= 0:
            return self.mark0[phase] + i * self.marks(phase) + self.unit_mark(phase, k) + 1
        if self.unit0[phase] + j < len(FIRST):
            return 1
        back = self.mark0[phase] - self.ends[self.unit0[phase] + k]
        if PHASES[phase][0] > 1:
            inside = self.marks(phase) - 1 - self.unit_mark(phase, k + len(PHASES[phase][1]))
            back = inside if again else min(back, inside)
        return self.mark0[phase] + i * self.marks(phase) - back

    def first_free(self, phase):
        n = self.unit0[phase]
        assert self.slots[n] == self.slots[n - 3] and self.slots[n] not in self.slots[n - 2:n]
        return self.ends[n - 3]

    def unit(self, phase, i, j):
        return self.unit0[phase] + i * len(PHASES[phase][1]) + j

    def landed(self, phase, i, j):
        raw = PHASES[phase][1]
        s = raw[j]
        return s, (i * raw.count(s) + self.raw0[phase][s] + raw[:j + 1].count(s)) * 16

    def split_slot(self, phase, j):
        return PHASES[phase][2][j]

    def summed(self, phase, i, n):
        return self.mark0[phase] + i * self.marks(phase) + self.sum_mark(phase, n) + 1

    def pair(self, phase, n):
        return PHASES[phase][3][n]

    def drained(self, phase, i, n):
        pair = PHASES[phase][3]
        return i * pair.count(pair[n]) + self.pair0[phase][pair[n]] + pair[:n].count(pair[n])


class Steps:

    def __init__(self, sem, names):
        self.sem, self.names, self.at = sem, names, 0

    def done(self, ins, name):
        assert self.names[self.at % len(self.names)] == name, (name, self.names[self.at % len(self.names)])
        self.at += 1
        ins.then_inc(self.sem, 1)

    def wait(self, eng, i, name):
        eng.wait_ge(self.sem, i * len(self.names) + self.names.index(name) + 1)


MASKS = (1, 2, 4, 8, 16, 32, 64)


def constants():
    j, i = np.arange(P)[:, None], np.arange(P)[None, :]
    same = (j // LS == i // LS)[:TS, :TS]

    def padded(a):
        return np.pad(a, ((0, P - a.shape[0]), (0, 0)))

    ident, ones = (i == j), np.ones((P, P))
    block = padded(np.arange(TS)[:, None] // LS == np.arange(NB)[None, :])
    every = np.concatenate([ident, ones, block], axis=1)
    tri, low = j <= i, j > i
    levels = [(j // (2 * s) == i // (2 * s)) & (j // s % 2 == 1) & (i // s % 2 == 0) for s in MASKS]
    even = np.concatenate([tri, low, padded(tri[:TS, :TS] & same), padded(low[:TS, :TS] & same), *levels], axis=1)
    pos = np.concatenate([np.arange(TP), np.tile(PAST + np.arange(LS), NB)]).astype(np.float32)
    inv = (ROPE_BASE ** (-np.arange(P // 2) / (P // 2))).astype(np.float32)
    ang = (inv[:, None] * pos[None, :]).astype(np.float32).astype(np.float64)
    odd = np.concatenate([np.tile(np.cos(ang), (2, 1)), np.concatenate([-np.sin(ang), np.sin(ang)])], axis=1)
    heads = []
    for h in range(RET_H):
        gamma = 1.0 - 2.0 ** (-5.0 - h)
        att = np.where(j <= i, gamma ** np.maximum(i - j, 0), 0.0)
        att_s = padded(att[:TS, :TS] * same)
        inner = np.tile(gamma ** (np.arange(P) + 1.0), (P, 1))
        inner_s = np.tile(gamma ** (np.arange(TS) % LS + 1.0), (P, 1))
        kdec = gamma ** (P - 1.0 - np.arange(P))[:, None]
        kdec_s = gamma ** (LS - 1.0 - np.arange(P) % LS)[:, None]
        cdec = np.tile([[gamma ** float(P), gamma ** float(LS)]], (P, 1))
        heads.append(np.concatenate([att, att_s, inner, inner_s, kdec, kdec_s, cdec], axis=1))
    return {"every": every.astype(np.float32), "even": even.astype(np.float32), "odd": odd.astype(np.float32),
            "heads": np.stack(heads).astype(np.float32)}


COL_NORM = (0, 16, 8, 24, 32)
COL_GN_G, COL_GN_B = 40, 56
ROWS_1 = 72
COL_CONV_A, COL_CONV_Q, COL_DN = ROWS_1, ROWS_1 + WA * 4, ROWS_1 + WA * 4 + WQ * 12
ROWS_2 = WA * 4 + WQ * 12 + 1

_LATER = tuple(s for s in MASKS if s > 1)
A_PE = ("ab_t", "gcum")
A_ACT = ("abs", "exp", "nega", "ln", "beta", "kdec")
A_DVE = ("zero", "gate", "sum", "ad", "relu", "softplus", "neg", "g", "gc0", "gc")
E_PE = ("rows", "l2k", "kk", "l2q", "tk", "kq", "tv", "P1", *(f"{a}{s}" for s in _LATER for a in "PQ"),
        "u0", "Rs", "S0", "o0", "R1", "u1", "S1", "o1", "R2", "u2", "us", "S2", "o2", "R3", "u3", "S3", "o3",
        "os", "onorm", "Ss")
E_ACT = ("gr", "eg", "ks", "k_sq", "dt_lo", "dm_lo", "k_ln", "k_inv", "dm", "dt", "qs", "q_sq", "vs", "q_ln", "q_inv",
         *(f"p{s}" for s in _LATER), "yah", "uu0", "uu1", "uu2", "us_", "uu3", "o_sq", "o_ln", "o_inv", "ybh")
E_DVE = ("pw", "gate", "pre_k", "ck0", "ck1", "ck2", "ck", "pre_v", "bg", "pre_q",
         "cq0", "cq1", "cq2", "cq", "cv0", "cv1", "cv2", "cv", "kT", "dmb", "A", "qT",
         "aqk", "kd", "vb", *(f"{a}{s}" for s in (1, 2, 4, 8, 16) for a in "zx"),
         "ca0", "ca1", "ca2", "z32", "x32", "z64", "s0", "rr1", "rs", "s1", "rr2", "s2", "rr3", "s3", "yal",
         "oT_s", "oT_p", "s_dec", "on", "yb", "ybl", "s_new")
E_POOL = ("df", "dtm", "b1", "b2", "kbg", "km", "b4", "b8", "qg", "b16", "b32", "b64", "um")
O_PE = ("att", "tk", "tv0", "tv1", "kv", "op", "os", "mean", "var", "kvs")
O_ACT = ("kdt", "v0", "v1", "osq", "oln", "oinv", "yh0", "yh1")
O_DVE = ("tk", "rk", "tq", "rq", "qg", "att", "r0", "r1", "r2", "r3", "of_p", "of_s", "o_both", "cen", "sq_both",
         "on0", "y0", "on1", "y1", "yl0", "yl1", "rs")
O_POOL = ("kdm",)


def build(nc, x_prompt, x_sample, state_conv_a, state_conv_qkv, state_delta, state_ret, norm_mix, norm_ffn,
          final_norm, even_w_in, even_conv_a, even_conv_qkv, even_a_log, even_dt_bias, even_dn_norm, even_w_out,
          odd_w_in, odd_gn_g, odd_gn_b, odd_w_out, ffn_w_gate, ffn_w_up, ffn_w_down,
          c_every, c_even, c_odd, c_heads,
          y_prompt, y_sample, conv_a_p, conv_qkv_p, delta_p, ret_p, conv_a_s, conv_qkv_s, delta_s, ret_s):
    plan = Plan()
    ctx = ExitStack()
    with ctx:
        def sb(stack, name, shape, dt=F32):
            return stack.enter_context(nc.sbuf_tensor(name, [P] + shape, dt))

        def sem(name):
            return ctx.enter_context(nc.semaphore(name))

        x = sb(ctx, "x", [KT, T])
        xn_hi = sb(ctx, "xn_hi", [KT, T], F32R)
        with ExitStack() as m:
            n_sq = sb(m, "n_sq", [2, T])
            n_ss = sb(m, "n_ss", [T])
        xn_lo = sb(ctx, "xn_lo", [KT, T], F32R)
        raw = sb(ctx, "raw", [4, KT * P])
        w_hi = sb(ctx, "w_hi", [3, KT * P], F32R)
        w_lo = sb(ctx, "w_lo", [3, KT * P], F32R)
        every = sb(ctx, "every", [2 * P + NB])
        cols = sb(ctx, "cols", [ROWS_1 + ROWS_2])
        eps = sb(ctx, "eps", [2])
        dtb, nega = sb(ctx, "dtb", [DN_H]), sb(ctx, "nega", [DN_H])
        spare = sb(ctx, "spare", [RAW_LAG + 2])
        ident, ones, block = every[:, 0:P], every[:, P:2 * P], every[:, 2 * P:2 * P + NB]
        acc = ctx.enter_context(nc.psum_tensor("acc", [P, 2, 2, 512], F32))
        mx = ctx.enter_context(nc.psum_tensor("mx", [P, 4, 512], F32))

        with ExitStack() as m:
            n_rs = sb(m, "n_rs", [T])
            n_xf = sb(m, "n_xf", [4, T])
            x_in = sb(m, "x_in", [NC + 1, D])
            rows_1 = sb(m, "rows_1", [P])
            rows_2 = sb(m, "rows_2", [P])
            rows_a = sb(m, "rows_a", [CA])
            rows_q = sb(m, "rows_q", [3 * CA])
        with ExitStack() as m:
            gate = sb(m, "gate", [NC + 1, 2 * DN_H])
            g_ab, g_sp, g_rl, g_g, g_beta = (sb(m, n, [NC + 1, DN_H]) for n in
                                             ("g_ab", "g_sp", "g_rl", "g_g", "g_beta"))
            gcum, kdec = sb(m, "gcum", [NC + 1, DN_H]), sb(m, "kdec", [NC + 1, DN_H])
            yf = sb(m, "yf", [T])
            gh, bh = sb(m, "gh", [NC + 1]), sb(m, "bh", [NC + 1])
            cbuf, cbq, ca1, ca2 = (sb(m, n, [PADQ]) for n in ("cbuf", "cbq", "ca1", "ca2"))
            cs = sb(m, "cs", [T])
            ks, qs, vs = sb(m, "ks", [T]), sb(m, "qs", [T]), sb(m, "vs", [T])
            sq, std = sb(m, "sq", [T]), sb(m, "std", [T])
            kT, qT, kbg, qg = sb(m, "kT", [T]), sb(m, "qT", [T]), sb(m, "kbg", [T]), sb(m, "qg", [T])
            gr, eg, bg = qs, sb(m, "eg", [T]), sb(m, "bg", [T])
            dm, dt_ = sb(m, "dm", [T]), sb(m, "dt", [T])
            zi, xi, pp = sb(m, "zi", [T]), sb(m, "xi", [T]), sb(m, "pp", [T])
            bm = sb(m, "bm", [2, T])
            kd, vb = sb(m, "kd", [NC + 1, P]), sb(m, "vb", [NC + 1, P])
            rr, uu, rs_, us_, s_p = (sb(m, n, [P]) for n in ("rr", "uu", "rs_", "us_", "s_p"))
            oT = sb(m, "oT", [T])
            km = sb(m, "km", [NB * (TS + LS)])
            um = sb(m, "um", [NB, P])
            s_s = sb(m, "s_s", [NB, P])
            zs, gcs, bufa = sb(m, "zs", [T]), sb(m, "gcs", [T]), sb(m, "bufa", [PADA])
            yh = sb(m, "yh", [2, T], F32R)
            yl = sb(m, "yl", [2, T], F32R)
            pw = sb(m, "pw", [16])
            pre_a, pre_q = sb(m, "pre_a", [4, 2 * NB]), sb(m, "pre_q", [3, 4, 3 * NB])
            out_a, out_q = sb(m, "out_a", [4, 2 + 2 * NB]), sb(m, "out_q", [3, 4, 3 + 3 * NB])
            out_rows = sb(m, "out_rows", [4, CA])
            ce = sb(m, "ce", [2 * P + 2 * TS + len(MASKS) * P])
        tri, low = ce[:, 0:P], ce[:, P:2 * P]
        tri_s, low_s = ce[0:TS, 2 * P:2 * P + TS], ce[0:TS, 2 * P + TS:2 * P + 2 * TS]
        level = [ce[:, 2 * P + 2 * TS + n * P:2 * P + 2 * TS + (n + 1) * P] for n in range(len(MASKS))]
        with ExitStack() as m:
            h_hi = sb(m, "h_hi", [FT, T], F32R)
            h_lo = sb(m, "h_lo", [FT, T], F32R)
            f_g = sb(m, "f_g", [T])
            f_h = sb(m, "f_h", [T])
        with ExitStack() as m:
            o_pad = sb(m, "o_pad", [5 * T])
            co = sb(m, "co", [2, T])
            ch = sb(m, "ch", [3 * P + 4])
            qa, qb, ka, kb = (sb(m, n, [T]) for n in ("qa", "qb", "ka", "kb"))
            t1, t2, rq, rk, rqg = (sb(m, n, [T]) for n in ("t1", "t2", "rq", "rk", "rqg"))
            va = sb(m, "va", [2, T])
            gs = sb(m, "gs", [2, T])
            vtok = sb(m, "vtok", [NC + 1, RET_V])
            kdt = sb(m, "kdt", [NC + 1, P])
            kdm = sb(m, "kdm", [NB, P])
            att = sb(m, "att", [T])
            gnw = sb(m, "gnw", [2, 2])
            rst = sb(m, "rst", [NC, RET_V])
            r_s = sb(m, "r_s", [NB, RET_V])
            of = sb(m, "of", [2, T])
            osq = sb(m, "osq", [2, T])
            both = sb(m, "both", [T])
            orv = sb(m, "orv", [T])
            oyh = sb(m, "oyh", [2, T], F32R)
            oyl = sb(m, "oyl", [2, T], F32R)
        with ExitStack() as m:
            y_pad = sb(m, "y_pad", [5 * T])
            yT = sb(m, "yT", [KT, T])
            y_out = sb(m, "y_out", [2, D])

        s_every, s_in, s_par, s_a, s_q, s_gp, s_ce = (sem(n) for n in (
            "every_in", "x_in_landed", "rows_in", "rows_a_in", "rows_q_in", "gate_params_in", "even_consts_in"))
        s_co, s_ch = sem("odd_consts_in"), sem("head_decays_in")
        raw_in = [sem(f"raw_in_{s}") for s in range(4)]
        hi_ready = sem("w_hi_ready")
        w_ready = sem("w_ready")
        multiplied = sem("multiplied")
        drained = [sem("drained_0"), sem("drained_1")]
        s_setup_t, s_setup_c = sem("setup_transposed"), sem("setup_copied")
        s_eps = sem("constants_set")
        q_sq, q_ss, q_sum, q_std, q_rs, q_xf, q_hi = (sem("norm_" + n) for n in (
            "squared", "added", "summed", "log", "inverse", "scaled", "hi"))
        q_lo = [sem("norm_lo_even"), sem("norm_lo_odd")]
        f_hi, f_lo = sem("ffn_hi"), sem("ffn_lo")
        state_in, state_free = sem("state_in"), sem("state_sent")
        ret_in, ret_free = sem("ret_in"), sem("ret_sent")
        rows_turned, rows_copied, rows_sent = sem("rows_turned"), sem("rows_copied"), sem("rows_sent")
        y_norm, y_row, y_sent = sem("y_normed"), sem("y_row_ready"), [sem("y_sent_0"), sem("y_sent_1")]

        e_pe, e_act, e_dve, e_pool = (Steps(sem("even_" + n), N) for n, N in (
            ("tensor", E_PE), ("scalar", E_ACT), ("vector", E_DVE), ("gpsimd", E_POOL)))
        a_pe, a_act, a_dve = (Steps(sem("gates_" + n), N) for n, N in (
            ("tensor", A_PE), ("scalar", A_ACT), ("vector", A_DVE)))
        o_pe, o_act, o_dve, o_pool = (Steps(sem("odd_" + n), N) for n, N in (
            ("tensor", O_PE), ("scalar", O_ACT), ("vector", O_DVE), ("gpsimd", O_POOL)))
        block_ = ctx.enter_context(nc.Block())

        def pair_view(p):
            return acc[:, p, :, 0:HALF]

        def halves(a):
            return a.rearrange("p (a n) -> p a n", a=2)

        def chunks(a):
            return a.rearrange("p (c n) -> p c n", n=P)

        def sample_pad(buf, pre, pad):
            return buf[:, pre + TP:pad].rearrange("p (b n) -> p b n", b=NB)

        def seqs(a):
            return a.rearrange("p (b n) -> p b n", b=NB)

        def emptied(eng, phase, i, n):
            eng.wait_ge(drained[plan.pair(phase, n)], plan.drained(phase, i, n) + 1)

        def outputs_at(buf, at, stride):
            return buf[:, at:at + NB * stride].rearrange("p (b n) -> p b n", b=NB)[:, :, 0:LS]

        def diagonal(buf):
            return buf[:, :].rearrange("p (b n) -> p b n", b=NB)[:, :, 0:LS]

        def each_chunk(a):
            return a.unsqueeze(1).to_broadcast([P, NC, P])

        def state_in_wait(eng, i):
            eng.wait_ge(state_in, 16 * (i + 1))

        def wcol(w, col, n=P):
            return w.rearrange("(k p) c -> p k c", p=P)[:, :, ds(col, n)]

        w_e, w_o, w_eo, w_oo = even_w_in[0], odd_w_in[0], even_w_out[0], odd_w_out[0]
        E_K, E_Q, E_UNITS = 4 * CA, 3 * CA, (5 * CA, 6 * CA, CA, 2 * CA, 0)
        O_K, O_Q, O_UNITS = D, 0, (2 * D, 2 * D + P, 4 * D, 4 * D + P)

        def load(sp, phase, i, j, dst, src, slots=1):
            s, _ = plan.landed(phase, i, j)
            if slots:
                sp.wait_ge(w_ready, plan.unit(phase, i, j) + slots)
            sp.dma_start(dst(raw[:, s, :]), src).then_inc(raw_in[s], 16)

        def by_kt(n=KT):
            return lambda r: r[:, 0:n * P].rearrange("p (k c) -> p k c", k=n)

        def two_rows(r):
            return r.rearrange("p (k c) -> p k c", k=2)

        def split_hi(act, phase, i, j, n=KT, again=False, first=False):
            s, there = plan.landed(phase, i, j)
            d = plan.split_slot(phase, j)
            act.wait_ge(raw_in[s], there)
            act.wait_ge(multiplied, plan.first_free(phase) if first else plan.split_free(phase, i, j, again))
            nc.scalar.activation(w_hi[:, d, 0:n * P], raw[:, s, 0:n * P], ACT.Copy).then_inc(hi_ready, 1)

        def split_lo(pool, phase, i, j, n=KT, again=False):
            s, d = plan.landed(phase, i, j)[0], plan.split_slot(phase, j)
            pool.wait_ge(hi_ready, plan.unit(phase, i, j) + 1)
            nc.gpsimd.tensor_tensor(w_lo[:, d, 0:n * P], raw[:, s, 0:n * P], w_hi[:, d, 0:n * P].bitcast(F32),
                                    ALU.subtract).then_inc(w_ready, 1)

        def product(pe, out, whi, wlo, mhi, mlo, first, last):
            for n, (w, mv) in enumerate(((whi, mhi), (whi, mlo), (wlo, mhi))):
                for h in range(2):
                    ins = nc.tensor.matmul(out[:, h, :], w, mv[:, h * HALF:(h + 1) * HALF],
                                           start=first and n == 0, stop=last and n == 2)
            return ins

        def unit(pe, phase, i, j, a=0, b=KT, wait_norm=None):
            d, p = plan.split_slot(phase, j), plan.pair(phase, j)
            if a == 0:
                pe.wait_ge(w_ready, plan.unit(phase, i, j) + 1 + RAW_LAG)
                pe.wait_ge(drained[p], plan.drained(phase, i, j))
            for k in range(a, b):
                hi, lo = w_hi[:, d, k * P:(k + 1) * P], w_lo[:, d, k * P:(k + 1) * P]
                if wait_norm is None:
                    ins = product(pe, pair_view(p), hi, lo, xn_hi[:, k, :], xn_lo[:, k, :], k == 0, k == KT - 1)
                    continue
                pe.wait_ge(q_hi, wait_norm * KT + k + 1)
                for n, (w, mv) in enumerate(((hi, xn_hi), (lo, xn_hi), (hi, xn_lo))):
                    if mv is xn_lo:
                        pe.wait_ge(q_lo[k % 2], (wait_norm * KT + k) // 2 + 1)
                    for half in range(2):
                        ins = nc.tensor.matmul(pair_view(p)[:, half, :], w, mv[:, k, half * HALF:(half + 1) * HALF],
                                               start=k == 0 and n == 0, stop=k == KT - 1 and n == 2)
            if b == KT:
                ins.then_inc(multiplied, 1)

        def two_units(pe, norm, one, other):
            for k in range(KT):
                for phase, j in (one, other):
                    unit(pe, phase, 0, j, k, k + 1, wait_norm=norm)

        def rows_unit(pe, phase, i, j, base, src_hi, src_lo):
            d = plan.split_slot(phase, j)
            pe.wait_ge(w_ready, plan.unit(phase, i, j) + 1 + RAW_LAG)
            for mb in range(4):
                p = plan.pair(phase, base + mb)
                pe.wait_ge(drained[p], plan.drained(phase, i, base + mb))
                for k in range(2):
                    c = (4 * k + mb) * P
                    ins = product(pe, pair_view(p), w_hi[:, d, c:c + P], w_lo[:, d, c:c + P],
                                  src_hi[:, k, :], src_lo[:, k, :], k == 0, k == 1)
                ins.then_inc(multiplied, 1)

        NORM_AFTER = (lambda m: ("x", 0, m), lambda m: ("even_end", 0, PLAIN["even_end"] + m),
                      lambda m: ("down0", m // 2, m % 2), lambda m: ("odd_end", 0, PLAIN["odd_end"] + m),
                      lambda m: ("down1", m // 2, m % 2))

        POOLED = (0, 5, 7, 5, 7)

        def norm_sum(pe, k):
            first = POOLED[k]
            if first:
                pe.wait_ge(q_ss, k * (KT - 1) + first)
                for h in range(2):
                    nc.tensor.matmul(mx[:, h, 0:HALF], ones, n_ss[:, h * HALF:(h + 1) * HALF], start=True, stop=False)
            for t in range(first, KT):
                pe.wait_ge(q_sq, k * KT + t + 1)
                for h in range(2):
                    ins = nc.tensor.matmul(mx[:, h, 0:HALF], ones, n_sq[:, t % 2, h * HALF:(h + 1) * HALF],
                                           start=t == 0, stop=t == KT - 1)
                ins.then_inc(q_sum if t == KT - 1 else q_ss, 1)

        LN_EXP, SILU = "natural_log_exp_and_others", "silu_and_others"

        def load_table(name):
            nc.scalar.preload_act_table_set(name)

        def square(act, k, t):
            emptied(act, *NORM_AFTER[k](t))
            if t >= 2:
                act.wait_ge(q_ss, k * (KT - 1) + t - 1)
            nc.scalar.activation(n_sq[:, t % 2, :], x[:, t, :], ACT.Square).then_inc(q_sq, 1)

        def norm_scalar(act, k, last=False, meanwhile=()):
            load_table(LN_EXP)
            act.wait_ge(q_sum, k + 1)
            nc.scalar.activation(halves(n_rs[:, :]), mx[:, 0:2, 0:HALF], ACT.Ln, bias=eps[:, 0:1],
                                 scale=1.0 / D).then_inc(q_std, 1)
            act.wait_ge(q_std, k + 1)
            nc.scalar.activation(n_rs[:, :], n_rs[:, :], ACT.Exp, scale=-0.5).then_inc(q_rs, 1)
            if meanwhile:
                split_hi(act, *meanwhile, first=True)
            if not last:
                for t in range(KT):
                    act.wait_ge(q_xf, k * KT + t + 1)
                    nc.scalar.activation(xn_hi[:, t, :], n_xf[:, t % 4, :], ACT.Copy).then_inc(q_hi, 1)

        def add_square(pool, k, t):
            pool.wait_ge(q_sq, k * KT + t + 1)
            if t == 0:
                nc.gpsimd.tensor_copy(n_ss[:, :], n_sq[:, 0, :]).then_inc(q_ss, 1)
            else:
                pool.wait_ge(q_ss, k * (KT - 1) + t)
                nc.gpsimd.tensor_tensor(n_ss[:, :], n_ss[:, :], n_sq[:, t % 2, :], ALU.add).then_inc(q_ss, 1)

        def low_part(eng, k, t):
            eng.wait_ge(q_hi, k * KT + t + 1)
            engine = nc.gpsimd if t % 2 else nc.vector
            engine.tensor_tensor(xn_lo[:, t, :], n_xf[:, t % 4, :], xn_hi[:, t, :].bitcast(F32),
                                 ALU.subtract).then_inc(q_lo[t % 2], 1)

        def norm_gpsimd(pool, k):
            for t in range(1, KT, 2):
                low_part(pool, k, t)

        def norm_vector(dve, k, last=False):
            dve.wait_ge(q_rs, k + 1)
            for t in range(KT):
                if not last and t >= 4:
                    dve.wait_ge(q_lo[t % 2], (k * KT + t - 4) // 2 + 1)
                g = cols[:, COL_NORM[k] + t:COL_NORM[k] + t + 1]
                dst = yT[:, t, :] if last else n_xf[:, t % 4, :]
                nc.vector.scalar_tensor_tensor(out=dst, in0=x[:, t, :], scalar=g, in1=n_rs[:, :], op0=ALU.mult,
                                               op1=ALU.mult).then_inc(y_norm if last else q_xf, 1)
                if not last and t % 2 == 1:
                    low_part(dve, k, t - 1)
            if not last:
                dve.wait_ge(q_xf, (k + 1) * KT)
                for n in range(2):
                    dve.wait_ge(q_lo[n], (k + 1) * KT // 2)

        def add_to_x(dve, phase, i, n, m):
            p = plan.pair(phase, n)
            dve.wait_ge(multiplied, plan.summed(phase, i, n))
            dst = x[:, m, :] if isinstance(m, int) else x[:, m, :].rearrange("p a n -> p (a n)")
            nc.vector.tensor_tensor(halves(dst), pair_view(p), halves(dst), ALU.add).then_inc(drained[p], 1)

        def ffn_tensor(pe, layer):
            up, down, k = f"up{layer}", f"down{layer}", 2 * layer + 1
            with pe.Fori(0, FT // 2) as i:
                for t in range(2):
                    unit(pe, up, i, 2 * t, wait_norm=k if t == 0 else None)
                    unit(pe, up, i, 2 * t + 1)
            pe.wait_ge(f_lo, (layer + 1) * FT - 1)
            with pe.Fori(0, KT // 2) as i:
                for t in range(2):
                    p = plan.pair(down, t)
                    pe.wait_ge(drained[p], plan.drained(down, i, t))
                    for j in range(3):
                        d = plan.split_slot(down, 3 * t + j)
                        pe.wait_ge(w_ready, plan.unit(down, i, 3 * t + j) + 1 + RAW_LAG)
                        for q in range(DOWN[j]):
                            k2 = 8 * j + q
                            if k2 == FT - 1:
                                pe.wait_ge(f_lo, (layer + 1) * FT)
                            ins = product(pe, pair_view(p), w_hi[:, d, q * P:(q + 1) * P],
                                          w_lo[:, d, q * P:(q + 1) * P], h_hi[:, k2, :], h_lo[:, k2, :],
                                          k2 == 0, k2 == FT - 1)
                        ins.then_inc(multiplied, 1)

        def down_size(j):
            return DOWN[j % 3]

        def ahead(split, eng, phase, i, j, n=lambda j: KT):
            m = len(PHASES[phase][1])
            if j < m:
                split(eng, phase, i, j, n(j))
            else:
                split(eng, phase, i + 1, j - m, n(j - m), again=True)

        EVEN_END = (0, 1, 2, 3, ("up0", 0, 0), 4, 5, 6, ("up0", 0, 1), 7)
        ODD_END = (0, 1, 2, 3, ("up1", 0, 0), 4, 5, 6, ("up1", 0, 1), 7)

        def squares_while_splitting(eng, split, step, k, sequence):
            for what in sequence:
                if isinstance(what, int):
                    if what < POOLED[k] or step is square:
                        step(eng, k, what)
                else:
                    split(eng, *what)

        def ffn_scalar(act, layer):
            up, down = f"up{layer}", f"down{layer}"
            load_table(SILU)
            with act.Fori(0, FT // 2) as i:
                for t in range(2):
                    act.wait_ge(multiplied, plan.summed(up, i, 2 * t))
                    act.wait_ge(drained[1], plan.drained(up, i, 2 * t + 1))
                    nc.scalar.activation(halves(f_g[:, :]), pair_view(0), ACT.Silu).then_inc(drained[0], 1)
                    ahead(split_hi, act, up, i, 2 * t + 2)
                    ahead(split_hi, act, up, i, 2 * t + 3)
                    act.wait_ge(drained[1], plan.drained(up, i, 2 * t + 1) + 1)
                    nc.scalar.activation(h_hi[:, ds(i * 2 + t, 1), :].rearrange("p a n -> p (a n)"), f_h[:, :],
                                         ACT.Copy).then_inc(f_hi, 1)
            with act.Fori(0, KT // 2 - 1) as i:
                for j in range(6):
                    ahead(split_hi, act, down, i, j + 2, down_size)

        def ffn_gpsimd(pool, layer):
            up, down = f"up{layer}", f"down{layer}"
            with pool.Fori(0, FT // 2) as i:
                for j in range(4):
                    ahead(split_lo, pool, up, i, j + 2)
            with pool.Fori(0, KT // 2 - 1) as i:
                for j in range(6):
                    ahead(split_lo, pool, down, i, j + 2, down_size)

        def ffn_end(layer):
            down, i = f"down{layer}", KT // 2 - 1
            rest = [(down, i, j, down_size(j)) for j in range(2, 6)]
            after = [("odd_kq", 0, 0), ("odd_kq", 0, 1)] if layer == 0 else []
            return [rest[0], 0, 1, rest[1], 2, 3, rest[2], 4, 5, rest[3], 6, *after, 7]

        def ffn_vector(dve, layer):
            up, down = f"up{layer}", f"down{layer}"
            with dve.Fori(0, FT // 2) as i:
                for t in range(2):
                    n = layer * FT + i * 2 + t + 1
                    dve.wait_ge(multiplied, plan.summed(up, i, 2 * t + 1))
                    dve.wait_ge(drained[0], plan.drained(up, i, 2 * t) + 1)
                    nc.vector.tensor_tensor(halves(f_h[:, :]), pair_view(1), halves(f_g[:, :]),
                                            ALU.mult).then_inc(drained[1], 1)
                    dve.wait_ge(f_hi, n)
                    nc.vector.tensor_tensor(h_lo[:, ds(i * 2 + t, 1), :].rearrange("p a n -> p (a n)"), f_h[:, :],
                                            h_hi[:, ds(i * 2 + t, 1), :].rearrange("p a n -> p (a n)").bitcast(F32),
                                            ALU.subtract).then_inc(f_lo, 1)
                    dve.wait_ge(f_lo, n)
            with dve.Fori(0, KT // 2) as i:
                for t in range(2):
                    add_to_x(dve, down, i, t, ds(i * 2 + t, 1))

        C_ATT, C_ATT_S, C_IN, C_IN_S, C_KD = 0, P, P + TS, 2 * P + TS, 2 * P + 2 * TS
        kdec_p, kdec_s = ch[:, C_KD:C_KD + 1], ch[0:TS, C_KD + 1:C_KD + 2]
        cdec_p, cdec_s = ch[:, C_KD + 2:C_KD + 3], ch[:, C_KD + 3:C_KD + 4]

        def evacuate_odd(act, phase, i, n, a, b, scale):
            p = plan.pair(phase, n)
            act.wait_ge(multiplied, plan.summed(phase, i, n))
            nc.scalar.activation(halves(a[:, :]), pair_view(p), ACT.Copy, scale=scale)
            nc.scalar.activation(halves(b[0:64, :]), acc[64:128, p, :, 0:HALF], ACT.Copy, scale=scale)
            nc.scalar.activation(halves(b[64:128, :]), acc[0:64, p, :, 0:HALF], ACT.Copy, scale=scale)\
                .then_inc(drained[p], 1)

        def odd_scalar(act, phase, i, h, last=False):
            def evac(j, out, func):
                act.wait_ge(multiplied, plan.summed(phase, i, j))
                nc.scalar.activation(halves(out), pair_view(plan.pair(phase, j)), func)\
                    .then_inc(drained[plan.pair(phase, j)], 1)

            e = o_pe
            w = PLAIN[phase]
            load_table(SILU)
            ahead(split_hi, act, phase, i, 1)
            evac(0, va[:, 0, :], ACT.Copy)
            ahead(split_hi, act, phase, i, 2)
            e.wait(act, h, "tk")
            act.wait_ge(s_ch, 16 * (h + 1))
            nc.scalar.activation(kdt[:, 0:NC, :], chunks(mx[:, 2, :]), ACT.Copy, scale=kdec_p)
            o_act.done(nc.scalar.activation(kdt[0:TS, NC, :], mx[0:TS, 3, 0:P], ACT.Copy, scale=kdec_s), "kdt")
            e.wait(act, h, "tv0")
            nc.scalar.activation(vtok[:, 0:NC, 0:P], chunks(mx[:, 0, :]), ACT.Copy)
            o_act.done(nc.scalar.activation(vtok[0:TS, NC, 0:P], mx[0:TS, 1, 0:P], ACT.Copy), "v0")
            evac(1, va[:, 1, :], ACT.Copy)
            ahead(split_hi, act, phase, i, 3)
            e.wait(act, h, "tv1")
            nc.scalar.activation(vtok[:, 0:NC, P:2 * P], chunks(mx[:, 2, :]), ACT.Copy)
            o_act.done(nc.scalar.activation(vtok[0:TS, NC, P:2 * P], mx[0:TS, 3, 0:P], ACT.Copy), "v1")
            evac(2, gs[:, 0, :], ACT.Silu)
            ahead(split_hi, act, phase, i, 4)
            evac(3, gs[:, 1, :], ACT.Silu)
            load_table(LN_EXP)
            o_dve.wait(act, h, "cen")
            o_act.done(nc.scalar.activation(osq[:, :, :], of[:, :, :], ACT.Square), "osq")
            ahead(split_hi, act, phase, i, 5)
            e.wait(act, h, "var")
            o_act.done(nc.scalar.activation(halves(orv[:, :]), mx[:, 2:4, 0:HALF], ACT.Ln, bias=eps[:, 1:2],
                                            scale=1.0 / RET_V), "oln")
            o_act.wait(act, h, "oln")
            o_act.done(nc.scalar.activation(orv[:, :], orv[:, :], ACT.Exp, scale=-0.5), "oinv")
            if not last:
                evacuate_odd(act, phase, i, 4, ka, kb, P ** -0.5)
                ahead(split_hi, act, phase, i, w)
            for d in range(2):
                o_dve.wait(act, h, f"y{d}")
                o_act.done(nc.scalar.activation(oyh[:, d, :], of[:, d, :], ACT.Copy), f"yh{d}")
            if not last:
                evacuate_odd(act, phase, i, 5, qa, qb, 1.0)
                ahead(split_hi, act, phase, i, w + 1)
            o_dve.wait(act, h, "rs")
            act.dma_start(ret_s[0].rearrange("b h k v -> h k b v")[ds(h, 1)].rearrange("a k b v -> k (a b) v"),
                          r_s[:, :, :]).then_inc(ret_free, 16)
            act.dma_start(ret_p[0, 0][ds(h, 1)].rearrange("a k v -> k (a v)"), rst[:, NC - 1, :]).then_inc(ret_free, 16)
            if not last:
                ahead(split_hi, act, phase, i, w + 2)

        def odd_vector(dve, phase, i, h):
            def step(ins, name):
                o_dve.done(ins, name)
                o_dve.wait(dve, h, name)

            nc.vector.tensor_copy(gnw[:, 0, :], cols[:, COL_GN_G:COL_GN_G + 16].rearrange("p (h g) -> p h g", g=2)
                                  [:, ds(h, 1), :].rearrange("p a g -> p (a g)"))
            nc.vector.tensor_copy(gnw[:, 1, :], cols[:, COL_GN_B:COL_GN_B + 16].rearrange("p (h g) -> p h g", g=2)
                                  [:, ds(h, 1), :].rearrange("p a g -> p (a g)"))
            dve.wait_ge(s_co, 16)
            for n in range(2):
                dve.wait_ge(drained[plan.pair(phase, n)], plan.drained(phase, i, n))
            for a, b, out, n in ((ka, kb, rk, "k"), (qa, qb, rq, "q")):
                nc.vector.tensor_tensor(t1[:, :], a[:, :], co[:, 0, :], ALU.mult)
                step(nc.vector.tensor_tensor(t2[:, :], b[:, :], co[:, 1, :], ALU.mult), "t" + n)
                step(nc.vector.tensor_tensor(out[:, :], t1[:, :], t2[:, :], ALU.add), "r" + n)
            dve.wait_ge(s_ch, 16 * (h + 1))
            nc.vector.tensor_tensor(chunks(rqg[:, 0:TP]), chunks(rq[:, 0:TP]), each_chunk(ch[:, C_IN:C_IN + P]),
                                    ALU.mult)
            step(nc.vector.tensor_tensor(rqg[:, TP:T], rq[:, TP:T], ch[:, C_IN_S:C_IN_S + TS], ALU.mult), "qg")
            o_pe.wait(dve, h, "att")
            nc.vector.tensor_tensor(chunks(att[:, 0:TP]), chunks(mx[:, 0, :]), each_chunk(ch[:, C_ATT:C_ATT + P]),
                                    ALU.mult)
            step(nc.vector.tensor_tensor(att[0:TS, TP:T], mx[0:TS, 1, 0:TS], ch[0:TS, C_ATT_S:C_ATT_S + TS],
                                         ALU.mult), "att")
            o_pe.wait(dve, h, "kv")
            step(nc.vector.tensor_copy(rst[:, 0, :], mx[:, 0, 0:RET_V]), "r0")
            for c in range(1, NC):
                src = mx[:, c // 2, (c % 2) * RET_V:(c % 2 + 1) * RET_V]
                step(nc.vector.scalar_tensor_tensor(out=rst[:, c, :], in0=rst[:, c - 1, :], scalar=cdec_p, in1=src,
                                                    op0=ALU.mult, op1=ALU.add), f"r{c}")
            o_pe.wait(dve, h, "op")
            step(nc.vector.tensor_copy(of[:, :, 0:TP], mx[:, 2:4, :]), "of_p")
            o_pe.wait(dve, h, "os")
            step(nc.vector.tensor_copy(of[:, :, TP:T], mx[:, 0, 0:2 * TS].rearrange("p (d n) -> p d n", d=2)), "of_s")
            step(nc.vector.tensor_tensor(both[:, :], of[:, 0, :], of[:, 1, :], ALU.add), "o_both")
            o_pe.wait(dve, h, "mean")
            for d in range(2):
                ins = nc.vector.scalar_tensor_tensor(out=halves(of[:, d, :]), in0=mx[:, 0:2, 0:HALF],
                                                     scalar=-1.0 / RET_V, in1=halves(of[:, d, :]), op0=ALU.mult,
                                                     op1=ALU.add)
            step(ins, "cen")
            o_act.wait(dve, h, "osq")
            step(nc.vector.tensor_tensor(both[:, :], osq[:, 0, :], osq[:, 1, :], ALU.add), "sq_both")
            o_act.wait(dve, h, "oinv")
            for d in range(2):
                step(nc.vector.scalar_tensor_tensor(out=of[:, d, :], in0=of[:, d, :], scalar=gnw[:, 0, d:d + 1],
                                                    in1=orv[:, :], op0=ALU.mult, op1=ALU.mult), f"on{d}")
                emptied(dve, phase, i, 2 + d)
                step(nc.vector.scalar_tensor_tensor(out=of[:, d, :], in0=of[:, d, :], scalar=gnw[:, 1, d:d + 1],
                                                    in1=gs[:, d, :], op0=ALU.add, op1=ALU.mult), f"y{d}")
            for d in range(2):
                o_act.wait(dve, h, f"yh{d}")
                step(nc.vector.tensor_tensor(oyl[:, d, :], of[:, d, :], oyh[:, d, :].bitcast(F32), ALU.subtract),
                     f"yl{d}")
            o_pe.wait(dve, h, "kvs")
            step(nc.vector.scalar_tensor_tensor(out=r_s[:, :, :].rearrange("p b n -> p (b n)"),
                                                in0=r_s[:, :, :].rearrange("p b n -> p (b n)"), scalar=cdec_s,
                                                in1=mx[:, :, :].rearrange("p a n -> p (a n)"), op0=ALU.mult,
                                                op1=ALU.add), "rs")
            for m in range(KT):
                add_to_x(dve, phase, i, PLAIN[phase] + m, m)

        def odd_tensor(pe, phase, i, h, last=False):
            def mm(out, lhs, rhs, start=True, stop=True):
                return nc.tensor.matmul(out, lhs, rhs, start=start, stop=stop)

            def at(a, c):
                return a[:, c * P:(c + 1) * P]

            def turn(src, bank, name):
                for c in range(NC):
                    nc.tensor.transpose(mx[:, bank, c * P:(c + 1) * P], at(src, c), ident)
                o_pe.done(nc.tensor.transpose(mx[0:TS, bank + 1, 0:P], src[:, TP:T], ident), name)

            def sums(bank, src):
                for half in range(2):
                    ins = mm(mx[:, bank + half, 0:HALF], ones, src[:, half * HALF:(half + 1) * HALF])
                return ins

            def U(j, a=0, b=KT):
                unit(pe, phase, i, j, a, b)

            U(0)
            o_dve.wait(pe, h, "rq")
            for c in range(NC):
                mm(mx[:, 0, c * P:(c + 1) * P], at(rk, c), at(rq, c))
            o_pe.done(mm(mx[0:TS, 1, 0:TS], rk[:, TP:T], rq[:, TP:T]), "att")
            turn(rk, 2, "tk")
            U(1, 0, 3)
            emptied(pe, phase, i, 0)
            o_dve.wait(pe, h, "att")
            turn(va[:, 0, :], 0, "tv0")
            U(1, 3, 8)
            U(2, 0, 2)
            emptied(pe, phase, i, 1)
            o_act.wait(pe, h, "kdt")
            turn(va[:, 1, :], 2, "tv1")
            U(2, 2, 5)
            o_act.wait(pe, h, "v1")
            for c in range(NC):
                ins = mm(mx[:, c // 2, (c % 2) * RET_V:(c % 2 + 1) * RET_V], kdt[:, c, :], vtok[:, c, :])
            o_pe.done(ins, "kv")
            U(2, 5, 8)
            U(3, 0, 2)
            o_dve.wait(pe, h, f"r{NC - 1}")
            for d in range(2):
                for c in range(NC):
                    ins = mm(mx[:, 2 + d, c * P:(c + 1) * P], vtok[:, c, d * P:(d + 1) * P], at(att, c), True, c == 0)
                    if c:
                        ins = mm(mx[:, 2 + d, c * P:(c + 1) * P], rst[:, c - 1, d * P:(d + 1) * P], at(rqg, c),
                                 False, True)
            o_pe.done(ins, "op")
            U(3, 2, 4)
            pe.wait_ge(ret_in, 16 * (h + 1))
            for d in range(2):
                mm(mx[:, 0, d * TS:(d + 1) * TS], vtok[0:TS, NC, d * P:(d + 1) * P], att[0:TS, TP:T], True, False)
                for b in range(NB):
                    c = d * TS + b * LS
                    ins = mm(mx[:, 0, c:c + LS], r_s[:, b, d * P:(d + 1) * P], rqg[:, TP + b * LS:TP + (b + 1) * LS],
                             False, b == NB - 1)
            o_pe.done(ins, "os")
            U(3, 4, 6)
            o_dve.wait(pe, h, "o_both")
            o_pe.done(sums(0, both), "mean")
            U(3, 6, 8)
            if not last:
                U(4, 0, 6)
            o_dve.wait(pe, h, "sq_both")
            o_pe.done(sums(2, both), "var")
            if not last:
                U(4, 6, 8)
            o_pool.wait(pe, h, "kdm")
            o_act.wait(pe, h, "oln")
            for b in range(NB):
                ins = mm(mx[:, b // 2, (b % 2) * RET_V:(b % 2 + 1) * RET_V], kdm[0:TS, b, :], vtok[0:TS, NC, :])
            o_pe.done(ins, "kvs")
            if not last:
                U(5)
            o_dve.wait(pe, h, "yl1")
            for j in range(2):
                rows_unit(pe, phase, i, PLAIN[phase] + j, PLAIN[phase] + 4 * j, oyh, oyl)

        def odd_gpsimd(pool, phase, i, h, last=False):
            ahead(split_lo, pool, phase, i, 1)
            ahead(split_lo, pool, phase, i, 2)
            o_act.wait(pool, h, "kdt")
            o_pool.done(nc.gpsimd.tensor_tensor(kdm[0:TS, :, :], kdt[0:TS, NC, :].unsqueeze(1).to_broadcast([TS, NB, P]),
                                                block[0:TS, :].unsqueeze(2).to_broadcast([TS, NB, P]), ALU.mult), "kdm")
            for j in (3, 4, 5) if last else range(3, 9):
                ahead(split_lo, pool, phase, i, j)

        @block_.sync
        def _(sp):
            sp.dma_start(every[:, :], c_every).then_inc(s_every, 16)
            sp.dma_start(x_in[:, 0:NC, :], x_prompt[0].rearrange("(c p) d -> p c d", p=P)).then_inc(s_in, 16)
            sp.dma_start(x_in[0:TS, NC, :], x_sample.rearrange("b t d -> (b t) d")).then_inc(s_in, 16)
            at = 0
            for src in (norm_mix, norm_ffn, final_norm, odd_gn_g, odd_gn_b):
                a = (src.rearrange("l (k p) -> (l k) p", p=P) if len(src.shape) == 2
                     else src.rearrange("(k p) -> k p", p=P))
                sp.dma_start(rows_1[at:at + a.shape[0], :], a).then_inc(s_par, 16)
                at += a.shape[0]
            at = 0
            for src in (even_conv_a, even_conv_qkv, even_dn_norm):
                a = (src[0].rearrange("w (k p) -> (w k) p", p=P) if len(src.shape) == 3 else src)
                sp.dma_start(rows_2[at:at + a.shape[0], :], a).then_inc(s_par, 16)
                at += a.shape[0]
            load(sp, "ab", 0, 0, by_kt(), wcol(w_e, EVEN_IN - P))
            sp.dma_start(rows_a[0:2 * NB, :], state_conv_a[0].rearrange("b w c -> (b w) c")).then_inc(s_a, 16)
            sp.dma_start(rows_q[0:3 * NB, :], state_conv_qkv[0].rearrange("b w c -> (b w) c")).then_inc(s_q, 16)
            sp.dma_start(ce[:, :], c_even).then_inc(s_ce, 16)
            sp.dma_start(dtb[:, :], even_dt_bias[0].partition_broadcast(P)).then_inc(s_gp, 16)
            sp.dma_start(nega[:, :], even_a_log[0].partition_broadcast(P)).then_inc(s_gp, 16)

            def even_rows(phase, i, j, h):
                load(sp, phase, i, PLAIN[phase] + j, two_rows, w_eo.rearrange("(g r p) n -> r p g n", g=2, p=P)
                     [ds(h, 1), :, :, j * 512:(j + 1) * 512].rearrange("a p g n -> p (a g) n"))

            def even_head(phase, i, h, last=False):
                for j, col in enumerate(E_UNITS):
                    load(sp, phase, i, j, by_kt(), wcol(w_e, col + h * P), slots={3: 2, 4: 0}.get(j, 1))
                    if j == 2:
                        sp.wait_ge(state_free, 32 * h + 1)
                        sp.dma_start(s_s[:, :, :], state_delta[0].rearrange("b h k v -> h k b v")[ds(h, 1)]
                                     .rearrange("a k b v -> k (a b) v")).then_inc(state_in, 16)
                if not last:
                    load(sp, phase, i, 5, by_kt(), wcol(w_e, E_K + P + h * P))
                    load(sp, phase, i, 6, by_kt(), wcol(w_e, E_Q + P + h * P))
                for j in range(2):
                    even_rows(phase, i, j, h)

            def head_decays(h):
                sp.dma_start(ch[:, :], c_heads[ds(h, 1)].rearrange("a p n -> p (a n)")).then_inc(s_ch, 16)

            def odd_head(phase, i, h, last=False):
                for j, col in enumerate(O_UNITS):
                    load(sp, phase, i, j, by_kt(), wcol(w_o, col + h * 2 * P))
                    if j == 1:
                        sp.wait_ge(ret_free, 32 * h + 1)
                        sp.dma_start(r_s[:, :, :], state_ret[0].rearrange("b h k v -> h k b v")[ds(h, 1)]
                                     .rearrange("a k b v -> k (a b) v")).then_inc(ret_in, 16)
                if not last:
                    load(sp, phase, i, 4, by_kt(), wcol(w_o, O_K + P + h * P))
                    load(sp, phase, i, 5, by_kt(), wcol(w_o, O_Q + P + h * P))
                for j in range(2):
                    load(sp, phase, i, PLAIN[phase] + j, two_rows, w_oo.rearrange("(r g p) n -> r p g n", g=2, p=P)
                         [ds(h, 1), :, :, j * 512:(j + 1) * 512].rearrange("a p g n -> p (a g) n"))
                if not last:
                    o_dve.wait(sp, h, "rs")
                    head_decays(h + 1)

            load(sp, "even_kq", 0, 0, by_kt(), wcol(w_e, E_K))
            load(sp, "even_kq", 0, 1, by_kt(), wcol(w_e, E_Q))
            with sp.Fori(0, DN_H - 1) as i:
                even_head("even", i, i)
            even_head("even_end", 0, DN_H - 1, last=True)
            for layer in range(2):
                wg, wu, wd = ffn_w_gate[layer], ffn_w_up[layer], ffn_w_down[layer]
                up, down = f"up{layer}", f"down{layer}"
                with sp.Fori(0, FT // 2) as i:
                    for t in range(2):
                        load(sp, up, i, 2 * t, by_kt(), wcol(wg, i * 2 * P + t * P))
                        load(sp, up, i, 2 * t + 1, by_kt(), wcol(wu, i * 2 * P + t * P))
                with sp.Fori(0, KT // 2) as i:
                    for t in range(2):
                        for j in range(3):
                            load(sp, down, i, 3 * t + j, by_kt(DOWN[j]),
                                 wd.rearrange("(k p) c -> p k c", p=P)[:, 8 * j:8 * j + DOWN[j], ds(i * 2 * P + t * P, P)])
                if layer == 0:
                    load(sp, "odd_kq", 0, 0, by_kt(), wcol(w_o, O_K))
                    load(sp, "odd_kq", 0, 1, by_kt(), wcol(w_o, O_Q))
                    with sp.Fori(0, RET_H - 1) as i:
                        odd_head("odd", i, i)
                    odd_head("odd_end", 0, RET_H - 1, last=True)
            for c in range(NC + 1):
                sp.wait_ge(y_row, c + 1)
                dst = y_prompt[0, c * P:(c + 1) * P, :] if c < NC else y_sample.rearrange("b t d -> (b t) d")
                n = P if c < NC else TS
                sp.dma_start(dst, y_out[0:n, c % 2, :]).then_inc(y_sent[c % 2], 16)
            sp.wait_ge(y_sent[0], 16 * 3)
            sp.wait_ge(y_sent[1], 16 * 2)
            sp.wait_ge(state_free, 32 * DN_H + 1)
            sp.wait_ge(ret_free, 32 * RET_H + 1)
            sp.wait_ge(rows_sent, 16 * 8)

        def evacuate_conv(act, phase, i, n, buf):
            p = plan.pair(phase, n)
            act.wait_ge(multiplied, plan.summed(phase, i, n))
            nc.scalar.activation(buf[:, WQ - 1:WQ - 1 + HALF], acc[:, p, 0, 0:HALF], ACT.Copy)
            nc.scalar.activation(buf[:, WQ - 1 + HALF:SQ], acc[:, p, 1, 0:TP - HALF], ACT.Copy)
            nc.scalar.activation(sample_pad(buf, WQ - 1, PADQ)[:, :, WQ - 1:], seqs(acc[:, p, 1, TP - HALF:HALF]),
                                 ACT.Copy).then_inc(drained[p], 1)

        def even_scalar(act, phase, i, h, last=False):
            def inverse_root(name, bank, scale):
                e_act.done(nc.scalar.activation(halves(std[:, :]), mx[:, bank:bank + 2, 0:HALF], ACT.Ln,
                                                bias=eps[:, 0:1], scale=scale), name + "_ln")
                e_act.wait(act, h, name + "_ln")
                e_act.done(nc.scalar.activation(std[:, :], std[:, :], ACT.Exp, scale=-0.5), name + "_inv")

            def copy_p(s):
                e_pe.wait(act, h, f"P{s}")
                if s <= 4:
                    nc.scalar.activation(pp[0:TS, TP:T], mx[0:TS, 1, 0:TS], ACT.Copy)
                e_act.done(nc.scalar.activation(pp[:, 0:TP], mx[:, 0, :], ACT.Copy), f"p{s}")

            ahead(split_hi, act, phase, i, 1)
            load_table(LN_EXP)
            e_pe.wait(act, h, "rows")
            nc.scalar.activation(gr[:, 0:TP], mx[:, 0, :], ACT.Copy)
            e_act.done(nc.scalar.activation(gr[:, TP:T], mx[:, 1, 0:TS], ACT.Copy), "gr")
            nc.scalar.activation(eg[:, 0:TP], mx[:, 0, :], ACT.Exp)
            e_act.done(nc.scalar.activation(eg[:, TP:T], mx[:, 1, 0:TS], ACT.Exp), "eg")
            load_table(SILU)
            e_dve.wait(act, h, "ck")
            e_act.done(nc.scalar.activation(ks[:, :], cs[:, :], ACT.Silu), "ks")
            e_act.wait(act, h, "ks")
            e_act.done(nc.scalar.activation(sq[:, :], ks[:, :], ACT.Square), "k_sq")
            load_table(LN_EXP)
            e_pool.wait(act, h, "df")
            e_act.done(nc.scalar.activation(dt_[:, :], dm[:, :], ACT.Relu, scale=-1.0), "dt_lo")
            e_act.wait(act, h, "dt_lo")
            e_act.done(nc.scalar.activation(dm[:, :], dm[:, :], ACT.Relu), "dm_lo")
            evacuate_conv(act, phase, i, 0, cbuf)
            e_pe.wait(act, h, "l2k")
            inverse_root("k", 0, 1.0)
            e_act.wait(act, h, "dm_lo")
            e_act.done(nc.scalar.activation(dm[:, :], dm[:, :], ACT.Exp, scale=-1.0), "dm")
            ahead(split_hi, act, phase, i, 2)
            e_act.done(nc.scalar.activation(dt_[:, :], dt_[:, :], ACT.Exp, scale=-1.0), "dt")
            load_table(SILU)
            e_dve.wait(act, h, "cq")
            e_act.done(nc.scalar.activation(qs[:, :], cs[:, :], ACT.Silu), "qs")
            e_act.wait(act, h, "qs")
            e_act.done(nc.scalar.activation(sq[:, :], qs[:, :], ACT.Square), "q_sq")
            e_dve.wait(act, h, "cv")
            e_act.done(nc.scalar.activation(vs[:, :], vs[:, :], ACT.Silu), "vs")
            load_table(LN_EXP)
            e_pe.wait(act, h, "l2q")
            e_dve.wait(act, h, "kT")
            inverse_root("q", 2, 1.0)
            load_table(SILU)
            act.wait_ge(multiplied, plan.summed(phase, i, 1))
            nc.scalar.activation(halves(zs[:, :]), pair_view(plan.pair(phase, 1)), ACT.Silu)\
                .then_inc(drained[plan.pair(phase, 1)], 1)
            ahead(split_hi, act, phase, i, 3)
            load_table(LN_EXP)
            copy_p(2)
            copy_p(4)
            act.wait_ge(multiplied, plan.summed(phase, i, 2))
            nc.scalar.activation(halves(gcs[:, :]), pair_view(plan.pair(phase, 2)), ACT.Copy)\
                .then_inc(drained[plan.pair(phase, 2)], 1)
            ahead(split_hi, act, phase, i, 4)
            copy_p(8)
            copy_p(16)
            ahead(split_hi, act, phase, i, 5)
            copy_p(32)
            copy_p(64)
            if not last:
                ahead(split_hi, act, phase, i, 6)
            emptied(act, phase, i, 4)
            e_act.done(nc.scalar.activation(yh[:, 0, :], ca1[:, 0:T], ACT.Copy), "yah")
            for c in range(NC):
                e_pe.wait(act, h, f"u{c}")
                e_act.done(nc.scalar.activation(uu[:, :], mx[:, 1, 256:384], ACT.Copy), f"uu{c}")
                if c == 2:
                    e_pe.wait(act, h, "us")
                    e_act.done(nc.scalar.activation(us_[0:TS, :], mx[0:TS, 2, P:2 * P], ACT.Copy), "us_")
            if last:
                ahead(split_hi, act, phase, i, 6)
            else:
                evacuate_conv(act, phase, i, 5, cbuf)
                ahead(split_hi, act, phase, i, 7)
            e_dve.wait(act, h, "oT_p")
            e_act.done(nc.scalar.activation(sq[:, :], oT[:, :], ACT.Square), "o_sq")
            e_pe.wait(act, h, "onorm")
            inverse_root("o", 0, 1.0 / DN_D)
            e_dve.wait(act, h, "yb")
            e_act.done(nc.scalar.activation(yh[:, 1, :], yf[:, :], ACT.Copy), "ybh")
            if not last:
                evacuate_conv(act, phase, i, 6, cbq)
                ahead(split_hi, act, phase, i, 8)
            e_dve.wait(act, h, "s_new")
            act.dma_start(delta_s[0].rearrange("b h k v -> h k b v")[ds(h, 1)].rearrange("a k b v -> k (a b) v"),
                          s_s[:, :, :]).then_inc(state_free, 16)
            act.dma_start(delta_p[0, 0][ds(h, 1)].rearrange("a k v -> k (a v)"), s_p[:, :]).then_inc(state_free, 16)
            if not last:
                ahead(split_hi, act, phase, i, 9)

        @block_.scalar
        def _(act):
            for t in range(1, KT, 2):
                act.wait_ge(multiplied, plan.summed("x", 0, t))
                nc.scalar.activation(x[:, t, 0:TP], acc[:, 1, 0, :], ACT.Copy)
                nc.scalar.activation(x[:, t, TP:T], acc[:, 1, 1, 0:TS], ACT.Copy).then_inc(drained[1], 1)
            act.wait_ge(s_eps, 1)
            split_hi(act, "ab", 0, 0)
            split_hi(act, "even_kq", 0, 0)
            split_hi(act, "even_kq", 0, 1)
            for t in range(KT):
                square(act, 0, t)
            norm_scalar(act, 0)
            act.wait_ge(multiplied, plan.summed("ab", 0, 0))
            nc.scalar.activation(halves(yf[:, :]), pair_view(1), ACT.Copy).then_inc(drained[1], 1)
            split_hi(act, "even", 0, 0)
            evacuate_conv(act, "even_kq", 0, 0, cbuf)
            a_dve.wait(act, 0, "ad")
            a_act.done(nc.scalar.activation(g_ab[:, :, :], g_ab[:, :, :], ACT.Abs), "abs")
            a_act.wait(act, 0, "abs")
            a_act.done(nc.scalar.activation(g_ab[:, :, :], g_ab[:, :, :], ACT.Exp, scale=-1.0), "exp")
            act.wait_ge(s_gp, 32)
            a_act.done(nc.scalar.activation(nega[:, :], nega[:, :], ACT.Exp), "nega")
            a_act.wait(act, 0, "exp")
            a_act.done(nc.scalar.activation(g_ab[:, :, :], g_ab[:, :, :], ACT.Ln, bias=1.0), "ln")
            a_act.done(nc.scalar.activation(g_beta[:, :, :], gate[:, :, DN_H:2 * DN_H], ACT.Sigmoid), "beta")
            a_pe.wait(act, 0, "gcum")
            nc.scalar.activation(kdec[:, 0:NC, :], mx[:, 3, 0:NC * DN_H].rearrange("p (c h) -> p c h", h=DN_H),
                                 ACT.Exp)
            a_act.done(nc.scalar.activation(kdec[0:TS, NC, :], mx[0:TS, 3, 16:16 + DN_H], ACT.Exp), "kdec")
            evacuate_conv(act, "even_kq", 0, 1, cbq)
            with act.Fori(0, DN_H - 1) as i:
                even_scalar(act, "even", i, i)
            even_scalar(act, "even_end", 0, DN_H - 1, last=True)
            squares_while_splitting(act, split_hi, square, 1, EVEN_END)
            norm_scalar(act, 1)
            for n in range(4):
                act.wait_ge(rows_copied, n + 1)
                k = 2 if n == 0 else 3
                dst_p = conv_a_p[0, 0] if n == 0 else conv_qkv_p[0, 0][:, (n - 1) * CA:n * CA]
                dst_s = (conv_a_s[0] if n == 0 else conv_qkv_s[0][:, :, (n - 1) * CA:n * CA])
                act.dma_start(dst_p, out_rows[0:k, n, :]).then_inc(rows_sent, 16)
                act.dma_start(dst_s.rearrange("b w c -> (b w) c"), out_rows[k:k + k * NB, n, :]).then_inc(rows_sent, 16)
            act.wait_ge(rows_sent, 16 * 8)
            act.wait_ge(state_free, 32 * DN_H + 1)
            ffn_scalar(act, 0)
            squares_while_splitting(act, split_hi, square, 2, ffn_end(0))
            act.dma_start(co[:, :, :], c_odd.rearrange("p (a n) -> p a n", a=2)).then_inc(s_co, 16)
            act.dma_start(ch[:, :], c_heads[0]).then_inc(s_ch, 16)
            norm_scalar(act, 2, meanwhile=("odd", 0, 0))
            evacuate_odd(act, "odd_kq", 0, 0, ka, kb, P ** -0.5)
            evacuate_odd(act, "odd_kq", 0, 1, qa, qb, 1.0)
            with act.Fori(0, RET_H - 1) as i:
                odd_scalar(act, "odd", i, i)
            odd_scalar(act, "odd_end", 0, RET_H - 1, last=True)
            squares_while_splitting(act, split_hi, square, 3, ODD_END)
            norm_scalar(act, 3)
            act.wait_ge(ret_free, 32 * RET_H + 1)
            ffn_scalar(act, 1)
            squares_while_splitting(act, split_hi, square, 4, ffn_end(1))
            norm_scalar(act, 4, last=True)
            for c in range(1, NC + 1, 2):
                act.wait_ge(multiplied, plan.summed("y", 0, c))
                if c > 1:
                    act.wait_ge(y_sent[1], 16)
                act.wait_ge(y_row, c)
                nc.scalar.activation(y_out[:, 1, :].rearrange("p (a n) -> p a n", a=2), acc[:, 1, :, :],
                                     ACT.Copy).then_inc(y_row, 1)

        def even_vector(dve, phase, i, h):
            def w(n):
                return pw[:, n:n + 1]

            def step(ins, name):
                e_dve.done(ins, name)
                e_dve.wait(dve, h, name)

            def conv_qkv(cbuf, kind, name, cs=cs):
                nc.vector.tensor_copy(out_q[:, kind, ds(h, 1), 0:3].rearrange("p a n -> p (a n)"), cbuf[:, SQ - 3:SQ])
                nc.vector.tensor_copy(out_q[:, kind, ds(h, 1), 3:].rearrange("p a (b n) -> p (a b) n", n=3),
                                      sample_pad(cbuf, WQ - 1, PADQ)[:, :, LS:])
                step(nc.vector.tensor_scalar(ca1[:, 0:NQ], cbuf[:, 0:NQ], w(kind), None, ALU.mult), name + "0")
                for t, (a, b) in ((1, (ca1, ca2)), (2, (ca2, ca1))):
                    step(nc.vector.scalar_tensor_tensor(out=b[:, 0:NQ], in0=cbuf[:, t:t + NQ], scalar=w(3 * t + kind),
                                                        in1=a[:, 0:NQ], op0=ALU.mult, op1=ALU.add),
                         f"{name}{t}")
                nc.vector.scalar_tensor_tensor(out=cs[:, 0:TP], in0=cbuf[:, 3:3 + TP], scalar=w(9 + kind),
                                               in1=ca1[:, 0:TP], op0=ALU.mult, op1=ALU.add)
                step(nc.vector.scalar_tensor_tensor(out=seqs(cs[:, TP:T]), in0=sample_pad(cbuf, WQ - 1, PADQ)[:, :, 3:],
                                                    scalar=w(9 + kind), in1=outputs_at(ca1, SQ, LS + WQ - 1),
                                                    op0=ALU.mult, op1=ALU.add), name)

            def beta_of(a, b, n):
                return bh[:, a:b].unsqueeze(2).to_broadcast([P, b - a, n])

            def beta_of_sample(n):
                return bh[0:TS, NC:NC + 1].to_broadcast([TS, n])

            def prefix(cbuf, kind, name):
                step(nc.vector.tensor_copy(sample_pad(cbuf, WQ - 1, PADQ)[:, :, 0:3],
                                           pre_q[:, kind, ds(h, 1), :].rearrange("p a (b n) -> p (a b) n", n=3)), name)

            nc.vector.tensor_copy(pw[:, 0:12].rearrange("p (t a) -> p t a", a=1),
                                  cols[:, COL_CONV_Q:COL_CONV_Q + 48].rearrange("p (t h) -> p t h", h=4)[:, :, ds(h, 1)])
            step(nc.vector.tensor_copy(pw[:, 12:15].rearrange("p (t a) -> p t a", a=1),
                                       cols[:, COL_CONV_A:COL_CONV_A + 12].rearrange("p (t h) -> p t h", h=4)
                                       [:, :, ds(h, 1)]), "pw")
            nc.vector.tensor_copy(gh[:, :].unsqueeze(2), g_g[:, :, ds(h, 1)])
            step(nc.vector.tensor_copy(bh[:, :].unsqueeze(2), g_beta[:, :, ds(h, 1)]), "gate")
            prefix(cbuf, 1, "pre_k")
            for n in range(2):
                dve.wait_ge(drained[plan.pair(phase, n)], plan.drained(phase, i, n))
            conv_qkv(cbuf, 1, "ck")
            prefix(cbuf, 2, "pre_v")
            e_act.wait(dve, h, "eg")
            nc.vector.tensor_tensor(bg[:, 0:TP], mx[:, 2, :], eg[:, 0:TP], ALU.mult)
            step(nc.vector.tensor_tensor(bg[:, TP:T], mx[:, 1, TS:2 * TS], eg[:, TP:T], ALU.mult), "bg")
            prefix(cbq, 0, "pre_q")
            e_act.wait(dve, h, "ks")
            conv_qkv(cbq, 0, "cq")
            emptied(dve, phase, i, 0)
            conv_qkv(cbuf, 2, "cv", cs=vs)
            e_act.wait(dve, h, "k_inv")
            step(nc.vector.tensor_tensor(kT[:, :], ks[:, :], std[:, :], ALU.mult), "kT")
            e_act.wait(dve, h, "dm")
            nc.vector.tensor_tensor(chunks(dm[:, 0:TP]), chunks(dm[:, 0:TP]), beta_of(0, NC, P), ALU.mult)
            step(nc.vector.tensor_tensor(dm[0:TS, TP:T], dm[0:TS, TP:T], beta_of_sample(TS), ALU.mult), "dmb")
            e_pe.wait(dve, h, "kk")
            nc.vector.tensor_tensor(dm[:, 0:TP], mx[:, 0, :], dm[:, 0:TP], ALU.mult)
            step(nc.vector.tensor_tensor(dm[0:TS, TP:T], mx[0:TS, 1, 0:TS], dm[0:TS, TP:T], ALU.mult), "A")
            e_act.wait(dve, h, "q_inv")
            step(nc.vector.scalar_tensor_tensor(out=qT[:, :], in0=qs[:, :], scalar=DN_D ** -0.5, in1=std[:, :],
                                                op0=ALU.mult, op1=ALU.mult), "qT")
            e_pe.wait(dve, h, "kq")
            e_pool.wait(dve, h, "dtm")
            nc.vector.tensor_tensor(dt_[:, 0:TP], mx[:, 2, :], dt_[:, 0:TP], ALU.mult)
            step(nc.vector.tensor_tensor(dt_[0:TS, TP:T], mx[0:TS, 3, 0:TS], dt_[0:TS, TP:T], ALU.mult), "aqk")
            e_pe.wait(dve, h, "tk")
            nc.vector.tensor_tensor(kd[:, 0:NC, :], chunks(mx[:, 0, :]),
                                    kdec[:, 0:NC, ds(h, 1)].to_broadcast([P, NC, P]), ALU.mult)
            step(nc.vector.tensor_tensor(kd[0:TS, NC, :], mx[0:TS, 1, 0:P],
                                         kdec[0:TS, NC, ds(h, 1)].to_broadcast([TS, P]), ALU.mult), "kd")
            e_pe.wait(dve, h, "tv")
            nc.vector.tensor_tensor(vb[:, 0:NC, :], chunks(mx[:, 2, :]), beta_of(0, NC, P), ALU.mult)
            step(nc.vector.tensor_tensor(vb[0:TS, NC, :], mx[0:TS, 3, 0:P], beta_of_sample(P), ALU.mult), "vb")

            e_pe.wait(dve, h, "P1")
            e_pool.wait(dve, h, "b1")
            nc.vector.tensor_tensor(zi[0:TS, TP:T], ident[0:TS, 0:TS], mx[0:TS, 1, 0:TS], ALU.subtract)
            nc.vector.tensor_tensor(xi[0:TS, TP:T], ident[0:TS, 0:TS], bm[0:TS, 0, TP:T], ALU.subtract)
            e_dve.done(nc.vector.tensor_tensor(chunks(zi[:, 0:TP]), each_chunk(ident), chunks(mx[:, 0, :]),
                                               ALU.subtract), "z1")
            step(nc.vector.tensor_tensor(chunks(xi[:, 0:TP]), each_chunk(ident), chunks(bm[:, 0, 0:TP]),
                                         ALU.subtract), "x1")

            def inverse_step(s):
                e_pe.wait(dve, h, f"Q{s}")
                if s <= 4:
                    nc.vector.tensor_tensor(zi[0:TS, TP:T], zi[0:TS, TP:T], mx[0:TS, 1, TS:2 * TS], ALU.subtract)
                    nc.vector.tensor_tensor(xi[0:TS, TP:T], xi[0:TS, TP:T], mx[0:TS, 1, 2 * TS:3 * TS], ALU.subtract)
                e_dve.done(nc.vector.tensor_tensor(zi[:, 0:TP], zi[:, 0:TP], mx[:, 2, :], ALU.subtract), f"z{s}")
                if s < MASKS[-1]:
                    e_dve.done(nc.vector.tensor_tensor(xi[:, 0:TP], xi[:, 0:TP], mx[:, 3, :], ALU.subtract), f"x{s}")
                e_dve.wait(dve, h, f"x{s}" if s < MASKS[-1] else f"z{s}")

            for s in (2, 4, 8, 16):
                inverse_step(s)
            p = plan.pair(phase, 3)
            dve.wait_ge(multiplied, plan.summed(phase, i, 3))
            emptied(dve, phase, i, 2)
            nc.vector.tensor_copy(sample_pad(bufa, WA - 1, PADA)[:, :, 0:2],
                                  pre_a[:, ds(h, 1), :].rearrange("p a (b n) -> p (a b) n", n=2))
            nc.vector.tensor_tensor(bufa[:, WA - 1:WA - 1 + HALF], acc[:, p, 0, 0:HALF], gcs[:, 0:HALF], ALU.mult)
            nc.vector.tensor_tensor(bufa[:, WA - 1 + HALF:SA], acc[:, p, 1, 0:TP - HALF], gcs[:, HALF:TP], ALU.mult)
            nc.vector.tensor_tensor(sample_pad(bufa, WA - 1, PADA)[:, :, 2:], seqs(acc[:, p, 1, TP - HALF:HALF]),
                                    seqs(gcs[:, TP:T]), ALU.mult).then_inc(drained[p], 1)
            emptied(dve, phase, i, 3)
            nc.vector.tensor_copy(out_a[:, ds(h, 1), 0:2].rearrange("p a n -> p (a n)"), bufa[:, SA - 2:SA])
            nc.vector.tensor_copy(out_a[:, ds(h, 1), 2:].rearrange("p a (b n) -> p (a b) n", n=2),
                                  sample_pad(bufa, WA - 1, PADA)[:, :, LS:])
            step(nc.vector.tensor_scalar(ca1[:, 0:NA], bufa[:, 0:NA], w(12), None, ALU.mult), "ca0")
            step(nc.vector.scalar_tensor_tensor(out=ca2[:, 0:NA], in0=bufa[:, 1:1 + NA], scalar=w(13), in1=ca1[:, 0:NA],
                                                op0=ALU.mult, op1=ALU.add), "ca1")
            nc.vector.scalar_tensor_tensor(out=cs[:, 0:TP], in0=bufa[:, 2:2 + TP], scalar=w(14), in1=ca2[:, 0:TP],
                                           op0=ALU.mult, op1=ALU.add)
            step(nc.vector.scalar_tensor_tensor(out=seqs(cs[:, TP:T]), in0=sample_pad(bufa, WA - 1, PADA)[:, :, 2:],
                                                scalar=w(14), in1=outputs_at(ca2, SA, LS + WA - 1), op0=ALU.mult,
                                                op1=ALU.add), "ca2")
            inverse_step(32)
            p = plan.pair(phase, 4)
            dve.wait_ge(multiplied, plan.summed(phase, i, 4))
            nc.vector.tensor_tensor(halves(ca1[:, 0:T]), pair_view(p), halves(cs[:, :]), ALU.mult)\
                .then_inc(drained[p], 1)
            inverse_step(64)

            state_in_wait(dve, h)
            e_pe.wait(dve, h, "S0")
            step(nc.vector.tensor_copy(s_p[:, :], mx[:, 0, 0:P]), "s0")
            for c in range(1, NC):
                e_pe.wait(dve, h, f"R{c}")
                step(nc.vector.tensor_tensor(rr[:, :], vb[:, c, :], mx[:, 1, 0:P], ALU.subtract), f"rr{c}")
                if c == 1:
                    e_pe.wait(dve, h, "Rs")
                    step(nc.vector.tensor_tensor(rs_[0:TS, :], vb[0:TS, NC, :], mx[0:TS, 2, 0:P],
                                                 ALU.subtract), "rs")
                e_pe.wait(dve, h, f"S{c}")
                step(nc.vector.scalar_tensor_tensor(out=s_p[:, :], in0=s_p[:, :],
                                                    scalar=eg[:, (c + 1) * P - 1:(c + 1) * P], in1=mx[:, 0, 0:P],
                                                    op0=ALU.mult, op1=ALU.add), f"s{c}")
            e_act.wait(dve, h, "yah")
            step(nc.vector.tensor_tensor(yl[:, 0, :], ca1[:, 0:T], yh[:, 0, :].bitcast(F32), ALU.subtract), "yal")
            e_pe.wait(dve, h, "os")
            step(nc.vector.tensor_copy(oT[:, TP:T], mx[:, 2, 256:256 + TS]), "oT_s")
            e_pe.wait(dve, h, f"o{NC - 1}")
            step(nc.vector.tensor_copy(oT[:, 0:TP], mx[:, 3, :]), "oT_p")
            step(nc.vector.tensor_tensor(s_s[:, :, :], s_s[:, :, :],
                                         seqs(eg[:, TP:T])[:, :, LS - 1:LS].to_broadcast([P, NB, P]), ALU.mult), "s_dec")
            e_act.wait(dve, h, "o_inv")
            step(nc.vector.scalar_tensor_tensor(out=yf[:, :], in0=oT[:, :], scalar=cols[:, COL_DN:COL_DN + 1],
                                                in1=std[:, :], op0=ALU.mult, op1=ALU.mult), "on")
            emptied(dve, phase, i, 1)
            step(nc.vector.tensor_tensor(yf[:, :], yf[:, :], zs[:, :], ALU.mult), "yb")
            e_act.wait(dve, h, "ybh")
            step(nc.vector.tensor_tensor(yl[:, 1, :], yf[:, :], yh[:, 1, :].bitcast(F32), ALU.subtract), "ybl")
            e_pe.wait(dve, h, "Ss")
            step(nc.vector.tensor_tensor(s_s[:, :, :].rearrange("p (a b) n -> p a (b n)", a=2),
                                         s_s[:, :, :].rearrange("p (a b) n -> p a (b n)", a=2), mx[:, 2:4, :],
                                         ALU.add), "s_new")
            for m in range(KT):
                add_to_x(dve, phase, i, PLAIN[phase] + m, m)

        @block_.vector
        def _(dve):
            nc.vector.memset(eps[:, 0:1], EPS)
            nc.vector.memset(eps[:, 1:2], GN_EPS).then_inc(s_eps, 1)
            for t in range(0, KT, 2):
                dve.wait_ge(multiplied, plan.summed("x", 0, t))
                nc.vector.tensor_copy(x[:, t, 0:TP], acc[:, 0, 0, :])
                nc.vector.tensor_copy(x[:, t, TP:T], acc[:, 0, 1, 0:TS]).then_inc(drained[0], 1)
            dve.wait_ge(s_setup_t, 1)
            nc.vector.tensor_copy(cols[:, :], mx[:, 0, 0:ROWS_1 + ROWS_2])
            nc.vector.tensor_copy(pre_a[:, :, :].rearrange("p t n -> p (t n)"), mx[:, 1, 0:4 * 2 * NB])
            nc.vector.tensor_copy(pre_q[:, :, :, :].rearrange("p k t n -> p (k t n)"), mx[:, 2, 0:12 * 3 * NB])\
                .then_inc(s_setup_c, 1)
            dve.wait_ge(s_setup_c, 1)
            norm_vector(dve, 0)

            def step(ins, name):
                a_dve.done(ins, name)
                a_dve.wait(dve, 0, name)

            step(nc.vector.memset(gate[:, :, :], 0.0), "zero")
            a_pe.wait(dve, 0, "ab_t")
            nc.vector.tensor_copy(gate[:, 0:NC, :], chunks(mx[:, 0, :])[:, :, P - 8:P])
            step(nc.vector.tensor_copy(gate[0:TS, NC, :], mx[0:TS, 1, P - 8:P]), "gate")
            dve.wait_ge(s_gp, 32)
            step(nc.vector.tensor_tensor(g_sp[:, :, :], gate[:, :, 0:DN_H],
                                         dtb[:, :].unsqueeze(1).to_broadcast([P, NC + 1, DN_H]), ALU.add), "sum")
            step(nc.vector.tensor_copy(g_ab[:, :, :], g_sp[:, :, :]), "ad")
            step(nc.vector.tensor_scalar(g_rl[:, :, :], g_sp[:, :, :], 0.0, None, ALU.max), "relu")
            a_act.wait(dve, 0, "ln")
            step(nc.vector.tensor_tensor(g_rl[:, :, :], g_rl[:, :, :], g_ab[:, :, :], ALU.add), "softplus")
            step(nc.vector.tensor_scalar(nega[:, :], nega[:, :], -1.0, None, ALU.mult), "neg")
            step(nc.vector.tensor_tensor(g_g[:, :, :], g_rl[:, :, :],
                                         nega[:, :].unsqueeze(1).to_broadcast([P, NC + 1, DN_H]), ALU.mult), "g")
            a_pe.wait(dve, 0, "gcum")
            nc.vector.memset(gcum[:, NC, :], 0.0)
            nc.vector.tensor_copy(gcum[:, 0:NC, :], mx[:, 2, 0:NC * DN_H].rearrange("p (c h) -> p c h", h=DN_H))
            a_dve.done(nc.vector.memset(bufa[:, 0:2], 0.0), "gc0")
            a_dve.wait(dve, 0, "gc0")
            nc.vector.tensor_copy(gcum[0:TS, NC, :], mx[0:TS, 2, 16:16 + DN_H])
            nc.vector.memset(km[:, :], 0.0)
            nc.vector.memset(cbq[:, 0:3], 0.0)
            a_dve.done(nc.vector.memset(cbuf[:, 0:3], 0.0), "gc")
            a_dve.wait(dve, 0, "gc")
            a_act.wait(dve, 0, "kdec")
            with dve.Fori(0, DN_H - 1) as i:
                even_vector(dve, "even", i, i)
            even_vector(dve, "even_end", 0, DN_H - 1)
            for n in range(4):
                dve.wait_ge(rows_turned, n + 1)
                r = 2 + 2 * NB if n == 0 else 3 + 3 * NB
                nc.vector.tensor_copy(out_rows[0:r, n, :], mx[0:r, n, :]).then_inc(rows_copied, 1)
            norm_vector(dve, 1)
            ffn_vector(dve, 0)
            norm_vector(dve, 2)
            with dve.Fori(0, RET_H - 1) as i:
                odd_vector(dve, "odd", i, i)
            odd_vector(dve, "odd_end", 0, RET_H - 1)
            norm_vector(dve, 3)
            ffn_vector(dve, 1)
            norm_vector(dve, 4, last=True)
            for c in range(0, NC + 1, 2):
                dve.wait_ge(multiplied, plan.summed("y", 0, c))
                if c:
                    dve.wait_ge(y_sent[0], 16 * (c // 2))
                    dve.wait_ge(y_row, c)
                n = P if c < NC else TS
                nc.vector.tensor_copy(y_out[0:n, 0, :].rearrange("p (a n) -> p a n", a=2), acc[0:n, 0, :, :])\
                    .then_inc(y_row, 1)

        def even_tensor(pe, phase, i, h, last=False):
            def mm(out, lhs, rhs, start=True, stop=True):
                return nc.tensor.matmul(out, lhs, rhs, start=start, stop=stop)

            def by_chunk(bank, lhs, rhs):
                for c in range(NC):
                    ins = mm(mx[:, bank, c * P:(c + 1) * P], lhs(c), rhs(c))
                return ins

            def at(a, c):
                return a[:, c * P:(c + 1) * P]

            def squares(b, name):
                for half in range(2):
                    ins = mm(mx[:, b + half, 0:HALF], ones, sq[:, half * HALF:(half + 1) * HALF])
                e_pe.done(ins, name)

            def U(j, a=0, b=KT):
                unit(pe, phase, i, j, a, b)

            def next_kq(a, b):
                if last:
                    return
                for n in range(a, b):
                    U(5 + n // KT, n % KT, n % KT + 1)

            def level_p(s):
                b = MASKS.index(s) % 2
                e_pool.wait(pe, h, f"b{s}")
                if s == 1:
                    e_dve.wait(pe, h, "kd")
                    for c in range(NC):
                        nc.tensor.transpose(mx[:, 0, c * P:(c + 1) * P], at(bm[:, b, :], c), ident)
                    e_pe.done(mm(mx[0:TS, 1, 0:TS], bm[0:TS, b, TP:T], ident[0:TS, 0:TS]), "P1")
                    return
                e_dve.wait(pe, h, f"x{s // 2}")
                ins = by_chunk(0, lambda c: bm[:, b, c * P:(c + 1) * P], lambda c: at(zi, c))
                if s <= 4:
                    ins = mm(mx[0:TS, 1, 0:TS], bm[0:TS, b, TP:T], zi[0:TS, TP:T])
                e_pe.done(ins, f"P{s}")

            def level_q(s):
                e_act.wait(pe, h, f"p{s}")
                if s == 2:
                    e_dve.wait(pe, h, "vb")
                ins = by_chunk(2, lambda c: at(xi, c), lambda c: at(pp, c))
                if s < MASKS[-1]:
                    ins = by_chunk(3, lambda c: at(pp, c), lambda c: at(xi, c))
                if s <= 4:
                    mm(mx[0:TS, 1, TS:2 * TS], xi[0:TS, TP:T], pp[0:TS, TP:T])
                    ins = mm(mx[0:TS, 1, 2 * TS:3 * TS], pp[0:TS, TP:T], xi[0:TS, TP:T])
                e_pe.done(ins, f"Q{s}")

            U(0, 0, 2)
            e_dve.wait(pe, h, "gate")
            by_chunk(0, lambda c: gh[:, c:c + 1].to_broadcast([P, P]), lambda c: tri)
            mm(mx[:, 1, 0:TS], gh[0:TS, NC:NC + 1].to_broadcast([TS, P]), tri_s)
            by_chunk(2, lambda c: bh[:, c:c + 1].to_broadcast([P, P]), lambda c: ident)
            e_pe.done(mm(mx[:, 1, TS:2 * TS], bh[0:TS, NC:NC + 1].to_broadcast([TS, P]), ident[0:TS, 0:TS]), "rows")
            U(0, 2, 8)
            e_act.wait(pe, h, "k_sq")
            e_dve.wait(pe, h, "bg")
            squares(0, "l2k")
            U(1, 0, 6)
            e_dve.wait(pe, h, "kT")
            by_chunk(0, lambda c: at(kT, c), lambda c: at(kT, c))
            e_pe.done(mm(mx[0:TS, 1, 0:TS], kT[:, TP:T], kT[:, TP:T]), "kk")
            e_act.wait(pe, h, "q_sq")
            squares(2, "l2q")
            U(1, 6, 8)
            e_dve.wait(pe, h, "A")
            for c in range(NC):
                nc.tensor.transpose(mx[:, 0, c * P:(c + 1) * P], at(kT, c), ident)
            e_pe.done(nc.tensor.transpose(mx[0:TS, 1, 0:P], kT[:, TP:T], ident), "tk")
            e_dve.wait(pe, h, "qT")
            mm(mx[0:TS, 3, 0:TS], kT[:, TP:T], qT[:, TP:T])
            e_pe.done(by_chunk(2, lambda c: at(kT, c), lambda c: at(qT, c)), "kq")
            e_act.wait(pe, h, "vs")
            e_dve.wait(pe, h, "aqk")
            for c in range(NC):
                nc.tensor.transpose(mx[:, 2, c * P:(c + 1) * P], at(vs, c), ident)
            e_pe.done(nc.tensor.transpose(mx[0:TS, 3, 0:P], vs[:, TP:T], ident), "tv")
            level_p(1)
            for j, pair in ((2, (2, 4)), (3, (8, 16)), (4, (32, 64))):
                for t, s in enumerate(pair):
                    U(j, 4 * t, 4 * t + 2)
                    level_p(s)
                    U(j, 4 * t + 2, 4 * t + 4)
                    level_q(s)
            next_kq(0, 1)
            e_dve.wait(pe, h, "z64")
            e_pe.done(mm(mx[:, 1, 256:384], at(zi, 0), vb[:, 0, :]), "u0")
            state_in_wait(pe, h)
            e_pool.wait(pe, h, "qg")
            for b in range(NB):
                ins = mm(mx[0:TS, 2, 0:P], km[:, b * TS:(b + 1) * TS], s_s[:, b, :], b == 0, b == NB - 1)
            e_pe.done(ins, "Rs")
            e_act.wait(pe, h, "uu0")
            e_pe.done(mm(mx[:, 0, 0:P], kd[:, 0, :], uu[:, :]), "S0")
            e_pe.done(mm(mx[:, 3, 0:P], uu[:, :], at(dt_, 0)), "o0")
            for c in range(1, NC):
                next_kq(3 * c - 2, 3 * c - 1)
                e_dve.wait(pe, h, f"s{c - 1}")
                e_pe.done(mm(mx[:, 1, 0:P], at(kbg, c), s_p[:, :]), f"R{c}")
                mm(mx[:, 3, c * P:(c + 1) * P], s_p[:, :], at(qg, c), True, False)
                next_kq(3 * c - 1, 3 * c)
                e_dve.wait(pe, h, f"rr{c}")
                e_pe.done(mm(mx[:, 1, 256:384], at(zi, c), rr[:, :]), f"u{c}")
                if c == 2:
                    e_pe.done(mm(mx[0:TS, 2, P:2 * P], zi[0:TS, TP:T], rs_[0:TS, :]), "us")
                next_kq(3 * c, 3 * c + 1)
                e_act.wait(pe, h, f"uu{c}")
                e_pe.done(mm(mx[:, 0, 0:P], kd[:, c, :], uu[:, :]), f"S{c}")
                e_pe.done(mm(mx[:, 3, c * P:(c + 1) * P], uu[:, :], at(dt_, c), False, True), f"o{c}")
            e_act.wait(pe, h, "us_")
            mm(mx[:, 2, 256:256 + TS], us_[0:TS, :], dt_[0:TS, TP:T], True, False)
            for b in range(NB):
                c = TP + b * LS
                ins = mm(mx[:, 2, 256 + b * LS:256 + (b + 1) * LS], s_s[:, b, :], qg[:, c:c + LS], False, b == NB - 1)
            e_pe.done(ins, "os")
            next_kq(10, 12)
            e_act.wait(pe, h, "o_sq")
            e_dve.wait(pe, h, f"s{NC - 1}")
            squares(0, "onorm")
            e_pool.wait(pe, h, "um")
            for half in range(2):
                ins = mm(mx[:, 2 + half, :], kd[0:TS, NC, :], um[0:TS, 4 * half:4 * half + 4, :])
            e_pe.done(ins, "Ss")
            next_kq(12, 16)
            e_dve.wait(pe, h, "ybl")
            for j in range(2):
                rows_unit(pe, phase, i, PLAIN[phase] + j, PLAIN[phase] + 4 * j, yh, yl)

        @block_.tensor
        def _(pe):
            pe.wait_ge(s_every, 16)
            pe.wait_ge(s_in, 32)
            for t in range(KT):
                p = t % 2
                if t >= 2:
                    pe.wait_ge(drained[p], plan.drained("x", 0, t))
                for c in range(NC):
                    nc.tensor.transpose(acc[:, p, 0, c * P:(c + 1) * P], x_in[:, c, t * P:(t + 1) * P], ident)
                nc.tensor.transpose(acc[:, p, 1, 0:TS], x_in[0:TS, NC, t * P:(t + 1) * P], ident[0:TS, 0:TS])\
                    .then_inc(multiplied, 1)
            pe.wait_ge(s_par, 16 * 8)
            nc.tensor.transpose(mx[:, 0, 0:ROWS_1], rows_1[0:ROWS_1, :], ident[0:ROWS_1, 0:ROWS_1])
            nc.tensor.transpose(mx[:, 0, ROWS_1:ROWS_1 + ROWS_2], rows_2[0:ROWS_2, :], ident[0:ROWS_2, 0:ROWS_2])
            pe.wait_ge(s_a, 16)
            pe.wait_ge(s_q, 16)
            for t in range(4):
                n = 2 * NB
                nc.tensor.transpose(mx[:, 1, t * n:(t + 1) * n], rows_a[0:n, t * P:(t + 1) * P], ident[0:n, 0:n])
            for t in range(12):
                n = 3 * NB
                ins = nc.tensor.transpose(mx[:, 2, t * n:(t + 1) * n], rows_q[0:n, t * P:(t + 1) * P], ident[0:n, 0:n])
            ins.then_inc(s_setup_t, 1)
            pe.wait_ge(s_setup_c, 1)
            norm_sum(pe, 0)
            two_units(pe, 0, ("ab", 0), ("even_kq", 0))
            unit(pe, "even_kq", 0, 1, 0, 1)
            emptied(pe, "ab", 0, 0)
            for c in range(NC):
                nc.tensor.transpose(mx[:, 0, c * P:(c + 1) * P], yf[:, c * P:(c + 1) * P], ident)
            a_pe.done(nc.tensor.transpose(mx[0:TS, 1, 0:P], yf[:, TP:T], ident), "ab_t")
            unit(pe, "even_kq", 0, 1, 1, 6)
            a_dve.wait(pe, 0, "g")
            pe.wait_ge(s_ce, 16)
            for bank, m, m_s in ((2, tri, tri_s), (3, low, low_s)):
                nc.tensor.matmul(mx[:, bank, 0:16], m, g_g[:, 0:NC, :].rearrange("p c h -> p (c h)"), start=True,
                                 stop=True)
                ins = nc.tensor.matmul(mx[0:TS, bank, 16:20], m_s, g_g[0:TS, NC, :], start=True, stop=True)
            a_pe.done(ins, "gcum")
            unit(pe, "even_kq", 0, 1, 6, KT)
            with pe.Fori(0, DN_H - 1) as i:
                even_tensor(pe, "even", i, i)
            even_tensor(pe, "even_end", 0, DN_H - 1, last=True)
            for t in range(4):
                ins = nc.tensor.transpose(mx[0:18, 0, t * P:(t + 1) * P], out_a[:, t, :], ident)
            ins.then_inc(rows_turned, 1)
            for kind in range(3):
                for t in range(4):
                    ins = nc.tensor.transpose(mx[0:27, 1 + kind, t * P:(t + 1) * P], out_q[:, kind, t, :], ident)
                ins.then_inc(rows_turned, 1)
            pe.wait_ge(rows_copied, 4)
            norm_sum(pe, 1)
            ffn_tensor(pe, 0)
            norm_sum(pe, 2)
            two_units(pe, 2, ("odd_kq", 0), ("odd_kq", 1))
            with pe.Fori(0, RET_H - 1) as i:
                odd_tensor(pe, "odd", i, i)
            odd_tensor(pe, "odd_end", 0, RET_H - 1, last=True)
            norm_sum(pe, 3)
            ffn_tensor(pe, 1)
            norm_sum(pe, 4)
            for c in range(NC + 1):
                p = c % 2
                n = P if c < NC else TS
                if c < 2:
                    pe.wait_ge(drained[p], plan.drained("y", 0, c))
                else:
                    pe.wait_ge(y_row, c - 1)
                for t in range(KT):
                    pe.wait_ge(y_norm, t + 1)
                    ins = nc.tensor.transpose(acc[0:n, p, t // 4, (t % 4) * P:(t % 4 + 1) * P],
                                              yT[:, t, c * P:c * P + n], ident)
                ins.then_inc(multiplied, 1)

        def even_gpsimd(pool, phase, i, h, last=False):
            def mask(s):
                n = MASKS.index(s)
                if n >= 2:
                    e_pe.wait(pool, h, f"P{MASKS[n - 2]}")
                    e_dve.wait(pool, h, "x1")
                else:
                    e_dve.wait(pool, h, "A")
                if s <= 4:
                    nc.gpsimd.tensor_tensor(bm[0:TS, n % 2, TP:T], dm[0:TS, TP:T], level[n][0:TS, 0:TS], ALU.mult)
                e_pool.done(nc.gpsimd.tensor_tensor(chunks(bm[:, n % 2, 0:TP]), chunks(dm[:, 0:TP]),
                                                    each_chunk(level[n]), ALU.mult), f"b{s}")

            def step(ins, name):
                e_pool.done(ins, name)
                e_pool.wait(pool, h, name)

            ahead(split_lo, pool, phase, i, 1)
            e_act.wait(pool, h, "gr")
            nc.gpsimd.tensor_tensor(chunks(dm[:, 0:TP]), chunks(gr[:, 0:TP]),
                                    gcum[:, 0:NC, ds(h, 1)].to_broadcast([P, NC, P]), ALU.subtract)
            step(nc.gpsimd.tensor_tensor(dm[:, TP:T], gr[:, TP:T],
                                         gcum[:, NC, ds(h, 1)].to_broadcast([P, TS]), ALU.subtract), "df")
            ahead(split_lo, pool, phase, i, 2)
            e_act.wait(pool, h, "dt")
            nc.gpsimd.tensor_tensor(dt_[0:TS, TP:T], dt_[0:TS, TP:T], tri_s, ALU.mult)
            e_pool.done(nc.gpsimd.tensor_tensor(chunks(dt_[:, 0:TP]), chunks(dt_[:, 0:TP]), each_chunk(tri), ALU.mult),
                        "dtm")
            mask(1)
            mask(2)
            ahead(split_lo, pool, phase, i, 3)
            step(nc.gpsimd.tensor_tensor(kbg[:, :], kT[:, :], bg[:, :], ALU.mult), "kbg")
            step(nc.gpsimd.tensor_tensor(diagonal(km), seqs(kT[:, TP:T]), seqs(bg[:, TP:T]), ALU.mult), "km")
            mask(4)
            mask(8)
            e_dve.wait(pool, h, "qT")
            step(nc.gpsimd.tensor_tensor(qg[:, :], qT[:, :], eg[:, :], ALU.mult), "qg")
            ahead(split_lo, pool, phase, i, 4)
            mask(16)
            mask(32)
            ahead(split_lo, pool, phase, i, 5)
            mask(64)
            ahead(split_lo, pool, phase, i, 6)
            e_act.wait(pool, h, "us_")
            e_pool.done(nc.gpsimd.tensor_tensor(um[0:TS, :, :], us_[0:TS, :].unsqueeze(1).to_broadcast([TS, NB, P]),
                                                block[0:TS, :].unsqueeze(2).to_broadcast([TS, NB, P]), ALU.mult), "um")
            if not last:
                for j in (7, 8, 9):
                    ahead(split_lo, pool, phase, i, j)

        @block_.gpsimd
        def _(pool):
            for n, free in enumerate((w_ready,) * RAW_LAG + (state_free, ret_free)):
                nc.gpsimd.memset(spare[:, n:n + 1], 0.0).then_inc(free, 1)
            split_lo(pool, "ab", 0, 0)
            split_lo(pool, "even_kq", 0, 0)
            split_lo(pool, "even_kq", 0, 1)
            norm_gpsimd(pool, 0)
            split_lo(pool, "even", 0, 0)
            pool.wait_ge(s_ce, 16)
            with pool.Fori(0, DN_H - 1) as i:
                even_gpsimd(pool, "even", i, i)
            even_gpsimd(pool, "even_end", 0, DN_H - 1, last=True)
            squares_while_splitting(pool, split_lo, add_square, 1, EVEN_END)
            norm_gpsimd(pool, 1)
            ffn_gpsimd(pool, 0)
            squares_while_splitting(pool, split_lo, add_square, 2, ffn_end(0))
            split_lo(pool, "odd", 0, 0)
            norm_gpsimd(pool, 2)
            with pool.Fori(0, RET_H - 1) as i:
                odd_gpsimd(pool, "odd", i, i)
            odd_gpsimd(pool, "odd_end", 0, RET_H - 1, last=True)
            squares_while_splitting(pool, split_lo, add_square, 3, ODD_END)
            norm_gpsimd(pool, 3)
            ffn_gpsimd(pool, 1)
            squares_while_splitting(pool, split_lo, add_square, 4, ffn_end(1))




_INS = ["x_prompt", "x_sample", "state_conv_a", "state_conv_qkv", "state_delta", "state_ret", "norm_mix", "norm_ffn",
        "final_norm", "even_w_in", "even_conv_a", "even_conv_qkv", "even_a_log", "even_dt_bias", "even_dn_norm",
        "even_w_out", "odd_w_in", "odd_gn_g", "odd_gn_b", "odd_w_out", "ffn_w_gate", "ffn_w_up", "ffn_w_down"]
_OUTS = [(1, TP, D), (NB, LS, D), (1, 1, WA - 1, CA), (1, 1, WQ - 1, 3 * CA), (1, 1, DN_H, DN_D, DN_D),
         (1, 1, RET_H, P, RET_V), (1, NB, WA - 1, CA), (1, NB, WQ - 1, 3 * CA), (1, NB, DN_H, DN_D, DN_D),
         (1, NB, RET_H, P, RET_V)]


def kernel(**inputs):
    import concourse.bacc as _bacc
    from concourse.bass_utils import run_bass_kernel_spmd as _run

    nc = _bacc.Bacc("TRN2", target_bir_lowering=False, num_devices=1)
    arrays, args = {}, []
    for name in _INS:
        arrays[f"in_{name}"] = np.ascontiguousarray(inputs[name])
    for name, a in constants().items():
        arrays[f"const_{name}"] = a
    for name, a in arrays.items():
        args.append(nc.dram_tensor(name, a.shape, mybir.dt.from_np(a.dtype), kind="ExternalInput").ap())
    for n, shape in enumerate(_OUTS):
        args.append(nc.dram_tensor(f"out_{n}", shape, F32, kind="ExternalOutput").ap())
    build(nc, *args)
    r = _run(nc, [arrays], core_ids=[0])
    return tuple(r.results[0][f"out_{n}"] for n in range(len(_OUTS)))
```
